# Optimizing a Trainium2 kernel written in Bass

```python
import math
import jax, jax.numpy as jnp
from jax import lax
import numpy as np

D_MODEL = 1024
BATCH = 1
SEQ = 512
DEPTH = 1

CHUNK = 64
N_META = 16
N_HEADS = 8
HEAD_DIM = 64
V_HEAD_DIM = 2 * HEAD_DIM
ATT_QK = N_HEADS * 2 * HEAD_DIM
ATT_V = N_HEADS * V_HEAD_DIM
CONV_CH = D_MODEL
CONV_K = 31
D_FF = 2816
FFN_CONV_K = 3
QB = 128
NEG_INF = -1e30
IN_COLS = 2 * ATT_QK + ATT_V + 2 * CONV_CH + 2 * D_MODEL


def _rms(x, w, eps=1e-6):
    xf = x.astype(jnp.float32)
    y = xf * lax.rsqrt(jnp.mean(xf * xf, axis=-1, keepdims=True) + eps)
    return (y * w.astype(jnp.float32)).astype(x.dtype)

def _layernorm(x, w, b, eps=1e-5):
    xf = x.astype(jnp.float32)
    mu = jnp.mean(xf, axis=-1, keepdims=True)
    xc = xf - mu
    y = xc * lax.rsqrt(jnp.mean(xc * xc, axis=-1, keepdims=True) + eps)
    return (y * w.astype(jnp.float32) + b.astype(jnp.float32)).astype(x.dtype)

def _causal_dwconv(x, w, b):
    k, c = w.shape
    y = lax.conv_general_dilated(
        x, w[:, None, :].astype(x.dtype), window_strides=(1,), padding=[(k - 1, 0)],
        dimension_numbers=('NWC', 'WIO', 'NWC'), feature_group_count=c)
    return y + b.astype(x.dtype)

def _diff_attention(q, k, v, lam, cid):
    b, lp = q.shape[0], q.shape[1]
    nblk = lp // QB
    qf = q.astype(jnp.float32) * (HEAD_DIM ** -0.5)
    kf = k.astype(jnp.float32)
    vf = v.astype(jnp.float32)

    def block(i):
        start = i * QB
        qb = lax.dynamic_slice_in_dim(qf, start, QB, axis=1)
        qc = lax.dynamic_slice_in_dim(cid, start, QB, axis=0)
        s = jnp.einsum('bqhmd,bkhmd->bhmqk', qb, kf)
        mask = cid[None, :] <= qc[:, None]
        p = jax.nn.softmax(jnp.where(mask, s, NEG_INF), axis=-1)
        a = p[:, :, 0] - lam * p[:, :, 1]
        return jnp.einsum('bhqk,bkhe->bqhe', a, vf)

    o = lax.map(block, jnp.arange(nblk))
    return jnp.moveaxis(o, 0, 1).reshape(b, lp, N_HEADS, V_HEAD_DIM)

def first_inputs(seed: int = 0) -> dict:
    key = jax.random.key(seed)
    ks = jax.random.split(key, 24)
    f32 = jnp.float32
    nrm = lambda k, shape, scale: (jax.random.normal(k, shape, f32) * scale)
    gain = lambda k, shape: 1.0 + 0.05 * jax.random.normal(k, shape, f32)
    L = DEPTH
    return {
        "x": nrm(ks[0], (BATCH, SEQ, D_MODEL), 1.0),
        "meta_tokens": nrm(ks[1], (N_META, D_MODEL), 0.5),
        "norm_mix_w": gain(ks[2], (L, D_MODEL)),
        "w_in": nrm(ks[3], (L, D_MODEL, IN_COLS), D_MODEL ** -0.5),
        "lambda_q1": nrm(ks[4], (L, HEAD_DIM), 0.1),
        "lambda_k1": nrm(ks[5], (L, HEAD_DIM), 0.1),
        "lambda_q2": nrm(ks[6], (L, HEAD_DIM), 0.1),
        "lambda_k2": nrm(ks[7], (L, HEAD_DIM), 0.1),
        "subln_w": gain(ks[8], (L, V_HEAD_DIM)),
        "conv_dw_w": nrm(ks[9], (L, CONV_K, CONV_CH), CONV_K ** -0.5),
        "conv_dw_b": nrm(ks[10], (L, CONV_CH), 0.02),
        "conv_ln_w": gain(ks[11], (L, CONV_CH)),
        "conv_ln_b": nrm(ks[12], (L, CONV_CH), 0.02),
        "w_conv_out": nrm(ks[13], (L, CONV_CH, D_MODEL), CONV_CH ** -0.5),
        "w_out": nrm(ks[14], (L, D_MODEL, D_MODEL), D_MODEL ** -0.5),
        "norm_ffn_w": gain(ks[15], (L, D_MODEL)),
        "w_up": nrm(ks[16], (L, D_MODEL, 2 * D_FF), D_MODEL ** -0.5),
        "ffn_dw_w": nrm(ks[17], (L, FFN_CONV_K, 2 * D_FF), FFN_CONV_K ** -0.5),
        "ffn_dw_b": nrm(ks[18], (L, 2 * D_FF), 0.02),
        "w_down": nrm(ks[19], (L, D_FF, D_MODEL), D_FF ** -0.5),
        "norm_final_w": gain(ks[20], (D_MODEL,)),
    }

def first_block(x, meta_tokens, norm_mix_w, w_in, lambda_q1, lambda_k1, lambda_q2, lambda_k2,
              subln_w, conv_dw_w, conv_dw_b, conv_ln_w, conv_ln_b, w_conv_out, w_out,
              norm_ffn_w, w_up, ffn_dw_w, ffn_dw_b, w_down, norm_final_w):
    b, s, d = x.shape
    total = s + N_META
    lp = ((total + QB - 1) // QB) * QB
    meta = jnp.broadcast_to(meta_tokens[None].astype(x.dtype), (b, N_META, d))
    h = jnp.concatenate([meta, x], axis=1)
    h = jnp.pad(h, ((0, 0), (0, lp - total), (0, 0)))
    pos = jnp.arange(lp)
    cid = jnp.where(pos < N_META, 0, (pos - N_META) // CHUNK + 1)

    splits = [ATT_QK, 2 * ATT_QK, 2 * ATT_QK + ATT_V,
              2 * ATT_QK + ATT_V + 2 * CONV_CH, 2 * ATT_QK + ATT_V + 2 * CONV_CH + D_MODEL]
    for l in range(DEPTH):
        lambda_init = 0.8 - 0.6 * math.exp(-0.3 * l)
        n = _rms(h, norm_mix_w[l])
        z = n @ w_in[l]
        q, k, v, glu, g_att, g_conv = jnp.split(z, splits, axis=-1)
        lam = (jnp.exp(jnp.sum(lambda_q1[l].astype(jnp.float32) * lambda_k1[l].astype(jnp.float32)))
               - jnp.exp(jnp.sum(lambda_q2[l].astype(jnp.float32) * lambda_k2[l].astype(jnp.float32)))
               + lambda_init)
        q = q.reshape(b, lp, N_HEADS, 2, HEAD_DIM)
        k = k.reshape(b, lp, N_HEADS, 2, HEAD_DIM)
        v = v.reshape(b, lp, N_HEADS, V_HEAD_DIM)
        o = _diff_attention(q, k, v, lam, cid)
        y_att = (_rms(o, subln_w[l]) * (1.0 - lambda_init)).reshape(b, lp, ATT_V).astype(h.dtype)
        u = glu[..., :CONV_CH] * jax.nn.sigmoid(glu[..., CONV_CH:])
        u = _causal_dwconv(u, conv_dw_w[l], conv_dw_b[l])
        u = jax.nn.silu(_layernorm(u, conv_ln_w[l], conv_ln_b[l]))
        y_conv = u @ w_conv_out[l]
        m = jax.nn.sigmoid(g_att) * y_att + jax.nn.sigmoid(g_conv) * y_conv
        h = h + m @ w_out[l]
        n2 = _rms(h, norm_ffn_w[l])
        up = _causal_dwconv(n2 @ w_up[l], ffn_dw_w[l], ffn_dw_b[l])
        gate, val = jnp.split(up, 2, axis=-1)
        h = h + (jax.nn.silu(gate) * val) @ w_down[l]

    out = _rms(h, norm_final_w)
    return out[:, N_META:N_META + s]


MIX_W = D_MODEL
MLSTM_HEADS = 4
MLSTM_DH = 3 * D_MODEL // 32
MLSTM_W = MLSTM_HEADS * MLSTM_DH
LRU_BLOCKS = 6
LRU_BW = D_MODEL // 16
LRU_W = LRU_BLOCKS * LRU_BW
LRU_CONV = 4
RG_C = 8.0
ATT_HEADS = 4
ATT_DH = D_MODEL // 16
ATT_W = ATT_HEADS * ATT_DH
IDX_HEADS = 4
IDX_DIM = 64
TOPK_MAX = 256
Q_BLOCK = CHUNK
D_FF_2 = 11 * D_MODEL // 4
FFN_CONV = 3
EPS = 1e-6

IN_SPLITS = (MLSTM_W, MLSTM_W, MLSTM_W, MLSTM_W, MLSTM_HEADS, MLSTM_HEADS,
             LRU_W, LRU_W,
             ATT_W, ATT_W, ATT_W, IDX_HEADS * IDX_DIM, IDX_DIM, IDX_HEADS)
D_IN = sum(IN_SPLITS)


def rmsnorm(x, g):
    xf = x.astype(jnp.float32)
    y = xf * lax.rsqrt(jnp.mean(xf * xf, axis=-1, keepdims=True) + EPS)
    return (y * g.astype(jnp.float32)).astype(x.dtype)

def causal_depthwise_conv(x, w, b):
    width, c = w.shape
    xp = jnp.pad(x, ((0, 0), (width - 1, 0), (0, 0)))
    y = lax.conv_general_dilated(xp, w[:, None, :].astype(x.dtype), window_strides=(1,),
                                 padding='VALID', dimension_numbers=('NWC', 'WIO', 'NWC'),
                                 feature_group_count=c)
    return y + b.astype(x.dtype)

def split_cols(p):
    idx, acc = [], 0
    for s in IN_SPLITS[:-1]:
        acc += s
        idx.append(acc)
    return jnp.split(p, idx, axis=-1)

def mlstm_chunkwise(q, k, v, ig, fg):
    B, S, H, D = q.shape
    L = CHUNK
    nc = S // L
    f32 = jnp.float32
    q = q.astype(f32)
    k = k.astype(f32) * (D ** -0.5)
    v = v.astype(f32)
    log_f = jax.nn.log_sigmoid(fg.astype(f32))
    ig = ig.astype(f32)

    def to_chunks(a):
        return a.reshape(B, nc, L, H, D).transpose(1, 0, 3, 2, 4)

    def gate_chunks(a):
        return a.reshape(B, nc, L, H).transpose(1, 0, 3, 2)

    qs, ks, vs = to_chunks(q), to_chunks(k), to_chunks(v)
    i_s = gate_chunks(ig)
    b_s = jnp.cumsum(gate_chunks(log_f), axis=-1)
    tril = jnp.tril(jnp.ones((L, L), dtype=bool))

    def step(carry, inp):
        C, n, m = carry
        qc, kc, vc, ic, bc = inp
        d_log = bc[..., :, None] - bc[..., None, :] + ic[..., None, :]
        d_log = jnp.where(tril, d_log, -jnp.inf)
        inter = bc + m[..., None]
        m_t = jnp.maximum(inter, jnp.max(d_log, axis=-1))
        w_intra = jnp.exp(d_log - m_t[..., None])
        w_inter = jnp.exp(inter - m_t)
        s = jnp.einsum('bhtd,bhsd->bhts', qc, kc) * w_intra
        num = (w_inter[..., None] * jnp.einsum('bhtd,bhde->bhte', qc, C)
               + jnp.einsum('bhts,bhse->bhte', s, vc))
        den = w_inter * jnp.einsum('bhtd,bhd->bht', qc, n) + jnp.sum(s, axis=-1)
        h = num / jnp.maximum(jnp.abs(den), jnp.exp(-m_t))[..., None]
        b_last = bc[..., -1]
        g = b_last[..., None] - bc + ic
        m_new = jnp.maximum(b_last + m, jnp.max(g, axis=-1))
        wg = jnp.exp(g - m_new[..., None])
        decay = jnp.exp(b_last + m - m_new)
        C_new = decay[..., None, None] * C + jnp.einsum('bhs,bhsd,bhse->bhde', wg, kc, vc)
        n_new = decay[..., None] * n + jnp.einsum('bhs,bhsd->bhd', wg, kc)
        return (C_new, n_new, m_new), h

    init = (jnp.zeros((B, H, D, D), f32), jnp.zeros((B, H, D), f32), jnp.zeros((B, H), f32))
    _, hs = lax.scan(step, init, (qs, ks, vs, i_s, b_s))
    return hs.transpose(1, 0, 3, 2, 4).reshape(B, S, H, D)

def rglru(x, w_a, b_a, w_x, b_x, lam):
    B, S, C = x.shape
    f32 = jnp.float32
    xf = x.astype(f32)
    xb = xf.reshape(B, S, LRU_BLOCKS, LRU_BW)
    r = jax.nn.sigmoid(jnp.einsum('bsnc,ncd->bsnd', xb, w_a.astype(f32)).reshape(B, S, C)
                       + b_a.astype(f32))
    i = jax.nn.sigmoid(jnp.einsum('bsnc,ncd->bsnd', xb, w_x.astype(f32)).reshape(B, S, C)
                       + b_x.astype(f32))
    log_a = -RG_C * r * jax.nn.softplus(-lam.astype(f32))
    a = jnp.exp(log_a)
    u = jnp.sqrt(-jnp.expm1(2.0 * log_a)) * (i * xf)

    def combine(e1, e2):
        a1, b1 = e1
        a2, b2 = e2
        return a1 * a2, a2 * b1 + b2

    _, h = lax.associative_scan(combine, (a, u), axis=1)
    return h.astype(x.dtype)

def dsa_attention(q, k, v, iq, ik, iw):
    B, S, H, Dh = q.shape
    n_sel = min(TOPK_MAX, S // 4)
    nblk = S // Q_BLOCK
    key_chunk = jnp.arange(S) // CHUNK
    bidx = jnp.arange(B)[:, None, None]
    idx_scale = (IDX_HEADS ** -0.5) * (IDX_DIM ** -0.5)
    att_scale = Dh ** -0.5
    ikf = ik.astype(jnp.float32)

    def to_blocks(a):
        return a.reshape((B, nblk, Q_BLOCK) + a.shape[2:]).swapaxes(0, 1)

    def block(args):
        blk, qb, iqb, iwb = args
        t = blk * Q_BLOCK + jnp.arange(Q_BLOCK)
        admissible = key_chunk[None, :] <= (t // CHUNK)[:, None]
        rel = jax.nn.relu(jnp.einsum('bqhd,bsd->bqhs', iqb.astype(jnp.float32), ikf))
        score = jnp.einsum('bqh,bqhs->bqs', iwb.astype(jnp.float32), rel) * idx_scale
        score = jnp.where(admissible[None], score, -jnp.inf)
        top_val, top_idx = lax.top_k(score, n_sel)
        valid = jnp.isfinite(top_val)
        ks = k[bidx, top_idx]
        vs = v[bidx, top_idx]
        logits = jnp.einsum('bqhd,bqkhd->bqhk', qb, ks).astype(jnp.float32) * att_scale
        logits = jnp.where(valid[:, :, None, :], logits, -jnp.inf)
        p = jax.nn.softmax(logits, axis=-1)
        return jnp.einsum('bqhk,bqkhd->bqhd', p.astype(vs.dtype), vs)

    out = lax.map(block, (jnp.arange(nblk), to_blocks(q), to_blocks(iq), to_blocks(iw)))
    return out.swapaxes(0, 1).reshape(B, S, H, Dh)

def hybrid_mixer(xn, w_in, b_igate, b_fgate, mlstm_norm, lru_conv_w, lru_conv_b,
                 lru_w_a, lru_b_a, lru_w_x, lru_b_x, lru_lambda, w_out):
    B, S, _ = xn.shape
    p = xn @ w_in
    mq, mk, mv, mo, mi, mf, lx, lg, aq, ak, av, iq, ik, iw = split_cols(p)
    shp = (B, S, MLSTM_HEADS, MLSTM_DH)
    hA = mlstm_chunkwise(mq.reshape(shp), mk.reshape(shp), mv.reshape(shp),
                         mi + b_igate, mf + b_fgate).astype(xn.dtype)
    hA = rmsnorm(hA, mlstm_norm.reshape(MLSTM_HEADS, MLSTM_DH)).reshape(B, S, MLSTM_W)
    hA = hA * jax.nn.sigmoid(mo)
    xc = causal_depthwise_conv(lx, lru_conv_w, lru_conv_b)
    hB = rglru(xc, lru_w_a, lru_b_a, lru_w_x, lru_b_x, lru_lambda) * jax.nn.gelu(lg, approximate=True)
    ashp = (B, S, ATT_HEADS, ATT_DH)
    hC = dsa_attention(aq.reshape(ashp), ak.reshape(ashp), av.reshape(ashp),
                       iq.reshape(B, S, IDX_HEADS, IDX_DIM), ik, iw).reshape(B, S, ATT_W)
    return jnp.concatenate([hA, hB, hC], axis=-1) @ w_out

def conv_ffn(xn, ffn_up, ffn_conv_w, ffn_conv_b, ffn_down):
    u = causal_depthwise_conv(xn @ ffn_up, ffn_conv_w, ffn_conv_b)
    gate, up = jnp.split(u, 2, axis=-1)
    return (jax.nn.gelu(gate, approximate=True) * up) @ ffn_down

def second_inputs(seed: int = 0) -> dict:
    key = jax.random.key(seed)
    ks = jax.random.split(key, 24)
    f32 = jnp.float32
    nrm = lambda k, shape, s: jax.random.normal(k, shape, f32) * s
    gain = lambda k, shape: 1.0 + 0.05 * jax.random.normal(k, shape, f32)
    u = jax.random.uniform(ks[20], (DEPTH, LRU_W), f32, minval=0.9, maxval=0.999)
    s = u ** (1.0 / RG_C)
    lru_lambda = jnp.log(s) - jnp.log1p(-s)
    return {
        "x": nrm(ks[0], (BATCH, SEQ, D_MODEL), 1.0),
        "norm_mix_pre": gain(ks[1], (DEPTH, D_MODEL)),
        "norm_mix_post": gain(ks[2], (DEPTH, D_MODEL)),
        "norm_ffn_pre": gain(ks[3], (DEPTH, D_MODEL)),
        "norm_ffn_post": gain(ks[4], (DEPTH, D_MODEL)),
        "w_in": nrm(ks[5], (DEPTH, D_MODEL, D_IN), D_MODEL ** -0.5),
        "b_igate": nrm(ks[6], (DEPTH, MLSTM_HEADS), 0.1),
        "b_fgate": 3.0 + nrm(ks[7], (DEPTH, MLSTM_HEADS), 0.1),
        "mlstm_norm": gain(ks[8], (DEPTH, MLSTM_W)),
        "lru_conv_w": nrm(ks[9], (DEPTH, LRU_CONV, LRU_W), LRU_CONV ** -0.5),
        "lru_conv_b": nrm(ks[10], (DEPTH, LRU_W), 0.01),
        "lru_w_a": nrm(ks[11], (DEPTH, LRU_BLOCKS, LRU_BW, LRU_BW), LRU_BW ** -0.5),
        "lru_b_a": nrm(ks[12], (DEPTH, LRU_W), 0.01),
        "lru_w_x": nrm(ks[13], (DEPTH, LRU_BLOCKS, LRU_BW, LRU_BW), LRU_BW ** -0.5),
        "lru_b_x": nrm(ks[14], (DEPTH, LRU_W), 0.01),
        "lru_lambda": lru_lambda,
        "w_out": nrm(ks[15], (DEPTH, MIX_W, D_MODEL), MIX_W ** -0.5),
        "ffn_up": nrm(ks[16], (DEPTH, D_MODEL, 2 * D_FF_2), D_MODEL ** -0.5),
        "ffn_conv_w": nrm(ks[17], (DEPTH, FFN_CONV, 2 * D_FF_2), FFN_CONV ** -0.5),
        "ffn_conv_b": nrm(ks[18], (DEPTH, 2 * D_FF_2), 0.01),
        "ffn_down": nrm(ks[19], (DEPTH, D_FF_2, D_MODEL), D_FF_2 ** -0.5),
    }

def second_block(x, norm_mix_pre, norm_mix_post, norm_ffn_pre, norm_ffn_post, w_in,
              b_igate, b_fgate, mlstm_norm, lru_conv_w, lru_conv_b, lru_w_a, lru_b_a,
              lru_w_x, lru_b_x, lru_lambda, w_out, ffn_up, ffn_conv_w, ffn_conv_b, ffn_down):
    for l in range(DEPTH):
        h = rmsnorm(x, norm_mix_pre[l])
        mix = hybrid_mixer(h, w_in[l], b_igate[l], b_fgate[l], mlstm_norm[l],
                           lru_conv_w[l], lru_conv_b[l], lru_w_a[l], lru_b_a[l],
                           lru_w_x[l], lru_b_x[l], lru_lambda[l], w_out[l])
        x = x + rmsnorm(mix, norm_mix_post[l])
        h = rmsnorm(x, norm_ffn_pre[l])
        x = x + rmsnorm(conv_ffn(h, ffn_up[l], ffn_conv_w[l], ffn_conv_b[l], ffn_down[l]),
                        norm_ffn_post[l])
    return x


def setup_inputs(seed=0):
    out = dict(first_inputs(seed))
    for name, value in second_inputs(seed + 1).items():
        if name != "x":
            out[name + "_2"] = value
    return out


def reference(
    x, meta_tokens, norm_mix_w, w_in, lambda_q1, lambda_k1, lambda_q2, lambda_k2, subln_w,
    conv_dw_w, conv_dw_b, conv_ln_w, conv_ln_b, w_conv_out, w_out, norm_ffn_w, w_up, ffn_dw_w,
    ffn_dw_b, w_down, norm_final_w, norm_mix_pre_2, norm_mix_post_2, norm_ffn_pre_2,
    norm_ffn_post_2, w_in_2, b_igate_2, b_fgate_2, mlstm_norm_2, lru_conv_w_2, lru_conv_b_2,
    lru_w_a_2, lru_b_a_2, lru_w_x_2, lru_b_x_2, lru_lambda_2, w_out_2, ffn_up_2, ffn_conv_w_2,
    ffn_conv_b_2, ffn_down_2,
):
    x = first_block(
        x, meta_tokens, norm_mix_w, w_in, lambda_q1, lambda_k1, lambda_q2, lambda_k2, subln_w,
        conv_dw_w, conv_dw_b, conv_ln_w, conv_ln_b, w_conv_out, w_out, norm_ffn_w, w_up,
        ffn_dw_w, ffn_dw_b, w_down, norm_final_w,
    )
    return second_block(
        x, norm_mix_pre_2, norm_mix_post_2, norm_ffn_pre_2, norm_ffn_post_2, w_in_2, b_igate_2,
        b_fgate_2, mlstm_norm_2, lru_conv_w_2, lru_conv_b_2, lru_w_a_2, lru_b_a_2, lru_w_x_2,
        lru_b_x_2, lru_lambda_2, w_out_2, ffn_up_2, ffn_conv_w_2, ffn_conv_b_2, ffn_down_2,
    )


_drawn_inputs = setup_inputs


def setup_inputs(seed=0):
    import zlib

    import numpy as np

    out = dict(_drawn_inputs(seed))
    spreads = {}
    factors = {'conv_ln_b': 3.434,
     'b_igate_2': 64.0,
     'b_fgate_2': 22.488,
     'lru_b_a_2': 59.626,
     'lru_b_x_2': 23.119,
     'ffn_conv_b_2': 6.942}
    for name, (base, spread) in spreads.items():
        noise = np.random.default_rng([zlib.crc32(name.encode()), seed]).standard_normal(out[name].shape)
        drawn = base * np.exp(spread * noise) if base else spread * noise
        out[name] = __import__('jax').numpy.asarray(drawn.astype(out[name].dtype))
    for name, factor in factors.items():
        out[name] = (out[name] * factor).astype(out[name].dtype)
    return out
```

```python
import math
from contextlib import ExitStack

import concourse.bass as bass
from concourse import mybir

D = 1024
KT = D // 128
S = 512
NM = 16
T = S + NM
HT = T // 2
C3 = NM - 4
T3 = T - C3
H3 = T3 // 2
NH = 8
CK = 31
PAD = CK - 1
DFF = 2816
FG = DFF // 128
KD = FG // 2
TT = S // 128
LAMBDA_INIT = 0.8 - 0.6 * math.exp(-0.3 * 0)
BIG = 1.0e30
OWN_HEADS = 80

ML_H, ML_D = 4, 96
ML_W = ML_H * ML_D
LRU_W = 384
LG = LRU_W // 128
AT_H, AT_D = 4, 64
AT_W = AT_H * AT_D
TOPK = 128
RG_C = 8.0
O_MQ, O_MK, O_MV, O_MO = 0, 384, 768, 1152
O_MI, O_MF = 1536, 1540
O_LX, O_LG = 1544, 1928
O_AQ, O_AK, O_AV = 2312, 2568, 2824
O_IQ, O_IK, O_IW = 3080, 3336, 3400
D_IN2 = 3404

N_GLU = 0
N_HEAD = N_GLU + 8
N_GC = N_HEAD + 2 * NH
N_CO = N_GC + 4
N_WO = N_CO + 4
N_UP = N_WO + 4
N_DN = N_UP + FG
N_IN2 = N_DN + 16
N_WO2 = N_IN2 + 15
N_UP2 = N_WO2 + 4
N_DN2 = N_UP2 + FG
N_END = N_DN2 + 16

CREDIT = 2

V_MIX, V_CB, V_LNW, V_LNB, V_FFN, V_FIN, V_PRE, V_POST, V_FPRE, V_FPOST = (8 * i for i in range(10))
V_SUB = 80
V_LCB, V_LBA, V_LBX, V_LAM = 81, 84, 87, 90
V_LCW = 93
V_ROWS = 105


def evacuations():
    e = []
    e += ["D", "A"] * 8
    e += ["A"] * (4 * NH)
    e += ["A"] * 8
    e += ["D"] * 8
    e += ["D"] * 8
    e += ["A"] * (2 * FG)
    e += ["-", "-", "-", "D"] * 8
    e += ["A"] * 30
    e += ["A"] * 8
    e += ["A"] * (2 * FG)
    e += ["-", "-", "-", "A"] * 8
    assert len(e) == 2 * N_END
    return e


def program(nc, A, out):
    f32, f32r = mybir.dt.float32, mybir.dt.float32r
    ALU, ACT = mybir.AluOpType, mybir.ActivationFunctionType
    AX = mybir.AxisListType.X
    ds = bass.ds
    EV = evacuations()

    def evacuated(gi):
        return EV[gi], CREDIT + EV[:gi + 1].count(EV[gi])

    def kp(w):
        return w.rearrange("(k p) c -> p k c", p=128)

    w_in, w_up, w_down = A["w_in"][0], A["w_up"][0], A["w_down"][0]
    w_co, w_o = A["w_conv_out"][0], A["w_out"][0]
    w_in2, w_o2, w_up2, w_down2 = A["w_in_2"][0], A["w_out_2"][0], A["ffn_up_2"][0], A["ffn_down_2"][0]

    with ExitStack() as ctx:
        def sem(name):
            return ctx.enter_context(nc.semaphore(name))

        def sb(name, shape, dt=f32):
            return ctx.enter_context(nc.sbuf_tensor(name, shape, dt))

        raw = sb("raw", [128, 2, 2, KT, 128])
        wh = sb("wh", [128, 2, 2, KT, 128], f32r)
        wl = sb("wl", [128, 2, 2, KT, 128], f32r)
        hT = sb("hT", [128, KT, T])
        ident = sb("ident", [128, 128])
        ones = sb("ones", [128, 128])
        vec = sb("vec", [128, V_ROWS])
        cdw = sb("cdw", [128, CK * 8])
        fdw = sb("fdw", [128, 2, 4, 2 * FG])
        eps6 = sb("eps6", [128, 1])
        eps5 = sb("eps5", [128, 1])
        cred = sb("cred", [128, 8])
        nlam = sb("nlam", [128, 1])
        tail_base = nc.sbuf_base

        psP = [ctx.enter_context(nc.psum_tensor(f"psP{i}", [128, 2, 512], f32)) for i in range(2)]
        psS = [ctx.enter_context(nc.psum_tensor(f"psS{i}", [128, 2, 512], f32)) for i in range(2)]

        place = [0]

        def at(name, shape, dt=f32, start=None):
            if start is not None:
                place[0] = start
            n = 4
            for d in shape[1:]:
                n *= d
            t = nc.alloc_sbuf_tensor_at(name, shape, dt, offset=place[0])
            place[0] += -(-n // 32) * 32
            assert place[0] <= nc.sbuf_usable_end, (name, place[0] - nc.sbuf_usable_end)
            return t

        x_start = -(-tail_base // 32) * 32
        xh = at("xh", [128, KT, T], f32r, start=x_start)
        xl = at("xl", [128, KT, T], f32r)
        base = place[0]
        xrow = at("xrow", [128, TT, D], start=base)
        mrow = at("mrow", [NM, D])
        vrow = at("vrow", [V_ROWS, 128])
        crow = at("crow", [124, 2, 128])
        frow = at("frow", [2 * FG, 2, 4, 128])
        lamv = at("lamv", [128, 4, 64])
        lamp = at("lamp", [128, 2, 64])
        lams = at("lams", [128, 6])
        conv = at("conv", [128, NH, T3], start=base)
        yT = at("yT", [128, NH, T])
        u_start = place[0]
        u = at("u", [128, NH, PAD + T])
        after_u = place[0]
        qkvg = at("qkvg", [128, 2, 4, T])
        prob_start = place[0]
        PW = [NM + 128 * (t + 1) for t in range(TT)]
        PO = [sum(PW[:t]) for t in range(TT)]
        prob = at("prob", [128, 2, sum(PW)])
        pmeta = at("pmeta", [NM, 2, NM])
        aT = at("aT", [128, TT, S])
        aTm = at("aTm", [NM, S + NM])
        vtok = at("vtok", [128, TT + 1, 128])
        cin = at("cin", [128, PAD + T])
        cwt = at("cwt", [128, CK + 1])
        cacc = at("cacc", [128, T3])
        osq = at("osq", [128, T])
        stat = at("stat", [128, 32])
        mki = at("mki", [128, 128])
        mkk = at("mkk", [128, 64])
        sgl = at("sgl", [128, 2, T], start=prob_start)
        sgc = at("sgc", [128, 8, T3], start=after_u)
        mh = at("mh", [128, KT, T3], f32r)
        ml = at("ml", [128, KT, T3], f32r, start=u_start)
        acth = at("acth", [128, FG, S], f32r, start=base)
        actl = at("actl", [128, FG, S], f32r)
        temp_start = place[0]
        upr = at("upr", [128, 2, 2, T3])
        acc = at("acc", [128, 2, S])
        prod = at("prod", [128, 2, S])
        sq = at("sq", [128, 2, T], start=temp_start)
        nf = at("nf", [128, 2, T])
        rstd = at("rstd", [128, T])


        ch = at("ch", [128, KT, S], f32r, start=base)
        cl = at("cl", [128, KT, S], f32r)
        sc = at("sc", [128, TT, S])
        aqk = at("aqk", [128, 4, S])
        av = at("av", [128, TT, AT_W])
        wab = at("wab", [128, 2, LG, 128])
        mnb = at("mnb", [128, ML_W])
        sel = at("sel", [ML_H, ML_H, 128])
        tri = at("tri", [128, 128])
        bif = at("bif", [ML_H, 2])
        gcol = at("gcol", [128, 3, TT, 4])
        lcol = at("lcol", [128, 6, LG])
        st2 = at("st2", [128, 2 * TT])
        m8 = at("m8", [128, 2, 8])
        mx2 = at("mx2", [128, 4, 8])
        rows = at("rows", [ML_H, 5, S])
        m_start = place[0]
        lx = at("lx", [128, LG, 3 + S])
        lg = at("lg", [128, LG, S])
        xc = at("xc", [128, LG, S])
        lt = at("lt", [128, LG, S])
        li = at("li", [128, LG, S])
        iq = at("iq", [128, 2, S])
        ik = at("ik", [128, S])
        rl = aqk[:, 0:2, :]
        mqk = at("mqk", [ML_D, 2, 2, S], start=m_start)
        va = at("va", [128, TT, ML_H * (ML_D + 1)])
        mo = at("mo", [128, TT, ML_W])
        hA_start = place[0]
        hA = at("hA", [128, TT, ML_W])
        md = at("md", [128, TT, 128])
        PT = at("PT", [128, TT, S])
        pr = at("pr", [128, 2, S], start=hA_start)
        mT = at("mT", [128, KT, S], start=m_start)
        mT2 = at("mT2", [128, KT, S], start=x_start)
        xo = at("xo", [128, 2, D], start=x_start + 4 * KT * T)
        ALLP = [psP[0], psP[1], psS[0], psS[1]]

        s_in = sem("inputs_loaded")
        s_raw = [sem("raw_loaded0"), sem("raw_loaded1")]
        s_hi = sem("hi_split")
        s_lo = sem("lo_split")
        s_mm = sem("half_chunks_multiplied")
        s_ea = sem("emptied_by_act")
        s_ed = sem("emptied_by_dve")
        s_id = sem("constants_set")
        s_ct = sem("constants_transposed")
        s_cc = sem("constants_copied")
        s_xt = sem("input_transposed")
        s_hx = sem("input_copied_by_act")
        s_hm = sem("input_copied_by_dve")
        s_lamo = sem("lambda_sums")
        s_lame = sem("lambda_exps")
        s_lamd = sem("lambda_ready")
        s_sq = sem("squared")
        s_sqf = sem("squares_summed")
        s_rt = sem("root_taken")
        s_nf = sem("normed")
        s_nh = sem("normed_hi")
        s_nl = sem("normed_lo")
        s_v = sem("dve_own_steps")
        s_a = sem("act_own_steps")
        s_qk = sem("scores_ready")
        s_mx = sem("maxima_ready")
        s_ex = sem("exps_ready")
        s_cb = sem("probs_combined")
        s_at = sem("attention_transposed")
        s_ac = sem("attention_copied")
        s_at_o = sem("head_output_ready")
        s_cf = sem("convolution_fetched")
        s_cst = sem("convolution_stored")
        s_hr = sem("head_roots")
        s_os = sem("head_squared")
        s_oy = sem("head_gated")
        s_ss = sem("head_squares_summed")
        s_sc = sem("head_sum_copied")
        s_yd = sem("head_outputs_ready")
        s_cv = sem("convolved")
        s_lm = sem("ln_means")
        s_lc = sem("ln_centred")
        s_ln = sem("ln_normed")
        s_lu = sem("ln_activated")
        s_m = sem("mixed")
        s_mhi = sem("mixed_hi")
        s_ml = sem("mixed_lo")
        s_cva = sem("ffn_convolved")
        s_sil = sem("gate_activated")
        s_pr = sem("gated")
        s_ph = sem("gated_hi")
        s_pl = sem("gated_lo")
        s_out = [sem("output_stored0"), sem("output_stored1")]
        s_x2 = sem("final_normed")
        s_pz = sem("pool_zeroed")
        s_pz2 = sem("value_ones_set")
        s_uz = sem("up_borders_cleared")
        s_p2 = sem("second_block_constants")
        s_ga = sem("gate_rows_copied")
        s_az = sem("gate_magnitudes")
        s_ez = sem("gate_exps")
        s_gt = sem("gate_rows_transposed")
        s_gc = sem("gate_columns_copied")
        s_ix = sem("index_products")
        s_rl = sem("index_relus")
        s_ixa = sem("index_accumulated")
        s_xc = sem("lru_convolved")
        s_rg = sem("lru_gates_multiplied")
        s_ri = sem("lru_sigmoids")
        s_la = sem("lru_decays")
        s_lb = sem("lru_decay_columns")
        s_lv = sem("lru_variances")
        s_lq = sem("lru_roots")
        s_hb = sem("lru_outputs")
        s_hbh = sem("lru_hi")
        s_hbl = sem("lru_lo")
        s_lg = sem("attention_logits")
        s_pm = sem("attention_maxima")
        s_pe = sem("attention_exps")
        s_pn = sem("attention_probs")
        s_pt = sem("attention_probs_transposed")
        s_pc = sem("attention_probs_copied")
        s_po = sem("attention_outputs")
        s_hc = sem("attention_hi")
        s_hcl = sem("attention_lo")
        s_mrow = sem("mlstm_rows")
        s_fl = sem("mlstm_floor")
        s_mb = sem("mlstm_maxima_spread")
        s_md = sem("mlstm_diagonals")
        s_mw = sem("mlstm_weights")
        s_st = sem("mlstm_scores")
        s_pp = sem("mlstm_products")
        s_mo = sem("mlstm_outputs")
        s_mn = sem("mlstm_normalised")
        s_hs = sem("mlstm_squares")
        s_h2 = sem("mlstm_sums")
        s_hrt = sem("mlstm_roots")
        s_hg = sem("mlstm_gated")
        s_ht = sem("mlstm_transposed")
        s_hh = sem("mlstm_hi")
        s_hl = sem("mlstm_lo")
        s_y = sem("residual_added")
        s_ot = sem("output_transposed")
        s_oc = sem("output_copied")

        def lin(a, b, i):
            return a if i is None else i * b + a

        class Own:

            def __init__(self, eng, s):
                self.eng, self.s, self.n, self.i, self.per = eng, s, 0, None, 0

            def __call__(self, ins):
                ins.then_inc(self.s, 1)
                self.n += 1
                self.eng.wait_ge(self.s, lin(self.n, self.per, self.i))

            def enter(self, i, per):
                self.i, self.per, self.n0 = i, per, self.n

            def leave(self, turns):
                assert self.n - self.n0 == self.per, ("steps in the loop", self.n - self.n0)
                self.n = self.n0 + self.per * turns
                self.i = None

        def span(t, g, c0, n):
            if isinstance(g, int):
                return t[:, g, c0:c0 + 2 * n].rearrange("p (a b) -> p a b", a=2)
            return t[:, ds(g, 1), c0:c0 + 2 * n].rearrange("p o (a b) -> p (o a) b", a=2)

        block = ctx.enter_context(nc.Block())

        @block.sync
        def _(sp):
            def load(n, i, st, srcs, dsts):
                if n >= 2:
                    sp.wait_ge(s_lo, lin(n - 1, st, i))
                for dst, src in zip(dsts, srcs):
                    sp.dma_start(dst, src).then_inc(s_raw[n % 2], 16)

            def pair(w, n, i, st, ca, cb):
                s = n % 2
                load(n, i, st, [kp(w)[:, :, ds(ca, 128)], kp(w)[:, :, ds(cb, 128)]],
                     [raw[:, s, 0], raw[:, s, 1]])

            def wide(w, n, turns, col=0):
                with sp.Fori(0, turns) as i:
                    for j in range(2):
                        c = i * 512 + (col + 256 * j)
                        pair(w, n + j, i, 2, c, c + 128)

            def up(w, n):
                with sp.Fori(0, FG // 2) as i:
                    for j in range(2):
                        c = i * 256 + 128 * j
                        pair(w, n + j, i, 2, c, c + DFF)

            def down(w, n):
                rows = w.rearrange("(j k p) c -> j p k c", p=128, k=KD)
                with sp.Fori(0, 8) as i:
                    for j in range(2):
                        s = (n + j) % 2
                        flat = raw[:, s].rearrange("p a k c -> p (a k) c")
                        src = rows[j][:, :, ds(i * 128, 128)]
                        load(n + j, i, 2, [src[:, 0:6], src[:, 6:KD]], [flat[:, 0:6], flat[:, 6:KD]])

            G = 3 * D
            for n in range(2):
                pair(w_in, n, None, 0, G + 128 * n, G + D + 128 * n)
            with sp.Fori(0, 3) as i:
                for j in range(2):
                    c = i * 256 + (G + 128 * (2 + j))
                    pair(w_in, 2 + j, i, 2, c, c + D)
            with sp.Fori(0, NH) as h:
                c = h * 128
                pair(w_in, N_HEAD, h, 2, c, c + D)
                pair(w_in, N_HEAD + 1, h, 2, c + 2 * D, c + 5 * D)
            wide(w_in, N_GC, 2, 6 * D)
            wide(w_co, N_CO, 2)
            wide(w_o, N_WO, 2)
            up(w_up, N_UP)
            down(w_down, N_DN)

            W2 = kp(w_in2)

            def parts(n, srcs, dsts):
                load(n, None, 0, srcs, dsts)

            def two(n, ca, cb, width=128):
                s = n % 2
                parts(n, [W2[:, :, ca:ca + width], W2[:, :, cb:cb + width]],
                      [raw[:, s, 0, :, 0:width], raw[:, s, 1, :, 0:width]])

            n = N_IN2
            two(n, O_IQ, O_IQ + 128)
            s = (n + 1) % 2
            parts(n + 1, [W2[:, :, O_IK:O_IK + 64], W2[:, :, O_IK:O_IK + 64], W2[:, :, O_MF:O_MF + 4],
                          W2[:, :, O_MI:O_MI + 4], W2[:, :, O_IW:O_IW + 4]],
                  [raw[:, s, 0, :, 0:64], raw[:, s, 0, :, 64:128], raw[:, s, 1, :, 0:4], raw[:, s, 1, :, 32:36],
                   raw[:, s, 1, :, 64:68]])
            for g in range(LG):
                two(n + 2 + g, O_LX + 128 * g, O_LG + 128 * g)
            two(n + 5, O_AQ, O_AQ + 128)
            two(n + 6, O_AK, O_AK + 128)
            two(n + 7, O_AV, O_AV + 128)
            for c in range(3):
                two(n + 8 + c, O_MV + 256 * c, O_MV + 256 * c + 128)
            for h in range(ML_H):
                two(n + 11 + h, O_MQ + ML_D * h, O_MK + ML_D * h, ML_D)
            wide(w_o2, N_WO2, 2)
            up(w_up2, N_UP2)
            down(w_down2, N_DN2)
            for t in range(TT):
                sp.wait_ge(s_oc, t + 1)
                sp.dma_start(out[0, 128 * t:128 * (t + 1), :], xo[:, t % 2, :]).then_inc(s_out[t % 2], 16)
            for b in range(2):
                sp.wait_ge(s_out[b], 8 * TT)

        @block.gpsimd
        def _(pool):
            x = A["x"][0]
            pool.dma_start(xrow[:], x.rearrange("(t p) d -> p t d", p=128)).then_inc(s_in, 16)
            pool.dma_start(mrow[:], A["meta_tokens"]).then_inc(s_in, 16)
            for v, name in ((V_MIX, "norm_mix_w"), (V_CB, "conv_dw_b"), (V_LNW, "conv_ln_w"), (V_LNB, "conv_ln_b"),
                            (V_FFN, "norm_ffn_w"), (V_PRE, "norm_mix_pre_2"), (V_POST, "norm_mix_post_2"),
                            (V_FPRE, "norm_ffn_pre_2"), (V_FPOST, "norm_ffn_post_2"), (V_SUB, "subln_w"),
                            (V_LCB, "lru_conv_b_2"), (V_LBA, "lru_b_a_2"), (V_LBX, "lru_b_x_2"),
                            (V_LAM, "lru_lambda_2")):
                a = A[name][0].rearrange("(g p) -> g p", p=128)
                pool.dma_start(vrow[v:v + a.shape[0], :], a).then_inc(s_in, 16)
            pool.dma_start(vrow[V_FIN:V_FIN + 8, :], A["norm_final_w"].rearrange("(g p) -> g p", p=128)).then_inc(s_in, 16)
            pool.dma_start(vrow[V_LCW:V_LCW + 12, :],
                           A["lru_conv_w_2"][0].rearrange("k (g p) -> (k g) p", p=128)).then_inc(s_in, 16)
            cw = A["conv_dw_w"][0].rearrange("k (g p) -> (k g) p", p=128)
            for j in range(2):
                pool.dma_start(crow[:, j, :], cw[124 * j:124 * (j + 1), :]).then_inc(s_in, 16)
            for b, (w, bias) in enumerate((("ffn_dw_w", "ffn_dw_b"), ("ffn_conv_w_2", "ffn_conv_b_2"))):
                pool.dma_start(frow[:, b, 0:3, :], A[w][0].rearrange("k (g p) -> g k p", p=128)).then_inc(s_in, 16)
                pool.dma_start(frow[:, b, 3, :], A[bias][0].rearrange("(g p) -> g p", p=128)).then_inc(s_in, 16)
            for j, name in enumerate(("lambda_q1", "lambda_k1", "lambda_q2", "lambda_k2")):
                pool.dma_start(lamv[:, j, :], A[name].to_broadcast([128, 64])).then_inc(s_in, 16)
            pool.memset(ident[:], 0.0).then_inc(s_id, 1)
            pool.wait_ge(s_id, 1)
            pool.affine_select(out=ident[:], in_=ident[:], compare_op=ALU.not_equal, fill=1.0, base=0,
                               pattern=[[-1, 128]], channel_multiplier=1).then_inc(s_id, 1)
            pool.memset(ones[:], 1.0).then_inc(s_id, 1)
            pool.memset(eps6[:], 1e-6).then_inc(s_id, 1)
            pool.memset(eps5[:], 1e-5).then_inc(s_id, 1)

            pool.wait_ge(s_x2, KT)
            pool.memset(wab[:], 0.0).then_inc(s_pz, 1)
            pool.memset(sel[:], 0.0).then_inc(s_pz, 1)
            pool.memset(tri[:], 0.0).then_inc(s_pz, 1)
            pool.wait_ge(s_pz, 3)
            pool.affine_select(out=sel[:], in_=sel[:], compare_op=ALU.not_equal, fill=1.0, base=0,
                               pattern=[[-1, ML_H], [0, 128]], channel_multiplier=1).then_inc(s_pz, 1)
            pool.affine_select(out=tri[:], in_=tri[:], compare_op=ALU.is_ge, fill=BIG, base=0,
                               pattern=[[1, 128]], channel_multiplier=-1).then_inc(s_pz, 1)
            for j, name in enumerate(("lru_w_a_2", "lru_w_x_2")):
                w = A[name][0]
                for b in range(2 * LG):
                    r = 64 * (b % 2)
                    pool.dma_start(wab[r:r + 64, j, b // 2, r:r + 64], w[b]).then_inc(s_p2, 16)
            pool.dma_start(mnb[:], A["mlstm_norm_2"].to_broadcast([128, ML_W])).then_inc(s_p2, 16)
            pool.dma_start(bif[:, 0:1], A["b_igate_2"].rearrange("a h -> h a")).then_inc(s_p2, 16)
            pool.dma_start(bif[:, 1:2], A["b_fgate_2"].rearrange("a h -> h a")).then_inc(s_p2, 16)

        N_IN = 16 * (2 + 14 + 2 + 2 + 4 + 4)

        @block.tensor
        def _(pe):
            mm, tr = nc.tensor.matmul, nc.tensor.transpose

            def all_free(gi):
                pe.wait_ge(s_ea, CREDIT + EV[:gi + 1].count("A"))
                pe.wait_ge(s_ed, CREDIT + EV[:gi + 1].count("D"))

            def project(ps, n, half, X, c0, nn, slots, i=None, st=0, rows=128, banks=2):
                if half == 0:
                    pe.wait_ge(s_lo, lin(n + 1, st, i))
                gi = 2 * n + half
                if slots and i is None:
                    e, c = evacuated(gi - slots)
                    if e != "-":
                        pe.wait_ge(s_ea if e == "A" else s_ed, c)
                elif slots:
                    e, c1 = evacuated(gi + 2 * st - slots)
                    first = gi - gi % 2
                    per = EV[first:first + 2 * st].count(e)
                    pe.wait_ge(s_ea if e == "A" else s_ed, lin(c1 - per, per, i))
                s = n % 2
                for k in range(KT):
                    for p, (W, Y) in enumerate(((wh, X[0]), (wh, X[1]), (wl, X[0]))):
                        for a in range(banks):
                            ins = mm(ps[0:rows, a, 0:nn], W[:, s, half, k, 0:rows], Y[:, k, c0 + a * nn:c0 + (a + 1) * nn],
                                     start=(k == 0 and p == 0), stop=(k == KT - 1 and p == 2))
                ins.then_inc(s_mm, 1)

            def wide(n0, X, c0, nn, slots, turns=2, banks=2, count=None):
                all_free(2 * n0 - 1)
                with pe.Fori(0, turns) as i:
                    for j in range(2):
                        for half in range(2):
                            project(ALLP[(2 * j + half) % slots], n0 + j, half, X, c0, nn, slots, i, 2, banks=banks)

            def down(n0):
                all_free(2 * n0 - 1)
                e = EV[2 * n0 + 3]
                before = CREDIT + EV[:2 * n0].count(e)
                with pe.Fori(0, 4) as i:
                    for g in range(2):
                        ps = psP[g]
                        for j in range(2):
                            n = n0 + 2 * g + j
                            pe.wait_ge(s_lo, lin(n + 1, 4, i))
                            if j == 0:
                                pe.wait_ge(s_ed if e == "D" else s_ea, lin(before + g - 1, 2, i))
                            s = n % 2
                            fh = wh[:, s].rearrange("p a k c -> p (a k) c")
                            fl = wl[:, s].rearrange("p a k c -> p (a k) c")
                            for k in range(KD):
                                kk = j * KD + k
                                for p, (W, Y) in enumerate(((fh, acth), (fh, actl), (fl, acth))):
                                    ins = mm(ps[:, 0, :], W[:, k, :], Y[:, kk, :], start=(kk == 0 and p == 0),
                                             stop=(kk == FG - 1 and p == 2))
                            ins.then_inc(s_mm, 2)

            def sums(use, ps, nn, inp=None):
                for k in range(KT):
                    pe.wait_ge(s_sq, 8 * use + k + 1)
                    for a in range(2):
                        ins = mm(ps[:, a, 0:nn], ones[:], sq[:, k % 2, a * nn:(a + 1) * nn], start=(k == 0), stop=(k == KT - 1))
                    ins.then_inc(s_sqf, 1)

            pe.wait_ge(s_id, 5)
            pe.wait_ge(s_in, N_IN)
            tr(psS[0][:, 0, 0:V_ROWS], vrow[:], ident[0:V_ROWS, 0:V_ROWS])
            for j in range(2):
                tr(psS[0][:, 0, 128 + 124 * j:252 + 124 * j], crow[:, j, :], ident[0:124, 0:124])
            for b in range(2):
                for v in range(4):
                    o = (4 * b + v) * 2 * FG
                    ins = tr(psS[0][:, 1, o:o + 2 * FG], frow[:, b, v, :], ident[0:2 * FG, 0:2 * FG])
            ins.then_inc(s_ct, 1)
            for k in range(KT):
                ps = ALLP[k % 4]
                if k == 2:
                    pe.wait_ge(s_cc, 2)
                if k >= 4:
                    pe.wait_ge(s_hx, k - 3)
                    pe.wait_ge(s_hm, k - 3)
                for t in range(TT):
                    tr(ps[:, 0, 128 * t:128 * (t + 1)], xrow[:, t, 128 * k:128 * (k + 1)], ident[:])
                tr(ps[:, 1, 0:NM], mrow[:, 128 * k:128 * (k + 1)], ident[0:NM, 0:NM]).then_inc(s_xt, 1)
            pe.wait_ge(s_hx, 8)
            pe.wait_ge(s_hm, 8)
            sums(0, psP[0], HT)
            pe.wait_ge(s_nl, 8)
            X = (xh, xl)
            for n in range(2):
                for half in range(2):
                    project(ALLP[2 * n + half], n, half, X, 0, HT, None)
            with pe.Fori(0, 3) as i:
                for j in range(2):
                    for half in range(2):
                        project(ALLP[2 * j + half], 2 + j, half, X, 0, HT, 4, i, 2)

            def scores(r, t, h, i):
                if t < 2:
                    pe.wait_ge(s_ex, lin(4 + 4 * h, 8, i))
                    if t == 0:
                        pe.wait_ge(s_sc, lin(1 + h, 2, i))
                elif t == 2:
                    pe.wait_ge(s_ex, lin(4 + 4 * h + 1, 8, i))
                else:
                    pe.wait_ge(s_ex, lin(4 + 4 * h + 3, 8, i))
                for m in range(2):
                    P = slice(64 * m, 64 * m + 64)
                    q = qkvg[P, r, 0, NM + 128 * t:NM + 128 * (t + 1)]
                    K = qkvg[P, r, 1, :]
                    if t < 3:
                        b = t % 2
                        mm(psS[m][:, b, 0:PW[t]], q, K[:, 0:PW[t]], start=True, stop=False)
                        last = psS[m][:, b, PW[t] - 64:PW[t]]
                    else:
                        mm(psS[m][:, 0, 0:HT], q, K[:, 0:HT], start=True, stop=True)
                        mm(psS[m][:, 1, 0:HT], q, K[:, HT:T], start=True, stop=False)
                        last = psS[m][:, 1, HT - 64:HT]
                    ins = mm(last, mki[P, :], mkk[P, :], start=False, stop=True)
                    if t == 0:
                        ins = mm(psS[m][0:NM, 0, PW[0]:PW[0] + NM], qkvg[P, r, 0, 0:NM], K[:, 0:NM], start=True, stop=True)
                ins.then_inc(s_qk, 1)

            def values(r, h, i):
                pe.wait_ge(s_os, lin(1 + h, 2, i))
                pe.wait_ge(s_oy, lin(1 + h, 2, i))
                for j in range(TT):
                    tr(psP[1][:, 0, 128 * j:128 * (j + 1)], qkvg[:, r, 2, NM + 128 * j:NM + 128 * (j + 1)], ident[:])
                tr(psP[1][0:NM, 1, 0:128], qkvg[:, r, 2, 0:NM], ident[:]).then_inc(s_at, 1)

            def probs(t, h, i):
                pe.wait_ge(s_cb, lin(4 * h + t + 1, 8, i))
                pe.wait_ge(s_ac, lin(5 * h + t + 1, 10, i))
                for j in range(t + 1):
                    o = PO[t] + NM + 128 * j
                    tr(psP[1][:, 0, 128 * j:128 * (j + 1)], prob[:, 0, o:o + 128], ident[:])
                ins = tr(psP[1][0:NM, 1, 0:128], prob[:, 0, PO[t]:PO[t] + NM], ident[:])
                if t == 0:
                    ins = tr(psP[1][0:NM, 1, 128:128 + NM], pmeta[:, 0, :], ident[0:NM, 0:NM])
                ins.then_inc(s_at, 1)

            def outputs(h, i):
                pe.wait_ge(s_ac, lin(5 * h + 5, 10, i))
                mm(psP[1][:, 0, :], vtok[0:NM, TT, :], aTm[:, 0:S], start=True, stop=False)
                for j in range(TT):
                    mm(psP[1][:, 0, 128 * j:S], vtok[:, j, :], aT[:, j, 128 * j:S], start=False, stop=(j == TT - 1))
                mm(psP[1][:, 1, 0:NM], vtok[0:NM, TT, :], aTm[:, S:S + NM], start=True, stop=True).then_inc(s_at_o, 1)
                pe.wait_ge(s_os, lin(1 + h + 1, 2, i))
                for a in range(2):
                    ins = mm(psS[0][:, a, 0:HT], ones[:], osq[:, a * HT:(a + 1) * HT], start=True, stop=True)
                ins.then_inc(s_ss, 1)

            def step(h, r, i, project_it=True, attend=True):
                n, p = N_HEAD + 2 * h, 1 - r
                a = h - 1
                if attend:
                    scores(p, 0, a, i)
                    scores(p, 1, a, i)
                if project_it:
                    project(psP[0], n, 0, X, 0, HT, 1, i, 4)
                if attend:
                    values(p, a, i)
                    probs(0, a, i)
                    scores(p, 2, a, i)
                if project_it:
                    project(psP[0], n, 1, X, 0, HT, 1, i, 4)
                if attend:
                    probs(1, a, i)
                    scores(p, 3, a, i)
                if project_it:
                    project(psP[0], n + 1, 0, X, 0, HT, 1, i, 4)
                if attend:
                    probs(2, a, i)
                if project_it:
                    project(psP[0], n + 1, 1, X, 0, HT, 1, i, 4)
                if attend:
                    probs(3, a, i)
                    outputs(a, i)

            all_free(2 * N_HEAD - 1)
            step(0, 0, None, attend=False)
            with pe.Fori(0, 3) as i:
                step(1, 1, i)
                step(2, 0, i)
            step(7, 1, None)
            step(8, 0, None, project_it=False)
            pe.wait_ge(s_sc, 1 + NH)
            pe.wait_ge(s_oy, 1 + NH)
            pe.wait_ge(s_cst, NH)
            for g in range(NH):
                for a in range(2):
                    ins = mm(psS[0][:, a, 0:H3], ones[:], conv[:, g, a * H3:(a + 1) * H3], start=(g == 0), stop=(g == NH - 1))
            ins.then_inc(s_lm, 1)
            wide(N_GC, X, C3, H3, 2, turns=2)
            sums(1, psS[1], H3)
            pe.wait_ge(s_nl, 16)
            pe.wait_ge(s_rt, 2)
            wide(N_CO, X, C3, H3, 2)
            pe.wait_ge(s_ml, 8)
            wide(N_WO, (mh, ml), 0, H3, 2)
            all_free(2 * N_UP - 1)
            sums(2, psP[0], H3)
            pe.wait_ge(s_nl, 24)
            wide(N_UP, X, C3, H3, 4, turns=FG // 2)
            pe.wait_ge(s_pl, CREDIT + FG)
            down(N_DN)

            all_free(2 * N_IN2 - 1)
            sums(3, psS[0], S // 2)
            sums(4, psS[1], S // 2)
            pe.wait_ge(s_nl, 8 * 4)
            ready2 = 16 * (12 + 3)

            def slot(gi):
                return psP[0][:, gi % 2, :]

            def project2(n, rows=(128, 128)):
                for half in range(2):
                    gi = 2 * n + half
                    ps = psP[0][:, gi % 2:gi % 2 + 1, :]
                    project(ps, n, half, X, NM, S, 2, rows=rows[half], banks=1)

            def project_tokens(n):
                for half in range(2):
                    gi = 2 * n + half
                    if half == 0:
                        pe.wait_ge(s_lo, n + 1)
                    e, c = evacuated(gi - 2)
                    pe.wait_ge(s_ea, c)
                    for a in range(2):
                        o = NM + 128 * (2 * half + a)
                        for k in range(KT):
                            for p, (Y, W) in enumerate(((xh, wh), (xl, wh), (xh, wl))):
                                ins = mm(psP[0][:, gi % 2, 256 * a:256 * (a + 1)], Y[:, k, o:o + 128], W[:, n % 2, :, k, :],
                                         start=(k == 0 and p == 0), stop=(k == KT - 1 and p == 2))
                    ins.then_inc(s_mm, 1)

            def index(t):
                if t:
                    pe.wait_ge(s_rl, 4 * t)
                n_ = 128 * (t + 1)
                for h in range(4):
                    P = slice(64 * (h % 2), 64 * (h % 2) + 64)
                    mm(psS[h // 2][:, h % 2, 0:n_], iq[P, h // 2, 128 * t:n_], ik[P, 0:n_], start=True, stop=True).then_inc(s_ix, 1)

            def lru_gates(g):
                pe.wait_ge(s_xc, g + 1)
                if g:
                    pe.wait_ge(s_ri, g)
                mm(psP[1][:, 0, :], wab[:, 0, g, :], xc[:, g, :], start=True, stop=True)
                mm(psP[1][:, 1, :], wab[:, 1, g, :], xc[:, g, :], start=True, stop=True).then_inc(s_rg, 1)

            def columns(src, j, count):
                for t in range(TT):
                    ins = tr(psP[1][:, 0, 16 * j + 4 * t:16 * j + 4 * t + 4], src[:, 128 * t:128 * (t + 1)], ident[0:4, 0:4])
                ins.then_inc(s_gt, 1)

            def logits(h, t):
                u_ = TT * h + t
                n_ = 128 * (t + 1)
                if u_ >= 4:
                    pe.wait_ge(s_pn, u_ - 3)
                P = slice(64 * (h % 2), 64 * (h % 2) + 64)
                mm(psS[u_ % 4 // 2][:, u_ % 2, 0:n_], aqk[P, h // 2, 128 * t:n_], aqk[P, 2 + h // 2, 0:n_], start=True,
                   stop=True).then_inc(s_lg, 1)

            def attend(h):
                for t in range(TT):
                    u_ = TT * h + t
                    pe.wait_ge(s_pn, u_ + 1)
                    if u_:
                        pe.wait_ge(s_pc, u_)
                    for j in range(t + 1):
                        ins = tr(psP[1][:, 0, 128 * j:128 * (j + 1)], pr[:, u_ % 2, 128 * j:128 * (j + 1)], ident[:])
                    ins.then_inc(s_pt, 1)
                pe.wait_ge(s_pc, TT * (h + 1))
                if h == 2:
                    pe.wait_ge(s_hcl, 1)
                r = 64 * (h % 2)
                for j in range(TT):
                    ins = mm(psP[1][r:r + 64, 1, 128 * j:S], av[:, j, 64 * h:64 * (h + 1)], PT[:, j, 128 * j:S], start=(j == 0),
                             stop=(j == TT - 1))
                ins.then_inc(s_po, 1)

            def mlstm(h):
                r = h % 2
                pe.wait_ge(s_mw, max(h, 0)) if h else None
                mm(psS[0][:, 0, :], sel[:, h, :], rows[:, 2, :], start=True, stop=True).then_inc(s_mb, 1)
                for j in range(TT):
                    if 4 * h + j >= 2:
                        pe.wait_ge(s_pp, 4 * h + j - 1)
                    mm(psS[1][:, j % 2, 0:S - 128 * j], mqk[:, r, 1, 128 * j:128 * (j + 1)], mqk[:, r, 0, 128 * j:S], start=True,
                       stop=True).then_inc(s_st, 1)
                pe.wait_ge(s_pp, 4 * h + 4)
                if h:
                    pe.wait_ge(s_mn, h)
                for t in range(TT):
                    for j in range(t + 1):
                        o = 97 * t
                        ins = mm(psP[1][:, 0, o:o + 97], PT[:, j, 128 * t:128 * (t + 1)], va[:, j, 97 * h:97 * (h + 1)],
                                 start=(j == 0), stop=(j == t))
                ins.then_inc(s_mo, 1)

            n = N_IN2
            project2(n)
            project2(n + 1, (128, 96))
            pe.wait_ge(s_ga, 1)
            columns(rows[:, 4, :], 0, 1)
            project2(n + 2)
            pe.wait_ge(s_gc, 1)
            index(0)
            project2(n + 3)
            index(1)
            index(2)
            pe.wait_ge(s_p2, ready2)
            pe.wait_ge(s_pz, 5)
            lru_gates(0)
            project2(n + 4)
            index(3)
            lru_gates(1)
            lru_gates(2)
            project2(n + 5)
            pe.wait_ge(s_mrow, 1)
            pe.wait_ge(s_ri, 3)
            columns(rows[:, 1, :], 1, 2)
            pe.wait_ge(s_fl, 1)
            pe.wait_ge(s_gc, 2)
            columns(rows[:, 3, :], 2, 3)
            project2(n + 6)
            project_tokens(n + 7)
            pe.wait_ge(s_ea, evacuated(2 * (n + 7) + 1)[1])
            pe.wait_ge(s_rl, 16)
            pe.wait_ge(s_gc, 3)
            for u_ in range(4):
                logits(0, u_)
            for c in range(3):
                project_tokens(n + 8 + c)
                attend(c)
                for t in range(TT):
                    logits(c + 1, t)
            project2(n + 11, (ML_D, ML_D))
            attend(3)
            project2(n + 12, (ML_D, ML_D))
            pe.wait_ge(s_pn, 16)
            pe.wait_ge(s_hcl, 2)
            mlstm(0)
            project2(n + 13, (ML_D, ML_D))
            mlstm(1)
            project2(n + 14, (ML_D, ML_D))
            mlstm(2)
            mlstm(3)
            pe.wait_ge(s_hg, 1)
            pe.wait_ge(s_pp, 16)
            pe.wait_ge(s_mw, 4)
            for g in range(LG):
                ps = (psS[0][:, 0, :], psS[0][:, 1, :], psS[1][:, 0, :])[g]
                for t in range(TT):
                    ins = tr(ps[:, 128 * t:128 * (t + 1)], hA[:, t, 128 * g:128 * (g + 1)], ident[:])
                ins.then_inc(s_ht, 1)
            pe.wait_ge(s_hl, 3)
            pe.wait_ge(s_hbl, 3)
            wide(N_WO2, (ch, cl), 0, S, 2, banks=1)
            sums(5, psS[0], S // 2)
            sums(6, psS[1], S // 2)
            pe.wait_ge(s_nl, 8 * 5)
            wide(N_UP2, X, NM, S, 4, turns=FG // 2, banks=1)
            pe.wait_ge(s_pl, CREDIT + 2 * FG)
            down(N_DN2)
            all_free(2 * N_END - 1)
            sums(7, psS[0], S // 2)
            pe.wait_ge(s_rt, 8)
            pe.wait_ge(s_y, 16)
            for t in range(TT):
                ps = psP[t % 2]
                if t >= 2:
                    pe.wait_ge(s_oc, t - 1)
                for k in range(KT):
                    ins = tr(ps[:, k // 4, 128 * (k % 4):128 * (k % 4 + 1)], hT[:, k, NM + 128 * t:NM + 128 * (t + 1)], ident[:])
                ins.then_inc(s_ot, 1)

        @block.scalar
        def _(act):
            fn = nc.scalar.activation
            own = Own(act, s_a)

            def hi(n, i=None, st=0):
                more = 48 if n >= N_IN2 + 1 and (n - N_IN2) % 2 else 0
                act.wait_ge(s_raw[n % 2], lin(32 * (n // 2 + 1) + more, 16 * st, i))
                if n >= 2:
                    act.wait_ge(s_mm, lin(2 * (n - 1), 2 * st, i))
                fn(wh[:, n % 2], raw[:, n % 2], ACT.Copy).then_inc(s_hi, 1)

            def squares(use, src, c0, n, ready):
                for k in range(KT):
                    ready(k)
                    if 8 * use + k >= 2:
                        act.wait_ge(s_sqf, 8 * use + k - 1)
                    fn(sq[:, k % 2, 0:n], src[:, k, c0:c0 + n], ACT.Square).then_inc(s_sq, 1)

            def root(use, ps, nn, eps):
                act.wait_ge(s_sqf, 8 * (use + 1))
                fn(rstd[:, 0:2 * nn].rearrange("p (a b) -> p a b", a=2), ps[:, :, 0:nn], ACT.Sqrt,
                   bias=eps[:], scale=1.0 / D).then_inc(s_rt, 1)

            def normed_hi(nf_use, c0, n):
                for k in range(KT):
                    act.wait_ge(s_nf, 8 * nf_use + k + 1)
                    fn(xh[:, k, c0:c0 + n], nf[:, k % 2, 0:n], ACT.Copy).then_inc(s_nh, 1)

            act.wait_ge(s_ct, 1)
            fn(vec[:], psS[0][:, 0, 0:V_ROWS], ACT.Copy)
            fn(cdw[:], psS[0][:, 0, 128:128 + CK * 8], ACT.Copy).then_inc(s_cc, 1)
            for k in range(KT):
                act.wait_ge(s_xt, k + 1)
                fn(hT[:, k, NM:T], ALLP[k % 4][:, 0, :], ACT.Copy).then_inc(s_hx, 1)
            act.wait_ge(s_lamo, 1)
            fn(lams[:, 2:4], lams[:, 0:2], ACT.Exp).then_inc(s_lame, 1)
            hi(0)

            def both(k):
                act.wait_ge(s_hx, k + 1)
                act.wait_ge(s_hm, k + 1)
            squares(0, hT, 0, T, both)
            root(0, psP[0], HT, eps6)
            normed_hi(0, 0, T)

            def glu_gate(n, i, st):
                hi(n + 1, i, st)
                act.wait_ge(s_mm, lin(2 * n + 2, 2 * st, i))
                act.wait_ge(s_ed, lin(CREDIT + n - 1, st, i))
                fn(sgl[:, n % 2, :].rearrange("p (a b) -> p a b", a=2), ALLP[(2 * n + 1) % 4][:, :, 0:HT],
                   ACT.Sigmoid).then_inc(s_ea, 1)

            glu_gate(0, None, 0)
            glu_gate(1, None, 0)
            with act.Fori(0, 3) as i:
                glu_gate(2, i, 2)
                glu_gate(3, i, 2)

            def empty(r, what, gi, i, st, func, scale):
                act.wait_ge(s_mm, lin(gi + 1, 2 * st, i))
                fn(qkvg[:, r, what, :].rearrange("p (a b) -> p a b", a=2), psP[0][:, :, 0:HT], func,
                   scale=scale).then_inc(s_ea, 1)

            def exps(t, h, i):
                act.wait_ge(s_mx, lin(4 * h + t + 1, 8, i))
                for m in range(2):
                    out = prob[:, m, PO[t]:PO[t] + PW[t]]
                    if t < 3:
                        src = psS[m][:, t % 2, 0:PW[t]]
                    else:
                        src = psS[m][:, :, 0:HT]
                        out = out.rearrange("p (a b) -> p a b", a=2)
                    ins = fn(out, src, ACT.Exp, bias=stat[:, 2 * t + m:2 * t + m + 1],
                             accum_out=stat[:, 8 + 2 * t + m:9 + 2 * t + m])
                    if t == 0:
                        ins = fn(pmeta[:, m, :], psS[m][0:NM, 0, PW[0]:PW[0] + NM], ACT.Exp,
                                 bias=stat[0:NM, 16 + m:17 + m], accum_out=stat[0:NM, 18 + m:19 + m])
                ins.then_inc(s_ex, 1)

            def copy_values(h, i):
                act.wait_ge(s_at, lin(5 * h + 1, 10, i))
                fn(vtok[:, 0:TT, :], psP[1][:, 0, :].rearrange("p (j e) -> p j e", j=TT), ACT.Copy)
                fn(vtok[0:NM, TT, :], psP[1][0:NM, 1, 0:128], ACT.Copy).then_inc(s_ac, 1)

            def copy_probs(t, h, i):
                act.wait_ge(s_at, lin(5 * h + t + 2, 10, i))
                fn(aT[:, 0:t + 1, 128 * t:128 * (t + 1)], psP[1][:, 0, 0:128 * (t + 1)].rearrange("p (j q) -> p j q", j=t + 1), ACT.Copy)
                ins = fn(aTm[:, 128 * t:128 * (t + 1)], psP[1][0:NM, 1, 0:128], ACT.Copy)
                if t == 0:
                    ins = fn(aTm[:, S:S + NM], psP[1][0:NM, 1, 128:128 + NM], ACT.Copy)
                ins.then_inc(s_ac, 1)

            def square_head(h, i):
                act.wait_ge(s_at_o, lin(h + 1, 2, i))
                fn(osq[:, NM:T], psP[1][:, 0, :], ACT.Square)
                fn(osq[:, 0:NM], psP[1][:, 1, 0:NM], ACT.Square).then_inc(s_os, 1)
                act.wait_ge(s_ss, lin(h + 1, 2, i))
                act.wait_ge(s_cv, lin(h + 1, 2, i))
                if i is None:
                    dst = u[:, h, 0:T].rearrange("p (a b) -> p a b", a=2)
                else:
                    dst = u[:, ds(i * 2 + h, 1), 0:T].rearrange("p o (a b) -> p (o a) b", a=2)
                fn(dst, psS[0][:, :, 0:HT], ACT.Copy).then_inc(s_sc, 1)

            def fetch(g, i, last=False):
                at_ = (lambda o: ds(i * 2 + o, 1)) if i is not None else (lambda o: slice(o, o + 1))
                if g > 0 or i is not None:
                    act.wait_ge(s_cv, lin(g, 2, i))
                    fn(conv[:, at_(g - 1), :], cacc[:], ACT.Copy).then_inc(s_cst, 1)
                if last:
                    return
                fn(cin[:], u[:, at_(g), :], ACT.Copy)
                taps = cdw[:].rearrange("p (k g) -> p g k", g=NH)
                fn(cwt[:, 0:CK], taps[:, at_(g), :], ACT.Copy)
                b = vec[:, V_CB:V_CB + 8]
                fn(cwt[:, CK:CK + 1], b[:, at_(g)], ACT.Copy).then_inc(s_cf, 1)

            def step(h, r, i, project_it=True, attend=True):
                n, p, a = N_HEAD + 2 * h, 1 - r, h - 1
                if project_it:
                    hi(n + 1, i, 4)
                if attend:
                    exps(0, a, i)
                    exps(1, a, i)
                if project_it:
                    empty(r, 0, 2 * n, i, 4, ACT.Copy, 0.125)
                if attend:
                    copy_values(a, i)
                    copy_probs(0, a, i)
                    exps(2, a, i)
                if project_it:
                    empty(r, 1, 2 * n + 1, i, 4, ACT.Copy, 1.0)
                    hi(n + 2, i, 4)
                if attend:
                    copy_probs(1, a, i)
                    exps(3, a, i)
                if project_it:
                    empty(r, 2, 2 * n + 2, i, 4, ACT.Copy, 1.0)
                if attend:
                    copy_probs(2, a, i)
                if project_it:
                    empty(r, 3, 2 * n + 3, i, 4, ACT.Tanh, 0.5)
                if attend:
                    copy_probs(3, a, i)
                    square_head(a, i)
                if project_it:
                    fetch(h + 1, i, last=(h == NH - 1 and i is None))

            act.wait_ge(s_ed, CREDIT + NH)
            fetch(0, None)
            step(0, 0, None, attend=False)
            with act.Fori(0, 3) as i:
                step(1, 1, i)
                step(2, 0, i)
            step(7, 1, None)
            step(8, 0, None, project_it=False)

            def sig_gate(n):
                hi(n + 1)
                for half in range(2):
                    gi = 2 * n + half
                    act.wait_ge(s_mm, gi + 1)
                    fn(sgc[:, 2 * (n - N_GC) + half, :].rearrange("p (a b) -> p a b", a=2), psP[gi % 2][:, :, 0:H3],
                       ACT.Sigmoid).then_inc(s_ea, 1)
            act.wait_ge(s_sc, 1 + NH)
            fn(u[:, :, 0:T], u[:, :, 0:T], ACT.Sqrt, bias=eps6[:], scale=1.0 / 128).then_inc(s_hr, 1)
            for n in range(N_GC, N_GC + 4):
                sig_gate(n)
            squares(1, conv, 0, T3, lambda k: act.wait_ge(s_lc, k + 1))
            root(1, psS[1], H3, eps5)
            for k in range(KT):
                act.wait_ge(s_ln, k + 1)
                if k >= 2:
                    act.wait_ge(s_nl, 8 + k - 1)
                own(fn(nf[:, k % 2, 0:T3], conv[:, k, :], ACT.Silu, scale=vec[:, V_LNW + k:V_LNW + k + 1],
                       bias=vec[:, V_LNB + k:V_LNB + k + 1]))
                fn(xh[:, k, C3:T], nf[:, k % 2, 0:T3], ACT.Copy).then_inc(s_nh, 1)
            for n in range(N_CO, N_CO + 4):
                hi(n + 1)
                for half in range(2):
                    g = 2 * (n - N_CO) + half
                    act.wait_ge(s_m, g + 1)
                    fn(mh[:, g, :], nf[:, g % 2, 0:T3], ACT.Copy).then_inc(s_mhi, 1)
            for n in range(N_WO, N_WO + 4):
                hi(n + 1)
            squares(2, hT, C3, T3, lambda k: act.wait_ge(s_ed, evacuated(2 * N_WO + k)[1]))
            root(2, psP[0], H3, eps6)
            normed_hi(1, C3, T3)

            def ffn(n0, slot0, func, start, width, use):
                with act.Fori(0, FG // 2) as i:
                    for j in range(2):
                        n = n0 + j
                        hi(n + 1, i, 2)
                        for x in range(2):
                            gi = 2 * n + x
                            act.wait_ge(s_mm, lin(gi + 1, 4, i))
                            if x == 0:
                                act.wait_ge(s_cva, lin(CREDIT * 2 + 2 * FG * use + 2 * (j - 1), 4, i))
                            src = ALLP[2 * j + x]
                            if width == T3:
                                fn(upr[:, j, x, :].rearrange("p (a b) -> p a b", a=2), src[:, :, 0:H3], ACT.Copy).then_inc(s_ea, 1)
                            else:
                                fn(upr[:, j, x, start:start + width], src[:, 0, :], ACT.Copy).then_inc(s_ea, 1)
                        act.wait_ge(s_cva, lin(CREDIT * 2 + 2 * FG * use + 2 * j + 1, 4, i))
                        fn(acc[:, 0, :], acc[:, 0, :], func).then_inc(s_sil, 1)
                        act.wait_ge(s_pr, lin(FG * use + j + 1, 2, i))
                        fn(acth[:, ds(i * 2 + j, 1), :], prod[:, j, :], ACT.Copy).then_inc(s_ph, 1)

            ffn(N_UP, 0, ACT.Silu, 0, T3, 0)
            def down(n0):
                with act.Fori(0, 8) as i:
                    for j in range(2):
                        hi(n0 + j + 1, i, 2)
            down(N_DN)

            HS = S // 2
            ready2 = 16 * (12 + 3)
            squares(3, hT, NM, S, lambda k: act.wait_ge(s_ed, CREDIT + EV[:2 * N_DN].count("D") + k + 1))
            root(3, psS[0], HS, eps6)
            squares(4, hT, NM, S, lambda k: act.wait_ge(s_x2, k + 1))
            root(4, psS[1], HS, eps6)
            normed_hi(2, NM, S)

            def full(gi):
                act.wait_ge(s_mm, gi + 1)
                return psP[0][:, gi % 2, :]

            def to(dst, gi, func=ACT.Copy, **kw):
                fn(dst, full(gi), func, **kw).then_inc(s_ea, 1)

            def index(t):
                n_ = 128 * (t + 1)
                for h in range(4):
                    act.wait_ge(s_ix, 4 * t + h + 1)
                    if 4 * t + h >= 2:
                        act.wait_ge(s_ixa, 4 * t + h - 1)
                    fn(rl[:, h % 2, 0:n_], psS[h // 2][:, h % 2, 0:n_], ACT.Relu, scale=0.5 * 0.125).then_inc(s_rl, 1)

            def lru_gates(g):
                act.wait_ge(s_rg, g + 1)
                fn(lx[:, g, 3:3 + S], psP[1][:, 0, :], ACT.Sigmoid, bias=vec[:, V_LBA + g:V_LBA + g + 1])
                fn(li[:, g, :], psP[1][:, 1, :], ACT.Sigmoid, bias=vec[:, V_LBX + g:V_LBX + g + 1]).then_inc(s_ri, 1)

            def columns(j):
                act.wait_ge(s_gt, j + 1)
                fn(gcol[:, j, :, :].rearrange("p a b -> p (a b)"), psP[1][:, 0, 16 * j:16 * j + 16], ACT.Copy).then_inc(s_gc, 1)

            def attend(h):
                for t in range(TT):
                    u_, n_ = TT * h + t, 128 * (t + 1)
                    act.wait_ge(s_pm, u_ + 1)
                    fn(pr[:, u_ % 2, 0:n_], pr[:, u_ % 2, 0:n_], ACT.Exp, bias=mx2[:, 0, u_ % 2:u_ % 2 + 1],
                       accum_out=mx2[:, 1, u_ % 2:u_ % 2 + 1]).then_inc(s_pe, 1)
                    act.wait_ge(s_pt, u_ + 1)
                    fn(PT[:, 0:t + 1, 128 * t:128 * (t + 1)], psP[1][:, 0, 0:n_].rearrange("p (j q) -> p j q", q=128),
                       ACT.Copy).then_inc(s_pc, 1)
                act.wait_ge(s_po, h + 1)
                if h % 2:
                    fn(ch[:, 6 + h // 2, :], psP[1][:, 1, :], ACT.Copy).then_inc(s_hc, 1)

            def mlstm(h):
                act.wait_ge(s_md, h + 1)
                for j in range(TT):
                    G = gcol[:, 1, j, h:h + 1]
                    ins = fn(PT[:, j, 128 * j:128 * (j + 1)], md[:, j, :], ACT.Exp, scale=-1.0, bias=G)
                    if j < TT - 1:
                        ins = fn(PT[:, j, 128 * (j + 1):S], psS[0][:, 0, 128 * (j + 1):S], ACT.Exp, scale=-1.0, bias=G)
                ins.then_inc(s_mw, 1)

            n = N_IN2
            hi(n + 1)
            to(iq[:, 0, :], 2 * n)
            to(iq[:, 1, :], 2 * n + 1)
            hi(n + 2)
            to(ik[:], 2 * n + 2)
            act.wait_ge(s_p2, ready2)
            g_ = full(2 * n + 3)
            fn(rows[:, 4, :], g_[64:68, :], ACT.Copy).then_inc(s_ga, 1)
            fn(rows[:, 1, :], g_[32:36, :], ACT.Copy).then_inc(s_ga, 1)
            fn(rows[:, 0, :], g_[0:4, :], ACT.Identity, bias=bif[:, 1:2]).then_inc(s_ea, 1)
            act.wait_ge(s_az, 1)
            fn(rows[:, 2, :], rows[:, 2, :], ACT.Exp, scale=-1.0).then_inc(s_ez, 1)
            act.wait_ge(s_lb, 1)
            fn(lcol[:, 1, :], lcol[:, 0, :], ACT.Exp, scale=-1.0).then_inc(s_ez, 1)
            columns(0)
            hi(n + 3)
            to(lx[:, 0, 3:], 2 * n + 4)
            to(lg[:, 0, :], 2 * n + 5, ACT.Gelu_apprx_tanh)
            index(0)
            hi(n + 4)
            to(lx[:, 1, 3:], 2 * n + 6)
            to(lg[:, 1, :], 2 * n + 7, ACT.Gelu_apprx_tanh)
            index(1)
            index(2)
            lru_gates(0)
            hi(n + 5)
            to(lx[:, 2, 3:], 2 * n + 8)
            to(lg[:, 2, :], 2 * n + 9, ACT.Gelu_apprx_tanh)
            index(3)
            lru_gates(1)
            lru_gates(2)
            act.wait_ge(s_lb, 2)
            for g in range(LG):
                act.wait_ge(s_ri, g + 1)
                own(fn(lt[:, g, :], lx[:, g, 3:], ACT.Tanh, scale=lcol[:, 2, g:g + 1]))
                fn(lx[:, g, 3:], lx[:, g, 3:], ACT.Exp, scale=lcol[:, 2, g:g + 1]).then_inc(s_la, 1)
            hi(n + 6)
            act.wait_ge(s_ixa, 16)
            to(aqk[:, 0, :], 2 * n + 10)
            to(aqk[:, 1, :], 2 * n + 11)
            act.wait_ge(s_mrow, 1)
            fn(rows[:, 3, :], rows[:, 3, :], ACT.Exp, scale=-1.0).then_inc(s_fl, 1)
            act.wait_ge(s_lv, 1)
            fn(lt[:], lt[:], ACT.Sqrt).then_inc(s_lq, 1)
            columns(1)
            columns(2)
            hi(n + 7)
            to(aqk[:, 2, :], 2 * n + 12)
            to(aqk[:, 3, :], 2 * n + 13)
            hi(n + 8)
            for half in range(2):
                to(av[:, 2 * half:2 * half + 2, :].rearrange("p a c -> p (a c)"), 2 * n + 14 + half)
            for g in range(LG):
                act.wait_ge(s_hb, g + 1)
                fn(ch[:, 3 + g, :], li[:, g, :], ACT.Copy).then_inc(s_hbh, 1)
            act.wait_ge(s_hbl, LG)
            act.wait_ge(s_pz2, 1)
            for c in range(3):
                hi(n + 9 + c)
                for half in range(2):
                    gi = 2 * (n + 8 + c) + half
                    f_ = full(gi).rearrange("p (a c) -> p a c", a=2)
                    tt = slice(2 * half, 2 * half + 2)
                    ins = None
                    c0 = 256 * c
                    for h in range(ML_H):
                        a0, a1 = max(c0, ML_D * h), min(c0 + 256, ML_D * (h + 1), ML_W)
                        if a0 < a1:
                            o = a0 - ML_D * h + (ML_D + 1) * h
                            ins = fn(va[:, tt, o:o + a1 - a0], f_[:, :, a0 - c0:a1 - c0], ACT.Copy)
                    a0 = max(c0, ML_W)
                    if a0 < c0 + 256:
                        ins = fn(mo[:, tt, a0 - ML_W:c0 + 256 - ML_W], f_[:, :, a0 - c0:256], ACT.Sigmoid)
                    ins.then_inc(s_ea, 1)
                attend(c)

            def qk(h):
                gi = 2 * (n + 11 + h)
                fn(mqk[:, h % 2, 0, :], full(gi)[0:ML_D, :], ACT.Copy).then_inc(s_ea, 1)
                fn(mqk[:, h % 2, 1, :], full(gi + 1)[0:ML_D, :], ACT.Copy, scale=ML_D ** -0.5).then_inc(s_ea, 1)

            hi(n + 12)
            qk(0)
            attend(3)
            hi(n + 13)
            qk(1)
            act.wait_ge(s_po, 4)
            mlstm(0)
            hi(n + 14)
            act.wait_ge(s_mo, 1)
            qk(2)
            mlstm(1)
            hi(n + 15)
            act.wait_ge(s_mo, 2)
            qk(3)
            mlstm(2)
            act.wait_ge(s_mo, 3)
            mlstm(3)
            act.wait_ge(s_mn, 4)
            act.wait_ge(s_mo, 4)
            fn(PT[:, 0:3, :].rearrange("p a b -> p (a b)"), hA[:].rearrange("p t c -> p (t c)"), ACT.Square).then_inc(s_hs, 1)
            act.wait_ge(s_h2, 1)
            fn(mx2[:, 2:4, :].rearrange("p a b -> p (a b)"), mx2[:, 2:4, :].rearrange("p a b -> p (a b)"), ACT.Sqrt,
               scale=1.0 / ML_D, bias=eps6[:]).then_inc(s_hrt, 1)
            for g in range(LG):
                act.wait_ge(s_ht, g + 1)
                ps = (psS[0][:, 0, :], psS[0][:, 1, :], psS[1][:, 0, :])[g]
                fn(ch[:, g, :], ps, ACT.Copy).then_inc(s_hh, 1)
            act.wait_ge(s_hl, 3)
            for c in range(4):
                hi(N_WO2 + c + 1)
                for half in range(2):
                    gi = 2 * (N_WO2 + c) + half
                    act.wait_ge(s_mm, gi + 1)
                    fn(mT[:, 2 * c + half, :], psP[half][:, 0, :], ACT.Copy).then_inc(s_ea, 1)
            squares(5, mT, 0, S, lambda k: act.wait_ge(s_ea, evacuated(2 * N_WO2 + k)[1]))
            root(5, psS[0], HS, eps6)
            squares(6, hT, NM, S, lambda k: act.wait_ge(s_y, k + 1))
            root(6, psS[1], HS, eps6)
            normed_hi(3, NM, S)
            act.wait_ge(s_uz, 1)
            ffn(N_UP2, 0, ACT.Gelu_apprx_tanh, 4, S, 1)

            def down2(i, turn_last=False):
                for g in range(2):
                    hi(N_DN2 + 2 * g + 1, i, 4)
                    if not (turn_last and g == 1):
                        hi(N_DN2 + 2 * g + 2, i, 4)
                    act.wait_ge(s_mm, lin(2 * N_DN2 + 4 * g + 4, 8, i))
                    fn(mT2[:, ds(i * 2 + g, 1), :] , psP[g][:, 0, :], ACT.Copy).then_inc(s_ea, 1)

            with act.Fori(0, 3) as i:
                down2(i)
            for g in range(2):
                hi(N_DN2 + 12 + 2 * g + 1)
                if g == 0:
                    hi(N_DN2 + 14)
                act.wait_ge(s_mm, 2 * N_DN2 + 24 + 4 * g + 4)
                fn(mT2[:, 6 + g, :], psP[g][:, 0, :], ACT.Copy).then_inc(s_ea, 1)
            squares(7, mT2, 0, S, lambda k: act.wait_ge(s_ea, evacuated(2 * N_DN2 + 4 * k + 3)[1]))
            root(7, psS[0], HS, eps6)
            for t in range(TT):
                act.wait_ge(s_ot, t + 1)
                if t >= 2:
                    act.wait_ge(s_out[t % 2], 8 * (t - t % 2))
                fn(xo[:, t % 2, :].rearrange("p (a b) -> p a b", a=2), psP[t % 2][:], ACT.Copy).then_inc(s_oc, 1)

        @block.vector
        def _(dve):
            V = nc.vector
            own = Own(dve, s_v)

            def lo(n, i=None, st=0):
                dve.wait_ge(s_hi, lin(n + 1, st, i))
                V.tensor_tensor(wl[:, n % 2], raw[:, n % 2], wh[:, n % 2].bitcast(f32), ALU.subtract).then_inc(s_lo, 1)

            def inverse(use, n):
                dve.wait_ge(s_rt, use + 1)
                own(V.reciprocal(rstd[:, 0:n], rstd[:, 0:n]))

            def normed_lo(k, use, c0, n):
                dve.wait_ge(s_nh, 8 * use + k + 1)
                V.tensor_tensor(xl[:, k, c0:c0 + n], nf[:, k % 2, 0:n], xh[:, k, c0:c0 + n].bitcast(f32),
                                ALU.subtract).then_inc(s_nl, 1)

            def norm(sum_use, use, src, s0, c0, n, weight):
                inverse(sum_use, n)
                for k in range(KT):
                    if 8 * use + k >= 2:
                        dve.wait_ge(s_nl, 8 * use + k - 1)
                    V.scalar_tensor_tensor(nf[:, k % 2, 0:n], src[:, k, s0:s0 + n], vec[:, weight + k:weight + k + 1],
                                           rstd[:, 0:n], ALU.mult, ALU.mult).then_inc(s_nf, 1)
                    if k:
                        normed_lo(k - 1, use, c0, n)
                normed_lo(KT - 1, use, c0, n)

            dve.wait_ge(s_in, N_IN)
            lv = lamv[:].rearrange("p (a b) c -> p a b c", b=2)
            own(V.tensor_tensor(lamp[:], lv[:, :, 0, :], lv[:, :, 1, :], ALU.mult))
            V.tensor_reduce(lams[:, 0:2], lamp[:], AX, ALU.add).then_inc(s_lamo, 1)
            dve.wait_ge(s_ct, 1)
            V.tensor_copy(fdw[:].rearrange("p b v g -> p (b v g)"), psS[0][:, 1, 0:16 * FG]).then_inc(s_cc, 1)
            for k in range(KT):
                dve.wait_ge(s_xt, k + 1)
                V.tensor_copy(hT[:, k, 0:NM], ALLP[k % 4][:, 1, 0:NM]).then_inc(s_hm, 1)
            dve.wait_ge(s_lame, 1)
            own(V.tensor_tensor(lams[:, 4:5], lams[:, 3:4], lams[:, 2:3], ALU.subtract))
            own(V.tensor_scalar(nlam[:], lams[:, 4:5], -LAMBDA_INIT, None, ALU.add))
            dve.wait_ge(s_cc, 2)
            own(V.tensor_scalar(vec[:, V_SUB:V_SUB + 1], vec[:, V_SUB:V_SUB + 1], 0.5 * (1.0 - LAMBDA_INIT), None, ALU.mult))
            for c, (sm, k) in enumerate(((s_ed, CREDIT), (s_ea, CREDIT), (s_oy, 1), (s_ex, 4), (s_sc, 1), (s_os, 1),
                                         (s_cva, 2 * CREDIT), (s_pl, CREDIT))):
                V.memset(cred[:, c:c + 1], 0.0).then_inc(sm, k)
            lo(0)
            norm(0, 0, hT, 0, 0, T, V_MIX)
            V.memset(u[:, :, 0:PAD], 0.0)
            V.memset(mki[:], 0.0)
            own(V.memset(mkk[:], 0.0))
            for m in range(2):
                V.memset(mki[64 * m:64 * m + 1, 0:64], 1.0)
                V.memset(mkk[64 * m:64 * m + 1, :], -BIG)

            def glu(n, i, st):
                lo(n + 1, i, st)
                dve.wait_ge(s_ea, lin(CREDIT + n + 1, st, i))
                g = slice(n, n + 1) if i is None else ds(i * 2 + n, 1)
                V.tensor_tensor(u[:, g, PAD:].rearrange("p o (a b) -> p (o a) b", a=2), ALLP[(2 * n) % 4][:, :, 0:HT],
                                sgl[:, n % 2, :].rearrange("p (a b) -> p a b", a=2), ALU.mult).then_inc(s_ed, 1)

            glu(0, None, 0)
            glu(1, None, 0)
            with dve.Fori(0, 3) as i:
                glu(2, i, 2)
                glu(3, i, 2)

            def maxima(t, h, i):
                dve.wait_ge(s_qk, lin(4 * h + t + 1, 8, i))
                for m in range(2):
                    src = psS[m][:, t % 2, 0:PW[t]] if t < 3 else psS[m][:, :, 0:HT]
                    ins = V.tensor_reduce(stat[:, 2 * t + m:2 * t + m + 1], src, AX if t < 3 else mybir.AxisListType.XY, ALU.max, negate=True)
                    if t == 0:
                        ins = V.tensor_reduce(stat[0:NM, 16 + m:17 + m], psS[m][0:NM, 0, PW[0]:PW[0] + NM], AX, ALU.max, negate=True)
                ins.then_inc(s_mx, 1)

            def combine(t, h, i):
                dve.wait_ge(s_ex, lin(4 + 4 * h + t + 1, 8, i))
                todo = [(slice(0, 128), prob[:, 0, PO[t]:PO[t] + PW[t]], prob[:, 1, PO[t]:PO[t] + PW[t]], 8 + 2 * t)]
                if t == 0:
                    todo.insert(0, (slice(0, NM), pmeta[:, 0, :], pmeta[:, 1, :], 18))
                for P, p0, p1, c in todo:
                    own(V.reciprocal(stat[P, c:c + 2], stat[P, c:c + 2]))
                    V.tensor_scalar(p0, p0, stat[P, c:c + 1], None, ALU.mult)
                    own(V.tensor_scalar(stat[P, c + 1:c + 2], stat[P, c + 1:c + 2], nlam[P, :], None, ALU.mult))
                    ins = V.scalar_tensor_tensor(p0, p1, stat[P, c + 1:c + 2], p0, ALU.mult, ALU.add)
                ins.then_inc(s_cb, 1)

            def taps(lo_, hi_, h, i):
                for k in range(lo_, hi_):
                    w = cwt[:, k:k + 1]
                    src = cin[:, C3 + k:C3 + k + T3]
                    if k == 0:
                        dve.wait_ge(s_cf, lin(h + 1, 2, i))
                        own(V.tensor_scalar(cacc[:], src, w, cwt[:, CK:CK + 1], ALU.mult, ALU.add))
                    elif k < CK - 1:
                        own(V.scalar_tensor_tensor(cacc[:], src, w, cacc[:], ALU.mult, ALU.add))
                    else:
                        V.scalar_tensor_tensor(cacc[:], src, w, cacc[:], ALU.mult, ALU.add).then_inc(s_cv, 1)

            def gated(h, r, i):
                dve.wait_ge(s_os, lin(1 + h + 1, 2, i))
                g = slice(h, h + 1) if i is None else ds(i * 2 + h, 1)
                V.scalar_tensor_tensor(yT[:, g, NM:T], qkvg[:, r, 3, NM:T], 1.0, psP[1][:, 0, :], ALU.add, ALU.mult)
                V.scalar_tensor_tensor(yT[:, g, 0:NM], qkvg[:, r, 3, 0:NM], 1.0, psP[1][:, 1, 0:NM], ALU.add,
                                       ALU.mult).then_inc(s_oy, 1)

            def step(h, r, i, project_it=True, attend=True):
                n, p, a = N_HEAD + 2 * h, 1 - r, h - 1
                if attend:
                    maxima(0, a, i)
                    maxima(1, a, i)
                if project_it:
                    lo(n + 1, i, 4)
                if attend:
                    combine(0, a, i)
                    combine(1, a, i)
                if project_it:
                    taps(0, 9, h, i)
                if attend:
                    maxima(2, a, i)
                    combine(2, a, i)
                if project_it:
                    taps(9, 17, h, i)
                    lo(n + 2, i, 4)
                if attend:
                    maxima(3, a, i)
                    combine(3, a, i)
                if project_it:
                    taps(17, CK, h, i)
                if attend:
                    gated(a, p, i)

            step(0, 0, None, attend=False)
            with dve.Fori(0, 3) as i:
                own.enter(i, OWN_HEADS)
                step(1, 1, i)
                step(2, 0, i)
                own.leave(3)
            step(7, 1, None)
            step(8, 0, None, project_it=False)

            lo(N_GC + 1)
            dve.wait_ge(s_lm, 1)
            for g in range(NH):
                V.scalar_tensor_tensor(span(conv, g, 0, H3), psS[0][:, :, 0:H3], -1.0 / D, span(conv, g, 0, H3),
                                       ALU.mult, ALU.add).then_inc(s_lc, 1)
            lo(N_GC + 2)
            dve.wait_ge(s_hr, 1)
            own(V.reciprocal(u[:, :, 0:T], u[:, :, 0:T]))
            lo(N_GC + 3)
            own(V.scalar_tensor_tensor(yT[:], yT[:], vec[:, V_SUB:V_SUB + 1], u[:, :, 0:T], ALU.mult, ALU.mult))
            lo(N_GC + 4)
            inverse(1, T3)
            for k in range(KT):
                V.tensor_tensor(conv[:, k, :], conv[:, k, :], rstd[:, 0:T3], ALU.mult).then_inc(s_ln, 1)
            for k in range(KT):
                normed_lo(k, 1, C3, T3)
            def mixed_lo(g):
                dve.wait_ge(s_mhi, g + 1)
                V.tensor_tensor(ml[:, g, :], nf[:, g % 2, 0:T3], mh[:, g, :].bitcast(f32), ALU.subtract).then_inc(s_ml, 1)

            for n in range(N_CO, N_CO + 4):
                lo(n + 1)
                for half in range(2):
                    gi = 2 * n + half
                    g = gi - 2 * N_CO
                    dve.wait_ge(s_mm, gi + 1)
                    t = nf[:, g % 2, 0:T3]
                    if g >= 2:
                        dve.wait_ge(s_ml, g - 1)
                    ins = V.tensor_tensor(t.rearrange("p (a b) -> p a b", a=2), psP[gi % 2][:, :, 0:H3],
                                          span(sgc, g, 0, H3), ALU.mult)
                    ins.then_inc(s_ed, 1)
                    dve.wait_ge(s_ed, evacuated(gi)[1])
                    V.tensor_tensor(t, t, yT[:, g, C3:T], ALU.add).then_inc(s_m, 1)
                    mixed_lo(g)
            for n in range(N_WO, N_WO + 4):
                lo(n + 1)
                for half in range(2):
                    gi = 2 * n + half
                    dve.wait_ge(s_mm, gi + 1)
                    V.tensor_tensor(span(hT, gi - 2 * N_WO, C3, H3), psP[gi % 2][:, :, 0:H3],
                                    span(hT, gi - 2 * N_WO, C3, H3), ALU.add).then_inc(s_ed, 1)
            norm(2, 2, hT, C3, C3, T3, V_FFN)

            def ffn(n0, b, use, per):
                f = FG * use
                with dve.Fori(0, FG // 2) as i:
                    own.enter(i, per)
                    for j in range(2):
                        lo(n0 + j + 1, i, 2)
                        for x in range(2):
                            e, c = evacuated(2 * (n0 + j) + x)
                            dve.wait_ge(s_ea, lin(c, 4, i))
                            w = [fdw[:, b, v, ds(i * 2 + (j + FG * x), 1)] for v in range(4)]
                            own(V.tensor_scalar(acc[:, x, :], upr[:, j, x, 4:4 + S], w[2], w[3], ALU.mult, ALU.add))
                            own(V.scalar_tensor_tensor(acc[:, x, :], upr[:, j, x, 3:3 + S], w[1], acc[:, x, :], ALU.mult, ALU.add))
                            V.scalar_tensor_tensor(acc[:, x, :], upr[:, j, x, 2:2 + S], w[0], acc[:, x, :], ALU.mult,
                                                   ALU.add).then_inc(s_cva, 1)
                        dve.wait_ge(s_cva, lin(2 * CREDIT + 2 * f + 2 * j + 2, 4, i))
                        dve.wait_ge(s_sil, lin(f + j + 1, 2, i))
                        dve.wait_ge(s_pl, lin(CREDIT + f + j - 1, 2, i))
                        V.tensor_tensor(prod[:, j, :], acc[:, 0, :], acc[:, 1, :], ALU.mult).then_inc(s_pr, 1)
                        dve.wait_ge(s_ph, lin(f + j + 1, 2, i))
                        V.tensor_tensor(actl[:, ds(i * 2 + j, 1), :], prod[:, j, :], acth[:, ds(i * 2 + j, 1), :].bitcast(f32),
                                        ALU.subtract).then_inc(s_pl, 1)
                    own.leave(FG // 2)

            ffn(N_UP, 0, 0, 8)
            with dve.Fori(0, 4) as i:
                for g in range(2):
                    lo(N_DN + 2 * g + 1, i, 4)
                    lo(N_DN + 2 * g + 2, i, 4)
                    gi = 2 * N_DN + 4 * g + 3
                    dve.wait_ge(s_mm, lin(gi + 1, 8, i))
                    h_ = hT[:, ds(i * 2 + g, 1), NM:T]
                    V.tensor_tensor(h_, psP[g][:, 0, :], h_, ALU.add).then_inc(s_ed, 1)

            inverse(3, S)
            for k in range(KT):
                dve.wait_ge(s_sqf, 8 * 3 + 8)
                V.scalar_tensor_tensor(hT[:, k, NM:T], hT[:, k, NM:T], vec[:, V_FIN + k:V_FIN + k + 1], rstd[:, 0:S],
                                       ALU.mult, ALU.mult).then_inc(s_x2, 1)
            norm(4, 3, hT, NM, NM, S, V_PRE)
            ready2 = 16 * (12 + 3)

            def log1p(e, z, z2, p):
                own(V.tensor_scalar(z, e, 2.0, None, ALU.add))
                own(V.reciprocal(z, z))
                own(V.tensor_tensor(z, z, e, ALU.mult))
                own(V.tensor_tensor(z2, z, z, ALU.mult))
                own(V.tensor_scalar(p, z2, 1.0 / 13, None, ALU.mult))
                for c in (11, 9, 7, 5, 3):
                    own(V.scalar_tensor_tensor(p, p, 1.0 / c, z2, ALU.add, ALU.mult))
                own(V.scalar_tensor_tensor(p, p, 1.0, z, ALU.add, ALU.mult))

            def index(t):
                n_ = 128 * (t + 1)
                for h in range(4):
                    dve.wait_ge(s_rl, 4 * t + h + 1)
                    iw = gcol[:, 0, t, h:h + 1]
                    if h == 0:
                        V.tensor_scalar(sc[:, t, 0:n_], rl[:, 0, 0:n_], iw, None, ALU.mult).then_inc(s_ixa, 1)
                    else:
                        dve.wait_ge(s_ixa, 4 * t + h)
                        V.scalar_tensor_tensor(sc[:, t, 0:n_], rl[:, h % 2, 0:n_], iw, sc[:, t, 0:n_], ALU.mult,
                                               ALU.add).then_inc(s_ixa, 1)

            def select(t):
                n_ = 128 * (t + 1)
                dve.wait_ge(s_ixa, 4 * (t + 1))
                if t == 0:
                    own(V.memset(sc[:, 0, 0:128], 0.0))
                    own(V.memset(sc[0:64, 0, 64:128], -BIG))
                    return
                own(V.memset(sc[0:64, t, n_ - 64:n_], -1.0e37))
                for r in range(TOPK // 8):
                    own(V.max(m8[:, r % 2, :], sc[:, t, 0:n_]))
                    own(V.match_replace(sc[:, t, 0:n_], m8[:, r % 2, :], sc[:, t, 0:n_], -3.0e38))
                own(V.tensor_scalar(sc[:, t, 0:n_], sc[:, t, 0:n_], -2.0e38, -BIG, ALU.is_gt, ALU.mult))

            def convolve(g):
                dve.wait_ge(s_ea, evacuated(2 * (n + 2 + g))[1])
                y = xc[:, g, :]
                own(V.tensor_scalar(y, lx[:, g, 0:S], vec[:, V_LCW + g:V_LCW + g + 1], vec[:, V_LCB + g:V_LCB + g + 1],
                                    ALU.mult, ALU.add))
                for k in range(1, 4):
                    w = vec[:, V_LCW + 3 * k + g:V_LCW + 3 * k + g + 1]
                    ins = V.scalar_tensor_tensor(y, lx[:, g, k:k + S], w, y, ALU.mult, ALU.add)
                    if k < 3:
                        own(ins)
                    else:
                        ins.then_inc(s_xc, 1)

            def attend(h):
                for t in range(TT):
                    u_, n_ = TT * h + t, 128 * (t + 1)
                    dve.wait_ge(s_lg, u_ + 1)
                    if u_ >= 2:
                        dve.wait_ge(s_pt, u_ - 1)
                    p = pr[:, u_ % 2, 0:n_]
                    own(V.scalar_tensor_tensor(p, psS[u_ % 4 // 2][:, u_ % 2, 0:n_], 0.125, sc[:, t, 0:n_], ALU.mult, ALU.add))
                    V.tensor_reduce(mx2[:, 0, u_ % 2:u_ % 2 + 1], p, AX, ALU.max, negate=True).then_inc(s_pm, 1)
                    dve.wait_ge(s_pe, u_ + 1)
                    c = mx2[:, 1, u_ % 2:u_ % 2 + 1]
                    own(V.reciprocal(c, c))
                    V.tensor_scalar(p, p, c, None, ALU.mult).then_inc(s_pn, 1)
                if h % 2:
                    dve.wait_ge(s_hc, h // 2 + 1)
                    V.tensor_tensor(cl[:, 6 + h // 2, :], psP[1][:, 1, :], ch[:, 6 + h // 2, :].bitcast(f32),
                                    ALU.subtract).then_inc(s_hcl, 1)

            def mlstm(h):
                dve.wait_ge(s_mb, h + 1)
                V.tensor_tensor(md[:], psS[0][:, 0, :].rearrange("p (t q) -> p t q", t=TT),
                                tri[:].rearrange("p (o q) -> p o q", o=1).to_broadcast([128, TT, 128]), ALU.add).then_inc(s_md, 1)
                dve.wait_ge(s_mw, h + 1)
                for j in range(TT):
                    dve.wait_ge(s_st, 4 * h + j + 1)
                    w = PT[:, j, 128 * j:S]
                    V.tensor_tensor(w, psS[1][:, j % 2, 0:S - 128 * j], w, ALU.mult).then_inc(s_pp, 1)
                dve.wait_ge(s_mo, h + 1)
                o = psP[1][:, 0, 0:97 * TT].rearrange("p (t c) -> p t c", c=97)
                den = st2[:, TT:2 * TT].rearrange("p (t o) -> p t o", o=1)
                neg = st2[:, 0:TT].rearrange("p (t o) -> p t o", o=1)
                own(V.tensor_copy(den, o[:, :, 96:97]))
                own(V.scalar_tensor_tensor(neg, den, -1.0, den, ALU.mult, ALU.max))
                own(V.tensor_tensor(den, neg, gcol[:, 2, :, h:h + 1], ALU.max))
                own(V.reciprocal(den, den))
                V.tensor_tensor(hA[:, :, ML_D * h:ML_D * (h + 1)], o[:, :, 0:96], den.to_broadcast([128, TT, ML_D]),
                                ALU.mult).then_inc(s_mn, 1)

            n = N_IN2
            V.memset(lx[:, :, 0:3], 0.0)
            lam = vec[:, V_LAM:V_LAM + LG]
            V.scalar_tensor_tensor(lcol[:, 0, :], lam, -1.0, lam, ALU.mult, ALU.max).then_inc(s_lb, 1)
            lo(n + 1)
            lo(n + 2)
            dve.wait_ge(s_p2, ready2)
            dve.wait_ge(s_pz, 5)
            dve.wait_ge(s_ea, evacuated(2 * n + 3)[1])
            f_, i_, e_, z_, iw_ = (rows[:, j, :] for j in range(5))
            own(V.tensor_scalar(i_, i_, bif[:, 0:1], None, ALU.add))
            V.scalar_tensor_tensor(e_, f_, -1.0, f_, ALU.mult, ALU.max).then_inc(s_az, 1)
            dve.wait_ge(s_ez, 1)
            dve.wait_ge(s_gt, 1)
            p_ = iw_
            log1p(e_, z_, e_, p_)
            own(V.tensor_scalar(f_, f_, 0.0, None, ALU.min))
            own(V.scalar_tensor_tensor(f_, p_, -2.0, f_, ALU.mult, ALU.add))
            own(V.memset(z_, 1.0))
            own(V.tensor_tensor_scan(p_, z_, f_, 0.0, ALU.mult, ALU.add))
            own(V.tensor_tensor(i_, i_, p_, ALU.subtract))
            own(V.tensor_tensor_scan(e_, i_, i_, 0.0, ALU.max, ALU.max))
            V.tensor_tensor(z_, p_, e_, ALU.add).then_inc(s_mrow, 1)
            dve.wait_ge(s_ez, 2)
            log1p(lcol[:, 1, :], lcol[:, 2, :], lcol[:, 3, :], lcol[:, 4, :])
            own(V.tensor_scalar(lcol[:, 5, :], lam, -1.0, 0.0, ALU.mult, ALU.max))
            own(V.scalar_tensor_tensor(lcol[:, 5, :], lcol[:, 4, :], 2.0, lcol[:, 5, :], ALU.mult, ALU.add))
            V.tensor_scalar(lcol[:, 2, :], lcol[:, 5, :], -RG_C, None, ALU.mult).then_inc(s_lb, 1)
            lo(n + 3)
            dve.wait_ge(s_gc, 1)
            index(0)
            convolve(0)
            lo(n + 4)
            index(1)
            index(2)
            convolve(1)
            lo(n + 5)
            index(3)
            convolve(2)
            select(0)
            select(1)
            lo(n + 6)
            dve.wait_ge(s_la, LG)
            own(V.tensor_tensor(li[:], li[:], xc[:], ALU.mult))
            own(V.tensor_scalar(xc[:], lt[:], -1.0, 1.0, ALU.mult, ALU.add))
            own(V.reciprocal(xc[:], xc[:]))
            V.scalar_tensor_tensor(lt[:], lt[:], -2.0, xc[:], ALU.mult, ALU.mult).then_inc(s_lv, 1)
            lo(n + 7)
            select(2)
            dve.wait_ge(s_lq, 1)
            own(V.tensor_tensor(li[:], li[:], lt[:], ALU.mult))
            for g in range(LG):
                own(V.tensor_tensor_scan(lt[:, g, :], lx[:, g, 3:], li[:, g, :], 0.0, ALU.mult, ALU.add))
                V.tensor_tensor(li[:, g, :], lt[:, g, :], lg[:, g, :], ALU.mult).then_inc(s_hb, 1)
            lo(n + 8)
            for g in range(LG):
                dve.wait_ge(s_hbh, g + 1)
                V.tensor_tensor(cl[:, 3 + g, :], li[:, g, :], ch[:, 3 + g, :].bitcast(f32), ALU.subtract).then_inc(s_hbl, 1)
            dve.wait_ge(s_hbl, LG)
            V.memset(va[:].rearrange("p t (h c) -> p t h c", h=ML_H)[:, :, :, ML_D:], 1.0).then_inc(s_pz2, 1)
            lo(n + 9)
            select(3)
            attend(0)
            lo(n + 10)
            attend(1)
            lo(n + 11)
            attend(2)
            lo(n + 12)
            attend(3)
            lo(n + 13)
            mlstm(0)
            lo(n + 14)
            mlstm(1)
            lo(n + 15)
            mlstm(2)
            mlstm(3)
            dve.wait_ge(s_hs, 1)
            ss = mx2[:, 2:4, :].rearrange("p a b -> p (a b)")
            V.tensor_reduce(ss, PT[:, 0:3, :].rearrange("p a b -> p (a b)").rearrange("p (x d) -> p x d", d=ML_D), AX,
                            ALU.add).then_inc(s_h2, 1)
            dve.wait_ge(s_hrt, 1)
            own(V.reciprocal(ss, ss))
            hx = hA[:].rearrange("p t (h d) -> p (t h) d", d=ML_D)
            own(V.tensor_tensor(hx, hx, ss.rearrange("p (x o) -> p x o", o=1).to_broadcast([128, 16, ML_D]), ALU.mult))
            own(V.tensor_tensor(hA[:], hA[:], mnb[:].rearrange("p (o c) -> p o c", o=1).to_broadcast([128, TT, ML_W]), ALU.mult))
            V.tensor_tensor(hA[:], hA[:], mo[:], ALU.mult).then_inc(s_hg, 1)
            for g in range(LG):
                dve.wait_ge(s_hh, g + 1)
                ps = (psS[0][:, 0, :], psS[0][:, 1, :], psS[1][:, 0, :])[g]
                V.tensor_tensor(cl[:, g, :], ps, ch[:, g, :].bitcast(f32), ALU.subtract).then_inc(s_hl, 1)
            for c in range(4):
                lo(N_WO2 + c + 1)

            def add_normed(use, src, weight, done):
                inverse(use, S)
                for k in range(KT):
                    own(V.scalar_tensor_tensor(src[:, k, :], src[:, k, :], vec[:, weight + k:weight + k + 1], rstd[:, 0:S],
                                               ALU.mult, ALU.mult))
                    V.tensor_tensor(hT[:, k, NM:T], hT[:, k, NM:T], src[:, k, :], ALU.add).then_inc(s_y, 1)

            add_normed(5, mT, V_POST, 0)
            norm(6, 4, hT, NM, NM, S, V_FPRE)
            dve.wait_ge(s_nl, 8 * 5)
            V.memset(upr[:, :, :, 0:4], 0.0).then_inc(s_uz, 1)
            dve.wait_ge(s_uz, 1)
            ffn(N_UP2, 1, 1, 8)
            with dve.Fori(0, 7) as i:
                for j in range(2):
                    lo(N_DN2 + j + 1, i, 2)
            lo(N_DN2 + 15)
            add_normed(7, mT2, V_FPOST, 0)


_INS = ["x", "meta_tokens", "norm_mix_w", "w_in", "lambda_q1", "lambda_k1", "lambda_q2", "lambda_k2", "subln_w",
        "conv_dw_w", "conv_dw_b", "conv_ln_w", "conv_ln_b", "w_conv_out", "w_out", "norm_ffn_w", "w_up", "ffn_dw_w",
        "ffn_dw_b", "w_down", "norm_final_w", "norm_mix_pre_2", "norm_mix_post_2", "norm_ffn_pre_2",
        "norm_ffn_post_2", "w_in_2", "b_igate_2", "b_fgate_2", "mlstm_norm_2", "lru_conv_w_2", "lru_conv_b_2",
        "lru_w_a_2", "lru_b_a_2", "lru_w_x_2", "lru_b_x_2", "lru_lambda_2", "w_out_2", "ffn_up_2", "ffn_conv_w_2",
        "ffn_conv_b_2", "ffn_down_2"]


def kernel(**inputs):
    import numpy as _np
    import concourse.bacc as _bacc
    from concourse import mybir as _mybir
    from concourse.bass_utils import run_bass_kernel_spmd as _run

    nc = _bacc.Bacc("TRN2", target_bir_lowering=False, num_devices=1)
    arrays, args = {}, {}
    for name in _INS:
        a = _np.ascontiguousarray(inputs[name])
        arrays[f"in_{name}_dram"] = a
        args[name] = nc.dram_tensor(f"in_{name}_dram", a.shape, _mybir.dt.from_np(a.dtype), kind="ExternalInput").ap()
    out = nc.dram_tensor("out_0_dram", [1, S, D], _mybir.dt.float32, kind="ExternalOutput").ap()
    program(nc, args, out)
    r = _run(nc, [arrays], core_ids=[0])
    return r.results[0]["out_0_dram"]
```

```python
import math
from contextlib import ExitStack

import concourse.bass as bass
from concourse import mybir

D = 1024
KT = D // 128
S = 512
NM = 16
T = S + NM
HT = T // 2
C3 = NM - 4
T3 = T - C3
H3 = T3 // 2
NH = 8
CK = 31
PAD = CK - 1
DFF = 2816
FG = DFF // 128
KD = FG // 2
TT = S // 128
LAMBDA_INIT = 0.8 - 0.6 * math.exp(-0.3 * 0)
BIG = 1.0e30
CKD = 22
OWN_HEADS = 20 + 2 * CKD

ML_H, ML_D = 4, 96
ML_W = ML_H * ML_D
LRU_W = 384
LG = LRU_W // 128
AT_H, AT_D = 4, 64
AT_W = AT_H * AT_D
TOPK = 128
RG_C = 8.0
O_MQ, O_MK, O_MV, O_MO = 0, 384, 768, 1152
O_MI, O_MF = 1536, 1540
O_LX, O_LG = 1544, 1928
O_AQ, O_AK, O_AV = 2312, 2568, 2824
O_IQ, O_IK, O_IW = 3080, 3336, 3400
D_IN2 = 3404

N_GLU = 0
N_HEAD = N_GLU + 8
N_GC = N_HEAD + 2 * NH
N_CO = N_GC + 4
N_WO = N_CO + 4
N_UP = N_WO + 4
N_DN = N_UP + FG
N_IN2 = N_DN + 16
N_WO2 = N_IN2 + 15
N_UP2 = N_WO2 + 4
N_DN2 = N_UP2 + FG
N_END = N_DN2 + 16

CREDIT = 2

V_MIX, V_CB, V_LNW, V_LNB, V_FFN, V_FIN, V_PRE, V_POST, V_FPRE, V_FPOST = (8 * i for i in range(10))
V_SUB = 80
V_LCB, V_LBA, V_LBX, V_LAM = 81, 84, 87, 90
V_LCW = 93
V_ROWS = 105
V_FP = V_ROWS


def evacuations():
    e = []
    e += ["D", "A"] * 8
    e += ["A"] * (4 * NH)
    e += ["A"] * 8
    e += ["D"] * 8
    e += ["D"] * 8
    e += ["A"] * (2 * FG)
    e += ["-", "-", "-", "D"] * 8
    e += ["A"] * 30
    e += ["A"] * 8
    e += ["A"] * (2 * FG)
    e += ["-", "-", "-", "A"] * 8
    assert len(e) == 2 * N_END
    return e


def program(nc, A, out):
    f32, f32r = mybir.dt.float32, mybir.dt.float32r
    ALU, ACT = mybir.AluOpType, mybir.ActivationFunctionType
    AX = mybir.AxisListType.X
    ds = bass.ds
    EV = evacuations()

    def evacuated(gi):
        return EV[gi], CREDIT + EV[:gi + 1].count(EV[gi])

    def kp(w):
        return w.rearrange("(k p) c -> p k c", p=128)

    w_in, w_up, w_down = A["w_in"][0], A["w_up"][0], A["w_down"][0]
    w_co, w_o = A["w_conv_out"][0], A["w_out"][0]
    w_in2, w_o2, w_up2, w_down2 = A["w_in_2"][0], A["w_out_2"][0], A["ffn_up_2"][0], A["ffn_down_2"][0]

    with ExitStack() as ctx:
        def sem(name):
            return ctx.enter_context(nc.semaphore(name))

        def sb(name, shape, dt=f32):
            return ctx.enter_context(nc.sbuf_tensor(name, shape, dt))

        raw = sb("raw", [128, 2, 2, KT, 128])
        wh = sb("wh", [128, 2, 2, KT, 128], f32r)
        wl = sb("wl", [128, 2, 2, KT, 128], f32r)
        hT = sb("hT", [128, KT, T])
        ident = sb("ident", [128, 128])
        ones = sb("ones", [128, 128])
        vec = sb("vec", [128, V_ROWS + 8])
        cdw = sb("cdw", [128, CK * 8])
        fdw = sb("fdw", [128, 2, 4, 2 * FG])
        eps6 = sb("eps6", [128, 1])
        eps5 = sb("eps5", [128, 1])
        cred = sb("cred", [128, 8])
        bif = sb("bif", [ML_H, 2])
        nlam = sb("nlam", [128, 1])
        tail_base = nc.sbuf_base

        psP = [ctx.enter_context(nc.psum_tensor(f"psP{i}", [128, 2, 512], f32)) for i in range(2)]
        psS = [ctx.enter_context(nc.psum_tensor(f"psS{i}", [128, 2, 512], f32)) for i in range(2)]

        place = [0]

        def at(name, shape, dt=f32, start=None):
            if start is not None:
                place[0] = start
            n = 4
            for d in shape[1:]:
                n *= d
            t = nc.alloc_sbuf_tensor_at(name, shape, dt, offset=place[0])
            place[0] += -(-n // 32) * 32
            assert place[0] <= nc.sbuf_usable_end, (name, place[0] - nc.sbuf_usable_end)
            return t

        x_start = -(-tail_base // 32) * 32
        xh = at("xh", [128, KT, T], f32r, start=x_start)
        xl = at("xl", [128, KT, T], f32r)
        base = place[0]
        xrow = at("xrow", [128, TT, D], start=base)
        mrow = at("mrow", [NM, D])
        vrow = at("vrow", [V_ROWS, 128])
        crow = at("crow", [124, 2, 128])
        frow = at("frow", [2 * FG, 2, 4, 128])
        lamv = at("lamv", [128, 4, 64])
        lamp = at("lamp", [128, 2, 64])
        lams = at("lams", [128, 6])
        conv = at("conv", [128, NH, T3], start=base)
        yT = at("yT", [128, NH, T])
        u_start = place[0]
        u = at("u", [128, NH, PAD + T])
        after_u = place[0]
        qkvg = at("qkvg", [128, 2, 4, T])
        prob_start = place[0]
        PW = [NM + 128 * (t + 1) for t in range(TT)]
        PO = [sum(PW[:t]) for t in range(TT)]
        prob = at("prob", [128, 2, sum(PW)])
        pmeta = at("pmeta", [NM, 2, NM])
        aT = at("aT", [128, TT, S])
        aTm = at("aTm", [NM, S + NM])
        vtok = at("vtok", [128, TT + 1, 128])
        cin = at("cin", [128, PAD + T])
        cwt = at("cwt", [128, CK + 1])
        cacc = at("cacc", [128, T3])
        caccp = at("caccp", [128, T3])
        cmark = at("cmark", [128, 1])
        cprod = at("cprod", [128, 2, T3])
        osq = at("osq", [128, T])
        stat = at("stat", [128, 32])
        mki = at("mki", [128, 128])
        mkk = at("mkk", [128, 64])
        sgl = at("sgl", [128, 2, T], start=prob_start)
        sgc = at("sgc", [128, 8, T3], start=after_u)
        mh = at("mh", [128, KT, T3], f32r)
        ml = at("ml", [128, KT, T3], f32r, start=u_start)
        acth = at("acth", [128, FG, S], f32r, start=base)
        actl = at("actl", [128, FG, S], f32r)
        temp_start = place[0]
        upr = at("upr", [128, 2, 2, T3])
        acc = at("acc", [128, 2, S])
        prod = at("prod", [128, 2, S])
        sq = at("sq", [128, 2, T], start=temp_start)
        nf = at("nf", [128, 2, T])
        rstd = at("rstd", [128, T])
        sacc = at("sacc", [128, 2, T])


        ch = at("ch", [128, KT, S], f32r, start=base)
        cl = at("cl", [128, KT, S], f32r)
        sc = at("sc", [128, TT, S])
        aqk = at("aqk", [128, 4, S])
        av = at("av", [128, TT, AT_W])
        wab = at("wab", [128, 2, LG, 128])
        mnb = at("mnb", [128, ML_W])
        sel = at("sel", [ML_H, ML_H, 128])
        tri = at("tri", [128, 128])
        gcol = at("gcol", [128, 3, TT, 4])
        lcol = at("lcol", [128, 6, LG])
        st2 = at("st2", [128, 2 * TT])
        m8 = at("m8", [128, 2, 8])
        mx2 = at("mx2", [128, 4, 8])
        rows = at("rows", [ML_H, 5, S])
        m_start = place[0]
        lx = at("lx", [128, LG, 3 + S])
        lg = at("lg", [128, LG, S])
        xc = at("xc", [128, LG, S])
        lt = at("lt", [128, LG, S])
        li = at("li", [128, LG, S])
        iq = at("iq", [128, 2, S])
        ik = at("ik", [128, S])
        rl = aqk[:, 0:2, :]
        mqk = at("mqk", [ML_D, 2, 2, S], start=m_start)
        va = at("va", [128, TT, ML_H * (ML_D + 1)])
        mo = at("mo", [128, TT, ML_W])
        hA_start = place[0]
        hA = at("hA", [128, TT, ML_W])
        md = at("md", [128, TT, 128])
        PT = at("PT", [128, TT, S])
        pr = at("pr", [128, 2, S], start=hA_start)
        mT = at("mT", [128, KT, S], start=m_start)
        mT2 = at("mT2", [128, KT, S], start=x_start)
        xo = at("xo", [128, TT, D], start=x_start + 4 * KT * T)
        ALLP = [psP[0], psP[1], psS[0], psS[1]]

        s_xin = sem("tokens_loaded")
        s_in = sem("constants_loaded")
        s_raw = [sem("raw_loaded0"), sem("raw_loaded1")]
        s_hi = sem("hi_split")
        s_lo = sem("lo_split")
        s_mm = sem("half_chunks_multiplied")
        s_ea = sem("emptied_by_act")
        s_ed = sem("emptied_by_dve")
        s_id = sem("constants_set")
        s_ct = sem("constants_transposed")
        s_cc = sem("constants_copied")
        s_xt = sem("input_transposed")
        s_hm = sem("input_copied")
        s_lamo = sem("lambda_sums")
        s_lame = sem("lambda_exps")
        s_sq = sem("squared")
        s_sqf = sem("squares_totalled")
        s_sa = sem("squares_added")
        s_rt = sem("root_taken")
        s_nf = sem("normed")
        s_nh = sem("normed_hi")
        s_nl = sem("normed_lo")
        s_v = sem("dve_own_steps")
        s_a = sem("act_own_steps")
        s_qk = sem("scores_ready")
        s_mx = sem("maxima_ready")
        s_ex = sem("exps_ready")
        s_cb = sem("probs_combined")
        s_at = sem("attention_transposed")
        s_ac = sem("attention_copied")
        s_at_o = sem("head_output_ready")
        s_cf = sem("convolution_fetched")
        s_cst = sem("convolution_stored")
        s_hr = sem("head_roots")
        s_os = sem("head_squared")
        s_oy = sem("head_gated")
        s_ss = sem("head_squares_summed")
        s_sc = sem("head_sum_copied")
        s_cv = sem("convolved")
        s_cp = sem("convolved_by_pool")
        s_g = sem("pool_own_steps")
        s_lm = sem("ln_means")
        s_lc = sem("ln_centred")
        s_ln = sem("ln_normed")
        s_lu = sem("ln_activated")
        s_m = sem("mixed")
        s_mhi = sem("mixed_hi")
        s_ml = sem("mixed_lo")
        s_cva = sem("ffn_convolved")
        s_sil = sem("gate_activated")
        s_pr = sem("gated")
        s_ph = sem("gated_hi")
        s_pl = sem("gated_lo")
        s_out = sem("output_stored")
        s_x2 = sem("final_normed")
        s_n2 = sem("both_norms_means")
        s_pz = sem("pool_zeroed")
        s_pz2 = sem("value_ones_set")
        s_uz = sem("up_borders_cleared")
        s_p2 = sem("second_block_constants")
        s_ga = sem("gate_rows_copied")
        s_az = sem("gate_magnitudes")
        s_ez = sem("gate_exps")
        s_gt = sem("gate_rows_transposed")
        s_gc = sem("gate_columns_copied")
        s_ix = sem("index_products")
        s_rl = sem("index_relus")
        s_ixa = sem("index_accumulated")
        s_xc = sem("lru_convolved")
        s_rg = sem("lru_gates_multiplied")
        s_ri = sem("lru_sigmoids")
        s_la = sem("lru_decays")
        s_lb = sem("lru_decay_columns")
        s_lv = sem("lru_variances")
        s_lq = sem("lru_roots")
        s_hb = sem("lru_outputs")
        s_hbh = sem("lru_hi")
        s_hbl = sem("lru_lo")
        s_lg = sem("attention_logits")
        s_pm = sem("attention_maxima")
        s_pe = sem("attention_exps")
        s_pn = sem("attention_probs")
        s_pt = sem("attention_probs_transposed")
        s_pc = sem("attention_probs_copied")
        s_po = sem("attention_outputs")
        s_hc = sem("attention_hi")
        s_hcl = sem("attention_lo")
        s_mrow = sem("mlstm_rows")
        s_fl = sem("mlstm_floor")
        s_mb = sem("mlstm_maxima_spread")
        s_md = sem("mlstm_diagonals")
        s_mw = sem("mlstm_weights")
        s_st = sem("mlstm_scores")
        s_pp = sem("mlstm_products")
        s_mo = sem("mlstm_outputs")
        s_mn = sem("mlstm_normalised")
        s_hs = sem("mlstm_squares")
        s_h2 = sem("mlstm_sums")
        s_hrt = sem("mlstm_roots")
        s_hg = sem("mlstm_gated")
        s_ht = sem("mlstm_transposed")
        s_hh = sem("mlstm_hi")
        s_hl = sem("mlstm_lo")
        s_w = sem("mixer_output_scaled")
        s_y = sem("residual_added")
        s_ot = sem("output_transposed")
        s_oc = sem("output_copied")
        s_od = sem("output_copied_by_dve")

        def lin(a, b, i):
            return a if i is None else i * b + a

        class Own:

            def __init__(self, eng, s):
                self.eng, self.s, self.n, self.i, self.per = eng, s, 0, None, 0

            def __call__(self, ins):
                ins.then_inc(self.s, 1)
                self.n += 1
                self.eng.wait_ge(self.s, lin(self.n, self.per, self.i))

            def enter(self, i, per):
                self.i, self.per, self.n0 = i, per, self.n

            def leave(self, turns):
                assert self.n - self.n0 == self.per, ("steps in the loop", self.n - self.n0)
                self.n = self.n0 + self.per * turns
                self.i = None

        def span(t, g, c0, n):
            if isinstance(g, int):
                return t[:, g, c0:c0 + 2 * n].rearrange("p (a b) -> p a b", a=2)
            return t[:, ds(g, 1), c0:c0 + 2 * n].rearrange("p o (a b) -> p (o a) b", a=2)

        block = ctx.enter_context(nc.Block())

        @block.sync
        def _(sp):
            def load(n, i, st, srcs, dsts):
                if n >= 2:
                    sp.wait_ge(s_lo, lin(n - 1, st, i))
                for dst, src in zip(dsts, srcs):
                    sp.dma_start(dst, src).then_inc(s_raw[n % 2], 16)

            def pair(w, n, i, st, ca, cb):
                s = n % 2
                load(n, i, st, [kp(w)[:, :, ds(ca, 128)], kp(w)[:, :, ds(cb, 128)]],
                     [raw[:, s, 0], raw[:, s, 1]])

            def wide(w, n, turns, col=0):
                with sp.Fori(0, turns) as i:
                    for j in range(2):
                        c = i * 512 + (col + 256 * j)
                        pair(w, n + j, i, 2, c, c + 128)

            def up(w, n):
                with sp.Fori(0, FG // 2) as i:
                    for j in range(2):
                        c = i * 256 + 128 * j
                        pair(w, n + j, i, 2, c, c + DFF)

            def down(w, n):
                rows = w.rearrange("(j k p) c -> j p k c", p=128, k=KD)
                with sp.Fori(0, 8) as i:
                    for j in range(2):
                        s = (n + j) % 2
                        flat = raw[:, s].rearrange("p a k c -> p (a k) c")
                        src = rows[j][:, :, ds(i * 128, 128)]
                        load(n + j, i, 2, [src[:, 0:6], src[:, 6:KD]], [flat[:, 0:6], flat[:, 6:KD]])

            def inputs():
                for v, name in ((V_MIX, "norm_mix_w"), (V_CB, "conv_dw_b"), (V_LNW, "conv_ln_w"), (V_LNB, "conv_ln_b"),
                                (V_FFN, "norm_ffn_w"), (V_PRE, "norm_mix_pre_2"), (V_POST, "norm_mix_post_2"),
                                (V_FPRE, "norm_ffn_pre_2"), (V_FPOST, "norm_ffn_post_2"), (V_SUB, "subln_w"),
                                (V_LCB, "lru_conv_b_2"), (V_LBA, "lru_b_a_2"), (V_LBX, "lru_b_x_2"),
                                (V_LAM, "lru_lambda_2")):
                    a = A[name][0].rearrange("(g p) -> g p", p=128)
                    sp.dma_start(vrow[v:v + a.shape[0], :], a).then_inc(s_in, 16)
                sp.dma_start(vrow[V_FIN:V_FIN + 8, :], A["norm_final_w"].rearrange("(g p) -> g p", p=128)).then_inc(s_in, 16)
                sp.dma_start(vrow[V_LCW:V_LCW + 12, :],
                               A["lru_conv_w_2"][0].rearrange("k (g p) -> (k g) p", p=128)).then_inc(s_in, 16)
                cw = A["conv_dw_w"][0].rearrange("k (g p) -> (k g) p", p=128)
                for j in range(2):
                    sp.dma_start(crow[:, j, :], cw[124 * j:124 * (j + 1), :]).then_inc(s_in, 16)
                for b, (w, bias) in enumerate((("ffn_dw_w", "ffn_dw_b"), ("ffn_conv_w_2", "ffn_conv_b_2"))):
                    sp.dma_start(frow[:, b, 0:3, :], A[w][0].rearrange("k (g p) -> g k p", p=128)).then_inc(s_in, 16)
                    sp.dma_start(frow[:, b, 3, :], A[bias][0].rearrange("(g p) -> g p", p=128)).then_inc(s_in, 16)
                for j, name in enumerate(("b_igate_2", "b_fgate_2")):
                    sp.dma_start(bif[:, j:j + 1], A[name].rearrange("a h -> h a")).then_inc(s_in, 16)
                for j, name in enumerate(("lambda_q1", "lambda_k1", "lambda_q2", "lambda_k2")):
                    sp.dma_start(lamv[:, j, :], A[name].to_broadcast([128, 64])).then_inc(s_in, 16)

            x = A["x"][0]
            sp.dma_start(mrow[:], A["meta_tokens"]).then_inc(s_xin, 16)
            for t in range(TT):
                sp.dma_start(xrow[:, t, :], x[128 * t:128 * (t + 1), :]).then_inc(s_xin, 16)
            G = 3 * D
            pair(w_in, 0, None, 0, G, G + D)
            inputs()
            pair(w_in, 1, None, 0, G + 128, G + D + 128)
            with sp.Fori(0, 3) as i:
                for j in range(2):
                    c = i * 256 + (G + 128 * (2 + j))
                    pair(w_in, 2 + j, i, 2, c, c + D)
            with sp.Fori(0, NH) as h:
                c = h * 128
                pair(w_in, N_HEAD, h, 2, c, c + D)
                pair(w_in, N_HEAD + 1, h, 2, c + 2 * D, c + 5 * D)
            wide(w_in, N_GC, 2, 6 * D)
            wide(w_co, N_CO, 2)
            wide(w_o, N_WO, 2)
            up(w_up, N_UP)
            down(w_down, N_DN)

            W2 = kp(w_in2)

            def parts(n, srcs, dsts):
                load(n, None, 0, srcs, dsts)

            def two(n, ca, cb, width=128):
                s = n % 2
                parts(n, [W2[:, :, ca:ca + width], W2[:, :, cb:cb + width]],
                      [raw[:, s, 0, :, 0:width], raw[:, s, 1, :, 0:width]])

            n = N_IN2
            two(n, O_IQ, O_IQ + 128)
            s = (n + 1) % 2
            parts(n + 1, [W2[:, :, O_IK:O_IK + 64], W2[:, :, O_IK:O_IK + 64], W2[:, :, O_MF:O_MF + 4],
                          W2[:, :, O_MI:O_MI + 4], W2[:, :, O_IW:O_IW + 4]],
                  [raw[:, s, 0, :, 0:64], raw[:, s, 0, :, 64:128], raw[:, s, 1, :, 0:4], raw[:, s, 1, :, 32:36],
                   raw[:, s, 1, :, 64:68]])
            for g in range(LG):
                two(n + 2 + g, O_LX + 128 * g, O_LG + 128 * g)
            two(n + 5, O_AQ, O_AQ + 128)
            two(n + 6, O_AK, O_AK + 128)
            two(n + 7, O_AV, O_AV + 128)
            for c in range(3):
                two(n + 8 + c, O_MV + 256 * c, O_MV + 256 * c + 128)
            for h in range(ML_H):
                two(n + 11 + h, O_MQ + ML_D * h, O_MK + ML_D * h, ML_D)
            wide(w_o2, N_WO2, 2)
            up(w_up2, N_UP2)
            down(w_down2, N_DN2)
            for half in range(2):
                for t in range(TT):
                    if half and t >= 2:
                        sp.wait_ge(s_od, t - 1)
                    else:
                        sp.wait_ge(s_oc, TT * half + t + 1)
                    c = slice(512 * half, 512 * (half + 1))
                    sp.dma_start(out[0, 128 * t:128 * (t + 1), c], xo[:, t, c]).then_inc(s_out, 16)
            sp.wait_ge(s_out, 16 * 2 * TT)

        @block.gpsimd
        def _(pool):
            pool.memset(ident[:], 0.0).then_inc(s_id, 1)
            pool.wait_ge(s_id, 1)
            pool.affine_select(out=ident[:], in_=ident[:], compare_op=ALU.not_equal, fill=1.0, base=0,
                               pattern=[[-1, 128]], channel_multiplier=1).then_inc(s_id, 1)
            pool.memset(ones[:], 1.0).then_inc(s_id, 1)
            pool.memset(eps6[:], 1e-6).then_inc(s_id, 1)
            pool.memset(eps5[:], 1e-5).then_inc(s_id, 1)
            per = 2 * (CK - CKD) - 2
            with pool.Fori(0, NH) as h:
                pool.wait_ge(s_cf, h + 1)
                pool.tensor_tensor(cmark[:], cwt[:, 0:1], cwt[:, 1:2], ALU.add)
                for k in range(CKD, CK):
                    w, src = cwt[:, k:k + 1], cin[:, C3 + k:C3 + k + T3]
                    j = k - CKD
                    dst = cprod[:, j % 2, :] if j else caccp[:]
                    pool.tensor_scalar(dst, src, w, None, ALU.mult).then_inc(s_g, 1)
                    if j:
                        pool.wait_ge(s_g, lin(2 * j, per, h))
                        pool.tensor_tensor(caccp[:], caccp[:], dst, ALU.add).then_inc(s_cp if k == CK - 1 else s_g, 1)

            pool.wait_ge(s_x2, KT)
            pool.memset(wab[:], 0.0).then_inc(s_pz, 1)
            pool.memset(sel[:], 0.0).then_inc(s_pz, 1)
            pool.memset(tri[:], 0.0).then_inc(s_pz, 1)
            pool.wait_ge(s_pz, 3)
            pool.affine_select(out=sel[:], in_=sel[:], compare_op=ALU.not_equal, fill=1.0, base=0,
                               pattern=[[-1, ML_H], [0, 128]], channel_multiplier=1).then_inc(s_pz, 1)
            pool.affine_select(out=tri[:], in_=tri[:], compare_op=ALU.is_ge, fill=BIG, base=0,
                               pattern=[[1, 128]], channel_multiplier=-1).then_inc(s_pz, 1)
            for j, name in enumerate(("lru_w_a_2", "lru_w_x_2")):
                w = A[name][0]
                for b in range(2 * LG):
                    r = 64 * (b % 2)
                    pool.dma_start(wab[r:r + 64, j, b // 2, r:r + 64], w[b]).then_inc(s_p2, 16)
            pool.dma_start(mnb[:], A["mlstm_norm_2"].to_broadcast([128, ML_W])).then_inc(s_p2, 16)

        N_IN = 16 * (2 + 14 + 2 + 2 + 4 + 4)

        @block.tensor
        def _(pe):
            mm, tr = nc.tensor.matmul, nc.tensor.transpose

            def all_free(gi):
                pe.wait_ge(s_ea, CREDIT + EV[:gi + 1].count("A"))
                pe.wait_ge(s_ed, CREDIT + EV[:gi + 1].count("D"))

            def project(ps, n, half, X, c0, nn, slots, i=None, st=0, rows=128, banks=2):
                if half == 0:
                    pe.wait_ge(s_lo, lin(n + 1, st, i))
                gi = 2 * n + half
                if slots and i is None:
                    e, c = evacuated(gi - slots)
                    if e != "-":
                        pe.wait_ge(s_ea if e == "A" else s_ed, c)
                elif slots:
                    e, c1 = evacuated(gi + 2 * st - slots)
                    first = gi - gi % 2
                    per = EV[first:first + 2 * st].count(e)
                    pe.wait_ge(s_ea if e == "A" else s_ed, lin(c1 - per, per, i))
                s = n % 2
                for k in range(KT):
                    for p, (W, Y) in enumerate(((wh, X[0]), (wh, X[1]), (wl, X[0]))):
                        for a in range(banks):
                            ins = mm(ps[0:rows, a, 0:nn], W[:, s, half, k, 0:rows], Y[:, k, c0 + a * nn:c0 + (a + 1) * nn],
                                     start=(k == 0 and p == 0), stop=(k == KT - 1 and p == 2))
                ins.then_inc(s_mm, 1)

            def project_pair(pss, n, X, c0, nn, slots, ready=None, i=None, st=0, banks=2, rows=(128, 128)):
                pe.wait_ge(s_lo, lin(n + 1, st, i))
                if slots:
                    e, c1 = evacuated(2 * n + 1 + 2 * st - slots)
                    per = EV[2 * n:2 * n + 2 * st].count(e)
                    pe.wait_ge(s_ea if e == "A" else s_ed, lin(c1 - per, per, i))
                s = n % 2
                for k in range(KT):
                    if ready:
                        pe.wait_ge(ready[0], ready[1] + k + 1)
                    for half, ps in enumerate(pss):
                        r = rows[half]
                        for p, (W, Y) in enumerate(((wh, X[0]), (wh, X[1]), (wl, X[0]))):
                            for a in range(banks):
                                ins = mm(ps[0:r, a, 0:nn], W[:, s, half, k, 0:r], Y[:, k, c0 + a * nn:c0 + (a + 1) * nn],
                                         start=(k == 0 and p == 0), stop=(k == KT - 1 and p == 2))
                        if k == KT - 1:
                            ins.then_inc(s_mm, 1)

            def wide(n0, X, c0, nn, slots, turns=2, banks=2, ready=None):
                def turn(i, st):
                    for j in range(2):
                        if ready and j == 0:
                            project_pair(ALLP[0:2], n0, X, c0, nn, slots, ready, i, st, banks)
                            continue
                        for half in range(2):
                            project(ALLP[(2 * j + half) % slots], n0 + j, half, X, c0, nn, slots, i, st, banks=banks)

                all_free(2 * n0 - 1)
                if turns == 1:
                    turn(None, 0)
                else:
                    with pe.Fori(0, turns) as i:
                        turn(i, 2)

            def down(n0, split):
                all_free(2 * n0 - 1)
                e = EV[2 * n0 + 3]
                before = CREDIT + EV[:2 * n0].count(e)
                with pe.Fori(0, 4) as i:
                    for g in range(2):
                        ps = psP[g]
                        for j in range(2):
                            n = n0 + 2 * g + j
                            pe.wait_ge(s_lo, lin(n + 1, 4, i))
                            if j == 0:
                                pe.wait_ge(s_ed if e == "D" else s_ea, lin(before + g - 1, 2, i))
                            s = n % 2
                            fh = wh[:, s].rearrange("p a k c -> p (a k) c")
                            fl = wl[:, s].rearrange("p a k c -> p (a k) c")
                            for k in range(KD):
                                kk = j * KD + k
                                for p, (W, Y) in enumerate(((fh, acth), (fh, actl), (fl, acth))):
                                    if p == 0:
                                        pe.wait_ge(s_pl, split + kk + 1)
                                    ins = mm(ps[:, 0, :], W[:, k, :], Y[:, kk, :], start=(kk == 0 and p == 0),
                                             stop=(kk == FG - 1 and p == 2))
                            ins.then_inc(s_mm, 2)

            def total(use, ps, nn, after, which=0):
                pe.wait_ge(s_sa, after)
                for a in range(2):
                    ins = mm(ps[:, a, 0:nn], ones[:], sacc[:, which, a * nn:(a + 1) * nn], start=True, stop=True)
                ins.then_inc(s_sqf, 1)

            def accumulate(m, ps, nn, k):
                pe.wait_ge(s_sq, m + 1)
                for a in range(2):
                    ins = mm(ps[:, a, 0:nn], ones[:], sq[:, m % 2, a * nn:(a + 1) * nn], start=(k == 0), stop=(k == KT - 1))
                ins.then_inc(s_sa, 1)

            pe.wait_ge(s_id, 3)
            pe.wait_ge(s_xin, 16 * (TT + 1))
            for k in range(KT + 2):
                if k < KT:
                    ps = ALLP[1 + k % 3]
                    if k >= 3:
                        pe.wait_ge(s_hm, k - 2)
                    for t in range(TT):
                        tr(ps[:, 0, 128 * t:128 * (t + 1)], xrow[:, t, 128 * k:128 * (k + 1)], ident[:])
                    tr(ps[:, 1, 0:NM], mrow[:, 128 * k:128 * (k + 1)], ident[0:NM, 0:NM]).then_inc(s_xt, 1)
                if k >= 2:
                    accumulate(k - 2, psP[0], HT, k - 2)
            pe.wait_ge(s_in, N_IN)
            tr(psS[0][:, 0, 0:V_ROWS], vrow[:], ident[0:V_ROWS, 0:V_ROWS])
            for j in range(2):
                tr(psS[0][:, 0, 128 + 124 * j:252 + 124 * j], crow[:, j, :], ident[0:124, 0:124])
            for b in range(2):
                for v in range(4):
                    o = (4 * b + v) * 2 * FG
                    ins = tr(psS[0][:, 1, o:o + 2 * FG], frow[:, b, v, :], ident[0:2 * FG, 0:2 * FG])
            ins.then_inc(s_ct, 1)
            pe.wait_ge(s_rt, 1)
            X = (xh, xl)
            project_pair(ALLP[0:2], 0, X, 0, HT, None, (s_nl, 0))
            pe.wait_ge(s_cc, 2)
            for half in range(2):
                project(ALLP[2 + half], 1, half, X, 0, HT, None)
            with pe.Fori(0, 3) as i:
                for j in range(2):
                    for half in range(2):
                        project(ALLP[2 * j + half], 2 + j, half, X, 0, HT, 4, i, 2)

            def scores(r, t, h, i):
                if t < 2:
                    pe.wait_ge(s_ex, lin(4 + 4 * h, 8, i))
                    if t == 0:
                        pe.wait_ge(s_sc, lin(1 + h, 2, i))
                elif t == 2:
                    pe.wait_ge(s_ex, lin(4 + 4 * h + 1, 8, i))
                else:
                    pe.wait_ge(s_ex, lin(4 + 4 * h + 3, 8, i))
                for m in range(2):
                    P = slice(64 * m, 64 * m + 64)
                    q = qkvg[P, r, 0, NM + 128 * t:NM + 128 * (t + 1)]
                    K = qkvg[P, r, 1, :]
                    if t < 3:
                        b = t % 2
                        mm(psS[m][:, b, 0:PW[t]], q, K[:, 0:PW[t]], start=True, stop=False)
                        last = psS[m][:, b, PW[t] - 64:PW[t]]
                    else:
                        mm(psS[m][:, 0, 0:HT], q, K[:, 0:HT], start=True, stop=True)
                        mm(psS[m][:, 1, 0:HT], q, K[:, HT:T], start=True, stop=False)
                        last = psS[m][:, 1, HT - 64:HT]
                    ins = mm(last, mki[P, :], mkk[P, :], start=False, stop=True)
                    if t == 0:
                        ins = mm(psS[m][0:NM, 0, PW[0]:PW[0] + NM], qkvg[P, r, 0, 0:NM], K[:, 0:NM], start=True, stop=True)
                ins.then_inc(s_qk, 1)

            def values(r, h, i):
                pe.wait_ge(s_os, lin(1 + h, 2, i))
                pe.wait_ge(s_oy, lin(1 + h, 2, i))
                for j in range(TT):
                    tr(psP[1][:, 0, 128 * j:128 * (j + 1)], qkvg[:, r, 2, NM + 128 * j:NM + 128 * (j + 1)], ident[:])
                tr(psP[1][0:NM, 1, 0:128], qkvg[:, r, 2, 0:NM], ident[:]).then_inc(s_at, 1)

            def probs(t, h, i):
                pe.wait_ge(s_cb, lin(4 * h + t + 1, 8, i))
                pe.wait_ge(s_ac, lin(5 * h + t + 1, 10, i))
                for j in range(t + 1):
                    o = PO[t] + NM + 128 * j
                    tr(psP[1][:, 0, 128 * j:128 * (j + 1)], prob[:, 0, o:o + 128], ident[:])
                ins = tr(psP[1][0:NM, 1, 0:128], prob[:, 0, PO[t]:PO[t] + NM], ident[:])
                if t == 0:
                    ins = tr(psP[1][0:NM, 1, 128:128 + NM], pmeta[:, 0, :], ident[0:NM, 0:NM])
                ins.then_inc(s_at, 1)

            def outputs(h, i):
                pe.wait_ge(s_ac, lin(5 * h + 5, 10, i))
                mm(psP[1][:, 0, :], vtok[0:NM, TT, :], aTm[:, 0:S], start=True, stop=False)
                for j in range(TT):
                    mm(psP[1][:, 0, 128 * j:S], vtok[:, j, :], aT[:, j, 128 * j:S], start=False, stop=(j == TT - 1))
                mm(psP[1][:, 1, 0:NM], vtok[0:NM, TT, :], aTm[:, S:S + NM], start=True, stop=True).then_inc(s_at_o, 1)
                pe.wait_ge(s_os, lin(1 + h + 1, 2, i))
                for a in range(2):
                    ins = mm(psS[0][:, a, 0:HT], ones[:], osq[:, a * HT:(a + 1) * HT], start=True, stop=True)
                ins.then_inc(s_ss, 1)

            def step(h, r, i, project_it=True, attend=True):
                n, p = N_HEAD + 2 * h, 1 - r
                a = h - 1
                if attend:
                    scores(p, 0, a, i)
                    scores(p, 1, a, i)
                if project_it:
                    project(psP[0], n, 0, X, 0, HT, 1, i, 4)
                if attend:
                    values(p, a, i)
                    probs(0, a, i)
                    scores(p, 2, a, i)
                if project_it:
                    project(psP[0], n, 1, X, 0, HT, 1, i, 4)
                if attend:
                    probs(1, a, i)
                    scores(p, 3, a, i)
                if project_it:
                    project(psP[0], n + 1, 0, X, 0, HT, 1, i, 4)
                if attend:
                    probs(2, a, i)
                if project_it:
                    project(psP[0], n + 1, 1, X, 0, HT, 1, i, 4)
                if attend:
                    probs(3, a, i)
                    outputs(a, i)

            all_free(2 * N_HEAD - 1)
            step(0, 0, None, attend=False)
            with pe.Fori(0, 3) as i:
                step(1, 1, i)
                step(2, 0, i)
            step(7, 1, None)
            step(8, 0, None, project_it=False)
            pe.wait_ge(s_sc, 1 + NH)
            pe.wait_ge(s_oy, 1 + NH)
            pe.wait_ge(s_cst, NH)
            for g in range(NH):
                for a in range(2):
                    ins = mm(psS[0][:, a, 0:H3], ones[:], conv[:, g, a * H3:(a + 1) * H3], start=(g == 0), stop=(g == NH - 1))
            ins.then_inc(s_lm, 1)
            wide(N_GC, X, C3, H3, 2, turns=1)
            total(1, psS[1], H3, 16)
            wide(N_GC + 2, X, C3, H3, 2, turns=1)
            pe.wait_ge(s_rt, 2)
            wide(N_CO, X, C3, H3, 4, ready=(s_nl, 8))
            wide(N_WO, (mh, ml), 0, H3, 4, ready=(s_ml, 0))
            all_free(2 * N_UP - 1)
            total(2, psP[0], H3, 24)
            pe.wait_ge(s_rt, 3)
            wide(N_UP, X, C3, H3, 4, turns=FG // 2, ready=(s_nl, 16))
            down(N_DN, CREDIT)

            all_free(2 * N_IN2 - 1)
            total(3, psS[0], S // 2, 40)
            total(4, psS[1], S // 2, 40, 1)
            ready2 = 16 * (12 + 1)

            def slot(gi):
                return psP[0][:, gi % 2, :]

            def project2(n, rows=(128, 128)):
                for half in range(2):
                    gi = 2 * n + half
                    ps = psP[0][:, gi % 2:gi % 2 + 1, :]
                    project(ps, n, half, X, NM, S, 2, rows=rows[half], banks=1)

            def project_tokens(n):
                for half in range(2):
                    gi = 2 * n + half
                    if half == 0:
                        pe.wait_ge(s_lo, n + 1)
                    e, c = evacuated(gi - 2)
                    pe.wait_ge(s_ea, c)
                    for a in range(2):
                        o = NM + 128 * (2 * half + a)
                        for k in range(KT):
                            for p, (Y, W) in enumerate(((xh, wh), (xl, wh), (xh, wl))):
                                ins = mm(psP[0][:, gi % 2, 256 * a:256 * (a + 1)], Y[:, k, o:o + 128], W[:, n % 2, :, k, :],
                                         start=(k == 0 and p == 0), stop=(k == KT - 1 and p == 2))
                    ins.then_inc(s_mm, 1)

            def index(t):
                if t:
                    pe.wait_ge(s_rl, 4 * t)
                n_ = 128 * (t + 1)
                for h in range(4):
                    P = slice(64 * (h % 2), 64 * (h % 2) + 64)
                    mm(psS[h // 2][:, h % 2, 0:n_], iq[P, h // 2, 128 * t:n_], ik[P, 0:n_], start=True, stop=True).then_inc(s_ix, 1)

            def lru_gates(g):
                pe.wait_ge(s_xc, g + 1)
                if g:
                    pe.wait_ge(s_ri, g)
                mm(psP[1][:, 0, :], wab[:, 0, g, :], xc[:, g, :], start=True, stop=True)
                mm(psP[1][:, 1, :], wab[:, 1, g, :], xc[:, g, :], start=True, stop=True).then_inc(s_rg, 1)

            def columns(src, j, count):
                for t in range(TT):
                    ins = tr(psP[1][:, 0, 16 * j + 4 * t:16 * j + 4 * t + 4], src[:, 128 * t:128 * (t + 1)], ident[0:4, 0:4])
                ins.then_inc(s_gt, 1)

            def logits(h, t):
                u_ = TT * h + t
                n_ = 128 * (t + 1)
                if u_ >= 4:
                    pe.wait_ge(s_pn, u_ - 3)
                P = slice(64 * (h % 2), 64 * (h % 2) + 64)
                mm(psS[u_ % 4 // 2][:, u_ % 2, 0:n_], aqk[P, h // 2, 128 * t:n_], aqk[P, 2 + h // 2, 0:n_], start=True,
                   stop=True).then_inc(s_lg, 1)

            def attend(h):
                for t in range(TT):
                    u_ = TT * h + t
                    pe.wait_ge(s_pn, u_ + 1)
                    if u_:
                        pe.wait_ge(s_pc, u_)
                    for j in range(t + 1):
                        ins = tr(psP[1][:, 0, 128 * j:128 * (j + 1)], pr[:, u_ % 2, 128 * j:128 * (j + 1)], ident[:])
                    ins.then_inc(s_pt, 1)
                pe.wait_ge(s_pc, TT * (h + 1))
                if h == 2:
                    pe.wait_ge(s_hcl, 1)
                r = 64 * (h % 2)
                for j in range(TT):
                    ins = mm(psP[1][r:r + 64, 1, 128 * j:S], av[:, j, 64 * h:64 * (h + 1)], PT[:, j, 128 * j:S], start=(j == 0),
                             stop=(j == TT - 1))
                ins.then_inc(s_po, 1)

            def mlstm(h):
                r = h % 2
                if h:
                    pe.wait_ge(s_mw, h)
                mm(psS[0][:, 0, :], sel[:, h, :], rows[:, 2, :], start=True, stop=True).then_inc(s_mb, 1)
                for j in range(TT):
                    if 4 * h + j >= 2:
                        pe.wait_ge(s_pp, 4 * h + j - 1)
                    mm(psS[1][:, j % 2, 0:S - 128 * j], mqk[:, r, 1, 128 * j:128 * (j + 1)], mqk[:, r, 0, 128 * j:S], start=True,
                       stop=True).then_inc(s_st, 1)
                pe.wait_ge(s_pp, 4 * h + 4)
                if h:
                    pe.wait_ge(s_mn, h)
                for t in range(TT):
                    for j in range(t + 1):
                        o = 97 * t
                        ins = mm(psP[1][:, 0, o:o + 97], PT[:, j, 128 * t:128 * (t + 1)], va[:, j, 97 * h:97 * (h + 1)],
                                 start=(j == 0), stop=(j == t))
                ins.then_inc(s_mo, 1)

            n = N_IN2
            project_pair((psP[0][:, 0:1, :], psP[0][:, 1:2, :]), n, X, NM, S, None, (s_nl, 24), banks=1)
            pe.wait_ge(s_rt, 5)
            project2(n + 1, (128, 96))
            pe.wait_ge(s_ga, 1)
            columns(rows[:, 4, :], 0, 1)
            pe.wait_ge(s_gc, 1)
            index(0)
            index(1)
            project2(n + 2)
            index(2)
            project2(n + 3)
            index(3)
            project2(n + 4)
            pe.wait_ge(s_p2, ready2)
            pe.wait_ge(s_pz, 5)
            lru_gates(0)
            project2(n + 5)
            lru_gates(1)
            lru_gates(2)
            pe.wait_ge(s_mrow, 1)
            pe.wait_ge(s_ri, 3)
            columns(rows[:, 1, :], 1, 2)
            pe.wait_ge(s_fl, 1)
            pe.wait_ge(s_gc, 2)
            columns(rows[:, 3, :], 2, 3)
            project2(n + 6)
            project_tokens(n + 7)
            pe.wait_ge(s_ea, evacuated(2 * (n + 7) + 1)[1])
            pe.wait_ge(s_rl, 16)
            pe.wait_ge(s_gc, 3)
            project_tokens(n + 8)
            project_tokens(n + 9)
            project_tokens(n + 10)
            for u_ in range(4):
                logits(0, u_)
            for h in range(3):
                attend(h)
                for t in range(TT):
                    logits(h + 1, t)
                if h < 2:
                    project2(n + 11 + h, (ML_D, ML_D))
            attend(3)
            pe.wait_ge(s_pn, 16)
            pe.wait_ge(s_hcl, 2)
            mlstm(0)
            project2(n + 13, (ML_D, ML_D))
            mlstm(1)
            project2(n + 14, (ML_D, ML_D))
            mlstm(2)
            mlstm(3)
            def first_out(groups, first, last):
                for k in groups:
                    for half in range(2):
                        for p, (W, Y) in enumerate(((wh, ch), (wh, cl), (wl, ch))):
                            ins = mm(psP[half][:, 0, :], W[:, N_WO2 % 2, half, k, :], Y[:, k, :],
                                     start=(k == first and p == 0), stop=(k == last and p == 2))
                        if k == last:
                            ins.then_inc(s_mm, 1)

            all_free(2 * N_WO2 - 1)
            pe.wait_ge(s_mn, ML_H)
            pe.wait_ge(s_lo, N_WO2 + 1)
            pe.wait_ge(s_hbl, 3)
            pe.wait_ge(s_hcl, 2)
            first_out(range(LG, KT), LG, LG - 1)
            pe.wait_ge(s_hg, 1)
            pe.wait_ge(s_pp, 16)
            pe.wait_ge(s_mw, 4)
            for g in range(LG):
                ps = (psS[0][:, 0, :], psS[0][:, 1, :], psS[1][:, 0, :])[g]
                for t in range(TT):
                    ins = tr(ps[:, 128 * t:128 * (t + 1)], hA[:, t, 128 * g:128 * (g + 1)], ident[:])
                ins.then_inc(s_ht, 1)
            pe.wait_ge(s_hl, 3)
            first_out(range(LG), LG, LG - 1)
            for c in range(1, 4):
                for half in range(2):
                    project(ALLP[half], N_WO2 + c, half, (ch, cl), 0, S, 2, banks=1)
            total(5, psS[0], S // 2, 48)
            for k in range(KT):
                accumulate(48 + k, psS[1], S // 2, k)
            pe.wait_ge(s_rt, 7)
            wide(N_UP2, X, NM, S, 4, turns=FG // 2, banks=1, ready=(s_nl, 32))
            down(N_DN2, CREDIT + FG)
            all_free(2 * N_END - 1)
            total(7, psS[0], S // 2, 64)
            pe.wait_ge(s_rt, 8)
            for k in range(KT):
                pe.wait_ge(s_y, 8 + k + 1)
                for t in range(TT):
                    ins = tr(ALLP[t][:, k // 4, 128 * (k % 4):128 * (k % 4 + 1)], hT[:, k, NM + 128 * t:NM + 128 * (t + 1)], ident[:])
                ins.then_inc(s_ot, 1)

        @block.scalar
        def _(act):
            fn = nc.scalar.activation
            own = Own(act, s_a)

            def hi(n, i=None, st=0):
                more = 48 if n >= N_IN2 + 1 and (n - N_IN2) % 2 else 0
                act.wait_ge(s_raw[n % 2], lin(32 * (n // 2 + 1) + more, 16 * st, i))
                if n >= 2:
                    act.wait_ge(s_mm, lin(2 * (n - 1), 2 * st, i))
                fn(wh[:, n % 2], raw[:, n % 2], ACT.Copy).then_inc(s_hi, 1)

            def square(m, src, n, i=None, st=0, scale=1.0):
                if m >= 2:
                    act.wait_ge(s_sa, lin(m - 1, st, i))
                fn(sq[:, m % 2, 0:n], src, ACT.Square, scale=scale).then_inc(s_sq, 1)

            def root(use, ps, nn, eps):
                if use in (0, 6):
                    act.wait_ge(s_sa, 8 * (use + 1))
                else:
                    act.wait_ge(s_sqf, use if use < 7 else 6)
                fn(rstd[:, 0:2 * nn].rearrange("p (a b) -> p a b", a=2), ps[:, :, 0:nn], ACT.Sqrt,
                   bias=eps[:], scale=1.0 / D).then_inc(s_rt, 1)

            def normed_hi(nf_use, c0, n):
                for k in range(KT):
                    act.wait_ge(s_nf, 8 * nf_use + k + 1)
                    fn(xh[:, k, c0:c0 + n], nf[:, k % 2, 0:n], ACT.Copy).then_inc(s_nh, 1)

            act.wait_ge(s_id, 5)
            for k in range(KT):
                act.wait_ge(s_hm, k + 1)
                square(k, hT[:, k, :], T)
            hi(0)
            root(0, psP[0], HT, eps6)
            act.wait_ge(s_ct, 1)
            fn(vec[:, 0:V_ROWS], psS[0][:, 0, 0:V_ROWS], ACT.Copy)
            fn(cdw[:], psS[0][:, 0, 128:128 + CK * 8], ACT.Copy).then_inc(s_cc, 1)
            normed_hi(0, 0, T)
            act.wait_ge(s_lamo, 1)
            fn(lams[:, 2:4], lams[:, 0:2], ACT.Exp).then_inc(s_lame, 1)

            def glu_gate(n, i, st):
                hi(n + 1, i, st)
                act.wait_ge(s_mm, lin(2 * n + 2, 2 * st, i))
                act.wait_ge(s_ed, lin(CREDIT + n - 1, st, i))
                fn(sgl[:, n % 2, :].rearrange("p (a b) -> p a b", a=2), ALLP[(2 * n + 1) % 4][:, :, 0:HT],
                   ACT.Sigmoid).then_inc(s_ea, 1)

            glu_gate(0, None, 0)
            glu_gate(1, None, 0)
            with act.Fori(0, 3) as i:
                glu_gate(2, i, 2)
                glu_gate(3, i, 2)

            def empty(r, what, gi, i, st, func, scale):
                act.wait_ge(s_mm, lin(gi + 1, 2 * st, i))
                fn(qkvg[:, r, what, :].rearrange("p (a b) -> p a b", a=2), psP[0][:, :, 0:HT], func,
                   scale=scale).then_inc(s_ea, 1)

            def exps(t, h, i):
                act.wait_ge(s_mx, lin(4 * h + t + 1, 8, i))
                for m in range(2):
                    out = prob[:, m, PO[t]:PO[t] + PW[t]]
                    if t < 3:
                        src = psS[m][:, t % 2, 0:PW[t]]
                    else:
                        src = psS[m][:, :, 0:HT]
                        out = out.rearrange("p (a b) -> p a b", a=2)
                    ins = fn(out, src, ACT.Exp, bias=stat[:, 2 * t + m:2 * t + m + 1],
                             accum_out=stat[:, 8 + 2 * t + m:9 + 2 * t + m])
                    if t == 0:
                        ins = fn(pmeta[:, m, :], psS[m][0:NM, 0, PW[0]:PW[0] + NM], ACT.Exp,
                                 bias=stat[0:NM, 16 + m:17 + m], accum_out=stat[0:NM, 18 + m:19 + m])
                ins.then_inc(s_ex, 1)

            def copy_values(h, i):
                act.wait_ge(s_at, lin(5 * h + 1, 10, i))
                fn(vtok[:, 0:TT, :], psP[1][:, 0, :].rearrange("p (j e) -> p j e", j=TT), ACT.Copy)
                fn(vtok[0:NM, TT, :], psP[1][0:NM, 1, 0:128], ACT.Copy).then_inc(s_ac, 1)

            def copy_probs(t, h, i):
                act.wait_ge(s_at, lin(5 * h + t + 2, 10, i))
                fn(aT[:, 0:t + 1, 128 * t:128 * (t + 1)], psP[1][:, 0, 0:128 * (t + 1)].rearrange("p (j q) -> p j q", j=t + 1), ACT.Copy)
                ins = fn(aTm[:, 128 * t:128 * (t + 1)], psP[1][0:NM, 1, 0:128], ACT.Copy)
                if t == 0:
                    ins = fn(aTm[:, S:S + NM], psP[1][0:NM, 1, 128:128 + NM], ACT.Copy)
                ins.then_inc(s_ac, 1)

            def square_head(h, i):
                act.wait_ge(s_at_o, lin(h + 1, 2, i))
                fn(osq[:, NM:T], psP[1][:, 0, :], ACT.Square)
                fn(osq[:, 0:NM], psP[1][:, 1, 0:NM], ACT.Square).then_inc(s_os, 1)
                act.wait_ge(s_ss, lin(h + 1, 2, i))
                act.wait_ge(s_cv, lin(h + 1, 2, i))
                if i is None:
                    dst = u[:, h, 0:T].rearrange("p (a b) -> p a b", a=2)
                else:
                    dst = u[:, ds(i * 2 + h, 1), 0:T].rearrange("p o (a b) -> p (o a) b", a=2)
                fn(dst, psS[0][:, :, 0:HT], ACT.Copy).then_inc(s_sc, 1)

            def fetch(g, i, last=False):
                at_ = (lambda o: ds(i * 2 + o, 1)) if i is not None else (lambda o: slice(o, o + 1))
                if g > 0 or i is not None:
                    act.wait_ge(s_cv, lin(g, 2, i))
                    fn(conv[:, at_(g - 1), :], cacc[:], ACT.Copy).then_inc(s_cst, 1)
                if last:
                    return
                fn(cin[:], u[:, at_(g), :], ACT.Copy)
                taps = cdw[:].rearrange("p (k g) -> p g k", g=NH)
                fn(cwt[:, 0:CK], taps[:, at_(g), :], ACT.Copy)
                b = vec[:, V_CB:V_CB + 8]
                fn(cwt[:, CK:CK + 1], b[:, at_(g)], ACT.Copy).then_inc(s_cf, 1)

            def step(h, r, i, project_it=True, attend=True):
                n, p, a = N_HEAD + 2 * h, 1 - r, h - 1
                if project_it:
                    hi(n + 1, i, 4)
                if attend:
                    exps(0, a, i)
                    exps(1, a, i)
                if project_it:
                    empty(r, 0, 2 * n, i, 4, ACT.Copy, 0.125)
                if attend:
                    copy_values(a, i)
                    copy_probs(0, a, i)
                    exps(2, a, i)
                if project_it:
                    empty(r, 1, 2 * n + 1, i, 4, ACT.Copy, 1.0)
                    hi(n + 2, i, 4)
                if attend:
                    copy_probs(1, a, i)
                    exps(3, a, i)
                if project_it:
                    empty(r, 2, 2 * n + 2, i, 4, ACT.Copy, 1.0)
                if attend:
                    copy_probs(2, a, i)
                if project_it:
                    empty(r, 3, 2 * n + 3, i, 4, ACT.Tanh, 0.5)
                if attend:
                    copy_probs(3, a, i)
                    square_head(a, i)
                if project_it:
                    fetch(h + 1, i, last=(h == NH - 1 and i is None))

            act.wait_ge(s_ed, CREDIT + NH)
            fetch(0, None)
            step(0, 0, None, attend=False)
            with act.Fori(0, 3) as i:
                step(1, 1, i)
                step(2, 0, i)
            step(7, 1, None)
            step(8, 0, None, project_it=False)

            def sig_gate(n):
                for half in range(2):
                    gi = 2 * n + half
                    act.wait_ge(s_mm, gi + 1)
                    fn(sgc[:, 2 * (n - N_GC) + half, :].rearrange("p (a b) -> p a b", a=2), psP[gi % 2][:, :, 0:H3],
                       ACT.Sigmoid).then_inc(s_ea, 1)
            act.wait_ge(s_sc, 1 + NH)
            fn(u[:, :, 0:T], u[:, :, 0:T], ACT.Sqrt, bias=eps6[:], scale=1.0 / 128).then_inc(s_hr, 1)
            hi(N_GC + 1)
            for k in range(KT):
                act.wait_ge(s_lc, k + 1)
                square(8 + k, conv[:, k, :], T3)
            sig_gate(N_GC)
            hi(N_GC + 2)
            sig_gate(N_GC + 1)
            hi(N_GC + 3)
            root(1, psS[1], H3, eps5)
            sig_gate(N_GC + 2)
            hi(N_GC + 4)
            for k in range(KT):
                act.wait_ge(s_ln, k + 1)
                fn(conv[:, k, :], conv[:, k, :], ACT.Silu, scale=vec[:, V_LNW + k:V_LNW + k + 1],
                   bias=vec[:, V_LNB + k:V_LNB + k + 1]).then_inc(s_lu, 1)
            sig_gate(N_GC + 3)
            for k in range(KT):
                act.wait_ge(s_lu, k + 1)
                fn(xh[:, k, C3:T], conv[:, k, :], ACT.Copy).then_inc(s_nh, 1)
            for n in range(N_CO, N_CO + 4):
                hi(n + 1)
                for half in range(2):
                    g = 2 * (n - N_CO) + half
                    act.wait_ge(s_m, g + 1)
                    fn(mh[:, g, :], nf[:, g % 2, 0:T3], ACT.Copy).then_inc(s_mhi, 1)
            for n in range(N_WO, N_WO + 4):
                hi(n + 1)
                for half in range(2):
                    k = 2 * (n - N_WO) + half
                    act.wait_ge(s_ed, evacuated(2 * n + half)[1])
                    square(16 + k, hT[:, k, C3:T], T3)
            root(2, psP[0], H3, eps6)
            normed_hi(1, C3, T3)

            def ffn(n0, slot0, func, start, width, use):
                with act.Fori(0, FG // 2) as i:
                    for j in range(2):
                        n = n0 + j
                        hi(n + 1, i, 2)
                        for x in range(2):
                            gi = 2 * n + x
                            act.wait_ge(s_mm, lin(gi + 1, 4, i))
                            if x == 0:
                                act.wait_ge(s_cva, lin(CREDIT * 2 + 2 * FG * use + 2 * (j - 1), 4, i))
                            src = ALLP[2 * j + x]
                            if width == T3:
                                fn(upr[:, j, x, :].rearrange("p (a b) -> p a b", a=2), src[:, :, 0:H3], ACT.Copy).then_inc(s_ea, 1)
                            else:
                                fn(upr[:, j, x, start:start + width], src[:, 0, :], ACT.Copy).then_inc(s_ea, 1)
                        act.wait_ge(s_cva, lin(CREDIT * 2 + 2 * FG * use + 2 * j + 1, 4, i))
                        fn(acc[:, 0, :], acc[:, 0, :], func).then_inc(s_sil, 1)
                        act.wait_ge(s_pr, lin(FG * use + j + 1, 2, i))
                        fn(acth[:, ds(i * 2 + j, 1), :], prod[:, j, :], ACT.Copy).then_inc(s_ph, 1)

            ffn(N_UP, 0, ACT.Silu, 0, T3, 0)
            def down_group(g, i):
                hi(N_DN + 2 * g + 1, i, 4)
                hi(N_DN + 2 * g + 2, i, 4)
                act.wait_ge(s_ed, lin(evacuated(2 * N_DN + 4 * g + 3)[1], 2, i))
                k = (lambda t: t[:, ds(i * 2 + g, 1), NM:T])
                square(24 + 2 * g, k(hT), S, i, 4)
                square(25 + 2 * g, k(hT), S, i, 4, scale=vec[:, V_FIN:V_FIN + 8][:, ds(i * 2 + g, 1)])

            with act.Fori(0, 4) as i:
                for g in range(2):
                    down_group(g, i)

            HS = S // 2
            ready2 = 16 * (12 + 1)
            hi(N_IN2 + 1)
            act.wait_ge(s_n2, 1)
            fn(rstd[:, 0:S], rstd[:, 0:S], ACT.Sqrt).then_inc(s_rt, 1)
            fn(sacc[:, 0, 0:S].rearrange("p (a b) -> p a b", a=2), psS[0][:, :, 0:HS], ACT.Sqrt, bias=eps6[:],
               scale=1.0 / D).then_inc(s_rt, 1)
            normed_hi(2, NM, S)
            act.wait_ge(s_x2, KT)

            def full(gi):
                act.wait_ge(s_mm, gi + 1)
                return psP[0][:, gi % 2, :]

            def to(dst, gi, func=ACT.Copy, **kw):
                fn(dst, full(gi), func, **kw).then_inc(s_ea, 1)

            def index(t):
                n_ = 128 * (t + 1)
                for h in range(4):
                    act.wait_ge(s_ix, 4 * t + h + 1)
                    if 4 * t + h >= 2:
                        act.wait_ge(s_ixa, 4 * t + h - 1)
                    fn(rl[:, h % 2, 0:n_], psS[h // 2][:, h % 2, 0:n_], ACT.Relu, scale=0.5 * 0.125).then_inc(s_rl, 1)

            def lru_gates(g):
                act.wait_ge(s_rg, g + 1)
                fn(lx[:, g, 3:3 + S], psP[1][:, 0, :], ACT.Sigmoid, bias=vec[:, V_LBA + g:V_LBA + g + 1])
                fn(li[:, g, :], psP[1][:, 1, :], ACT.Sigmoid, bias=vec[:, V_LBX + g:V_LBX + g + 1]).then_inc(s_ri, 1)

            def columns(j):
                act.wait_ge(s_gt, j + 1)
                fn(gcol[:, j, :, :].rearrange("p a b -> p (a b)"), psP[1][:, 0, 16 * j:16 * j + 16], ACT.Copy).then_inc(s_gc, 1)

            def attend(h):
                for t in range(TT):
                    u_, n_ = TT * h + t, 128 * (t + 1)
                    act.wait_ge(s_pm, u_ + 1)
                    fn(pr[:, u_ % 2, 0:n_], pr[:, u_ % 2, 0:n_], ACT.Exp, bias=mx2[:, 0, u_ % 2:u_ % 2 + 1],
                       accum_out=mx2[:, 1, u_ % 2:u_ % 2 + 1]).then_inc(s_pe, 1)
                    act.wait_ge(s_pt, u_ + 1)
                    fn(PT[:, 0:t + 1, 128 * t:128 * (t + 1)], psP[1][:, 0, 0:n_].rearrange("p (j q) -> p j q", q=128),
                       ACT.Copy).then_inc(s_pc, 1)
                act.wait_ge(s_po, h + 1)
                if h % 2:
                    fn(ch[:, 6 + h // 2, :], psP[1][:, 1, :], ACT.Copy).then_inc(s_hc, 1)

            def mlstm(h):
                act.wait_ge(s_md, h + 1)
                for j in range(TT):
                    G = gcol[:, 1, j, h:h + 1]
                    ins = fn(PT[:, j, 128 * j:128 * (j + 1)], md[:, j, :], ACT.Exp, scale=-1.0, bias=G)
                    if j < TT - 1:
                        ins = fn(PT[:, j, 128 * (j + 1):S], psS[0][:, 0, 128 * (j + 1):S], ACT.Exp, scale=-1.0, bias=G)
                ins.then_inc(s_mw, 1)

            n = N_IN2
            to(iq[:, 0, :], 2 * n)
            to(iq[:, 1, :], 2 * n + 1)
            hi(n + 2)
            to(ik[:], 2 * n + 2)
            g_ = full(2 * n + 3)
            fn(rows[:, 4, :], g_[64:68, :], ACT.Copy).then_inc(s_ga, 1)
            fn(rows[:, 1, :], g_[32:36, :], ACT.Copy).then_inc(s_ga, 1)
            fn(rows[:, 0, :], g_[0:4, :], ACT.Identity, bias=bif[:, 1:2]).then_inc(s_ea, 1)
            columns(0)
            index(0)
            index(1)
            act.wait_ge(s_az, 1)
            fn(rows[:, 2, :], rows[:, 2, :], ACT.Exp, scale=-1.0).then_inc(s_ez, 1)
            act.wait_ge(s_lb, 1)
            fn(lcol[:, 1, :], lcol[:, 0, :], ACT.Exp, scale=-1.0).then_inc(s_ez, 1)
            for g in range(LG):
                hi(n + 3 + g)
                to(lx[:, g, 3:], 2 * n + 4 + 2 * g)
                to(lg[:, g, :], 2 * n + 5 + 2 * g, ACT.Gelu_apprx_tanh)
                if g < 2:
                    index(2 + g)
            lru_gates(0)
            hi(n + 6)
            act.wait_ge(s_ixa, 16)
            to(aqk[:, 0, :], 2 * n + 10)
            to(aqk[:, 1, :], 2 * n + 11)
            lru_gates(1)
            lru_gates(2)
            act.wait_ge(s_lb, 2)
            for g in range(LG):
                act.wait_ge(s_ri, g + 1)
                own(fn(lt[:, g, :], lx[:, g, 3:], ACT.Tanh, scale=lcol[:, 2, g:g + 1]))
                fn(lx[:, g, 3:], lx[:, g, 3:], ACT.Exp, scale=lcol[:, 2, g:g + 1]).then_inc(s_la, 1)
            act.wait_ge(s_mrow, 1)
            fn(rows[:, 3, :], rows[:, 3, :], ACT.Exp, scale=-1.0).then_inc(s_fl, 1)
            columns(1)
            columns(2)
            hi(n + 7)
            to(aqk[:, 2, :], 2 * n + 12)
            to(aqk[:, 3, :], 2 * n + 13)
            act.wait_ge(s_lv, 1)
            fn(lt[:], lt[:], ACT.Sqrt).then_inc(s_lq, 1)
            hi(n + 8)
            for half in range(2):
                to(av[:, 2 * half:2 * half + 2, :].rearrange("p a c -> p (a c)"), 2 * n + 14 + half)
            for g in range(LG):
                act.wait_ge(s_hb, g + 1)
                fn(ch[:, 3 + g, :], li[:, g, :], ACT.Copy).then_inc(s_hbh, 1)
            act.wait_ge(s_hbl, LG)
            act.wait_ge(s_pz2, 1)
            def by_token(c):
                hi(n + 9 + c)
                for half in range(2):
                    gi = 2 * (n + 8 + c) + half
                    f_ = full(gi).rearrange("p (a c) -> p a c", a=2)
                    tt = slice(2 * half, 2 * half + 2)
                    ins = None
                    c0 = 256 * c
                    for h in range(ML_H):
                        a0, a1 = max(c0, ML_D * h), min(c0 + 256, ML_D * (h + 1), ML_W)
                        if a0 < a1:
                            o = a0 - ML_D * h + (ML_D + 1) * h
                            ins = fn(va[:, tt, o:o + a1 - a0], f_[:, :, a0 - c0:a1 - c0], ACT.Copy)
                    a0 = max(c0, ML_W)
                    if a0 < c0 + 256:
                        ins = fn(mo[:, tt, a0 - ML_W:c0 + 256 - ML_W], f_[:, :, a0 - c0:256], ACT.Sigmoid)
                    ins.then_inc(s_ea, 1)

            def qk(h):
                gi = 2 * (n + 11 + h)
                fn(mqk[:, h % 2, 0, :], full(gi)[0:ML_D, :], ACT.Copy).then_inc(s_ea, 1)
                fn(mqk[:, h % 2, 1, :], full(gi + 1)[0:ML_D, :], ACT.Copy, scale=ML_D ** -0.5).then_inc(s_ea, 1)

            by_token(0)
            by_token(1)
            by_token(2)
            attend(0)
            hi(n + 12)
            qk(0)
            attend(1)
            hi(n + 13)
            qk(1)
            attend(2)
            attend(3)
            hi(n + 14)
            act.wait_ge(s_po, 4)
            mlstm(0)
            hi(n + 15)
            act.wait_ge(s_mo, 1)
            qk(2)
            mlstm(1)
            act.wait_ge(s_mo, 2)
            qk(3)
            mlstm(2)
            act.wait_ge(s_mo, 3)
            mlstm(3)
            act.wait_ge(s_mn, 4)
            act.wait_ge(s_mo, 4)
            fn(PT[:, 0:3, :].rearrange("p a b -> p (a b)"), hA[:].rearrange("p t c -> p (t c)"), ACT.Square).then_inc(s_hs, 1)
            act.wait_ge(s_h2, 1)
            fn(mx2[:, 2:4, :].rearrange("p a b -> p (a b)"), mx2[:, 2:4, :].rearrange("p a b -> p (a b)"), ACT.Sqrt,
               scale=1.0 / ML_D, bias=eps6[:]).then_inc(s_hrt, 1)
            for g in range(LG):
                act.wait_ge(s_ht, g + 1)
                ps = (psS[0][:, 0, :], psS[0][:, 1, :], psS[1][:, 0, :])[g]
                fn(ch[:, g, :], ps, ACT.Copy).then_inc(s_hh, 1)
            act.wait_ge(s_hl, 3)
            for c in range(4):
                hi(N_WO2 + c + 1)
                for half in range(2):
                    gi = 2 * (N_WO2 + c) + half
                    act.wait_ge(s_mm, gi + 1)
                    square(40 + 2 * c + half, psP[half][:, 0, :], S)
                    fn(mT[:, 2 * c + half, :], psP[half][:, 0, :], ACT.Copy).then_inc(s_ea, 1)
            root(5, psS[0], HS, eps6)
            for k in range(KT):
                act.wait_ge(s_y, k + 1)
                square(48 + k, hT[:, k, NM:T], S)
            root(6, psS[1], HS, eps6)
            normed_hi(3, NM, S)
            act.wait_ge(s_uz, 1)
            ffn(N_UP2, 0, ACT.Gelu_apprx_tanh, 4, S, 1)

            def down2(i, turn_last=False):
                for g in range(2):
                    hi(N_DN2 + 2 * g + 1, i, 4)
                    if not (turn_last and g == 1):
                        hi(N_DN2 + 2 * g + 2, i, 4)
                    act.wait_ge(s_mm, lin(2 * N_DN2 + 4 * g + 4, 8, i))
                    square(56 + g, psP[g][:, 0, :], S, i, 2)
                    fn(mT2[:, ds(i * 2 + g, 1), :] , psP[g][:, 0, :], ACT.Copy).then_inc(s_ea, 1)

            with act.Fori(0, 3) as i:
                down2(i)
            for g in range(2):
                hi(N_DN2 + 12 + 2 * g + 1)
                if g == 0:
                    hi(N_DN2 + 14)
                act.wait_ge(s_mm, 2 * N_DN2 + 24 + 4 * g + 4)
                square(62 + g, psP[g][:, 0, :], S)
                fn(mT2[:, 6 + g, :], psP[g][:, 0, :], ACT.Copy).then_inc(s_ea, 1)
            root(7, psS[0], HS, eps6)
            for half in range(2):
                act.wait_ge(s_ot, 4 * half + 4)
                for t in range(2 if half else TT):
                    fn(xo[:, t, 512 * half:512 * (half + 1)], ALLP[t][:, half, :], ACT.Copy).then_inc(s_oc, 1)

        @block.vector
        def _(dve):
            V = nc.vector
            own = Own(dve, s_v)

            def lo(n, i=None, st=0):
                dve.wait_ge(s_hi, lin(n + 1, st, i))
                V.tensor_tensor(wl[:, n % 2], raw[:, n % 2], wh[:, n % 2].bitcast(f32), ALU.subtract).then_inc(s_lo, 1)

            def inverse(use, n):
                dve.wait_ge(s_rt, use + 1)
                own(V.reciprocal(rstd[:, 0:n], rstd[:, 0:n]))

            def normed_lo(k, use, c0, n):
                dve.wait_ge(s_nh, 8 * use + k + 1)
                V.tensor_tensor(xl[:, k, c0:c0 + n], nf[:, k % 2, 0:n], xh[:, k, c0:c0 + n].bitcast(f32),
                                ALU.subtract).then_inc(s_nl, 1)

            def clear_sums():
                own(V.memset(sacc[:], 0.0))

            def add_square(m, n, which=0, i=None, st=0):
                dve.wait_ge(s_sq, lin(m + 1, st, i))
                if m:
                    dve.wait_ge(s_sa, lin(m, st, i))
                V.tensor_tensor(sacc[:, which, 0:n], sacc[:, which, 0:n], sq[:, m % 2, 0:n], ALU.add).then_inc(s_sa, 1)

            def norm(sum_use, use, src, s0, c0, n, weight):
                inverse(sum_use, n)
                for k in range(KT):
                    if 8 * use + k >= 2:
                        dve.wait_ge(s_nl, 8 * use + k - 1)
                    V.scalar_tensor_tensor(nf[:, k % 2, 0:n], src[:, k, s0:s0 + n], vec[:, weight + k:weight + k + 1],
                                           rstd[:, 0:n], ALU.mult, ALU.mult).then_inc(s_nf, 1)
                    if k:
                        normed_lo(k - 1, use, c0, n)
                normed_lo(KT - 1, use, c0, n)

            for k in range(KT):
                dve.wait_ge(s_xt, k + 1)
                V.tensor_copy(hT[:, k, NM:T], ALLP[1 + k % 3][:, 0, :])
                V.tensor_copy(hT[:, k, 0:NM], ALLP[1 + k % 3][:, 1, 0:NM]).then_inc(s_hm, 1)
            for c, (sm, k) in enumerate(((s_ed, CREDIT), (s_ea, CREDIT), (s_oy, 1), (s_ex, 4), (s_sc, 1), (s_os, 1),
                                         (s_cva, 2 * CREDIT), (s_pl, CREDIT))):
                V.memset(cred[:, c:c + 1], 0.0).then_inc(sm, k)
            lo(0)
            dve.wait_ge(s_in, N_IN)
            lv = lamv[:].rearrange("p (a b) c -> p a b c", b=2)
            own(V.tensor_tensor(lamp[:], lv[:, :, 0, :], lv[:, :, 1, :], ALU.mult))
            V.tensor_reduce(lams[:, 0:2], lamp[:], AX, ALU.add).then_inc(s_lamo, 1)
            dve.wait_ge(s_ct, 1)
            V.tensor_copy(fdw[:].rearrange("p b v g -> p (b v g)"), psS[0][:, 1, 0:16 * FG]).then_inc(s_cc, 1)
            dve.wait_ge(s_cc, 2)
            norm(0, 0, hT, 0, 0, T, V_MIX)
            dve.wait_ge(s_lame, 1)
            own(V.tensor_tensor(lams[:, 4:5], lams[:, 3:4], lams[:, 2:3], ALU.subtract))
            own(V.tensor_scalar(nlam[:], lams[:, 4:5], -LAMBDA_INIT, None, ALU.add))
            own(V.tensor_scalar(vec[:, V_SUB:V_SUB + 1], vec[:, V_SUB:V_SUB + 1], 0.5 * (1.0 - LAMBDA_INIT), None, ALU.mult))
            own(V.tensor_tensor(vec[:, V_FP:V_FP + 8], vec[:, V_FIN:V_FIN + 8], vec[:, V_PRE:V_PRE + 8], ALU.mult))
            V.memset(u[:, :, 0:PAD], 0.0)
            V.memset(mki[:], 0.0)
            own(V.memset(mkk[:], 0.0))
            for m in range(2):
                V.memset(mki[64 * m:64 * m + 1, 0:64], 1.0)
                V.memset(mkk[64 * m:64 * m + 1, :], -BIG)

            def glu(n, i, st):
                lo(n + 1, i, st)
                dve.wait_ge(s_ea, lin(CREDIT + n + 1, st, i))
                g = slice(n, n + 1) if i is None else ds(i * 2 + n, 1)
                V.tensor_tensor(u[:, g, PAD:].rearrange("p o (a b) -> p (o a) b", a=2), ALLP[(2 * n) % 4][:, :, 0:HT],
                                sgl[:, n % 2, :].rearrange("p (a b) -> p a b", a=2), ALU.mult).then_inc(s_ed, 1)

            glu(0, None, 0)
            glu(1, None, 0)
            with dve.Fori(0, 3) as i:
                glu(2, i, 2)
                glu(3, i, 2)

            def maxima(t, h, i):
                dve.wait_ge(s_qk, lin(4 * h + t + 1, 8, i))
                for m in range(2):
                    src = psS[m][:, t % 2, 0:PW[t]] if t < 3 else psS[m][:, :, 0:HT]
                    ins = V.tensor_reduce(stat[:, 2 * t + m:2 * t + m + 1], src, AX if t < 3 else mybir.AxisListType.XY, ALU.max, negate=True)
                    if t == 0:
                        ins = V.tensor_reduce(stat[0:NM, 16 + m:17 + m], psS[m][0:NM, 0, PW[0]:PW[0] + NM], AX, ALU.max, negate=True)
                ins.then_inc(s_mx, 1)

            def combine(t, h, i):
                dve.wait_ge(s_ex, lin(4 + 4 * h + t + 1, 8, i))
                todo = [(slice(0, 128), prob[:, 0, PO[t]:PO[t] + PW[t]], prob[:, 1, PO[t]:PO[t] + PW[t]], 8 + 2 * t)]
                if t == 0:
                    todo.insert(0, (slice(0, NM), pmeta[:, 0, :], pmeta[:, 1, :], 18))
                for P, p0, p1, c in todo:
                    own(V.reciprocal(stat[P, c:c + 2], stat[P, c:c + 2]))
                    V.tensor_scalar(p0, p0, stat[P, c:c + 1], None, ALU.mult)
                    own(V.tensor_scalar(stat[P, c + 1:c + 2], stat[P, c + 1:c + 2], nlam[P, :], None, ALU.mult))
                    ins = V.scalar_tensor_tensor(p0, p1, stat[P, c + 1:c + 2], p0, ALU.mult, ALU.add)
                ins.then_inc(s_cb, 1)

            def taps(lo_, hi_, h, i):
                for k in range(lo_, hi_):
                    w = cwt[:, k:k + 1]
                    src = cin[:, C3 + k:C3 + k + T3]
                    if k == 0:
                        dve.wait_ge(s_cf, lin(h + 1, 2, i))
                        own(V.tensor_scalar(cacc[:], src, w, cwt[:, CK:CK + 1], ALU.mult, ALU.add))
                    else:
                        own(V.scalar_tensor_tensor(cacc[:], src, w, cacc[:], ALU.mult, ALU.add))
                if hi_ == CKD:
                    dve.wait_ge(s_cp, lin(h + 1, 2, i))
                    V.tensor_tensor(cacc[:], cacc[:], caccp[:], ALU.add).then_inc(s_cv, 1)

            def gated(h, r, i):
                dve.wait_ge(s_os, lin(1 + h + 1, 2, i))
                g = slice(h, h + 1) if i is None else ds(i * 2 + h, 1)
                V.scalar_tensor_tensor(yT[:, g, NM:T], qkvg[:, r, 3, NM:T], 1.0, psP[1][:, 0, :], ALU.add, ALU.mult)
                V.scalar_tensor_tensor(yT[:, g, 0:NM], qkvg[:, r, 3, 0:NM], 1.0, psP[1][:, 1, 0:NM], ALU.add,
                                       ALU.mult).then_inc(s_oy, 1)

            def step(h, r, i, project_it=True, attend=True):
                n, p, a = N_HEAD + 2 * h, 1 - r, h - 1
                if attend:
                    maxima(0, a, i)
                    maxima(1, a, i)
                if project_it:
                    lo(n + 1, i, 4)
                if attend:
                    combine(0, a, i)
                    combine(1, a, i)
                if project_it:
                    taps(0, 5, h, i)
                if attend:
                    maxima(2, a, i)
                    combine(2, a, i)
                if project_it:
                    taps(5, 10, h, i)
                    lo(n + 2, i, 4)
                if attend:
                    maxima(3, a, i)
                    combine(3, a, i)
                if project_it:
                    taps(10, CKD, h, i)
                if attend:
                    gated(a, p, i)

            step(0, 0, None, attend=False)
            with dve.Fori(0, 3) as i:
                own.enter(i, OWN_HEADS)
                step(1, 1, i)
                step(2, 0, i)
                own.leave(3)
            step(7, 1, None)
            step(8, 0, None, project_it=False)

            lo(N_GC + 1)
            clear_sums()
            dve.wait_ge(s_lm, 1)
            for g in range(NH):
                V.scalar_tensor_tensor(span(conv, g, 0, H3), psS[0][:, :, 0:H3], -1.0 / D, span(conv, g, 0, H3),
                                       ALU.mult, ALU.add).then_inc(s_lc, 1)
                if g:
                    add_square(8 + g - 1, T3)
            add_square(8 + KT - 1, T3)
            lo(N_GC + 2)
            dve.wait_ge(s_hr, 1)
            own(V.reciprocal(u[:, :, 0:T], u[:, :, 0:T]))
            lo(N_GC + 3)
            inverse(1, T3)
            for k in range(KT):
                V.tensor_tensor(conv[:, k, :], conv[:, k, :], rstd[:, 0:T3], ALU.mult).then_inc(s_ln, 1)
            lo(N_GC + 4)
            own(V.scalar_tensor_tensor(yT[:], yT[:], vec[:, V_SUB:V_SUB + 1], u[:, :, 0:T], ALU.mult, ALU.mult))
            for k in range(KT):
                dve.wait_ge(s_nh, 8 + k + 1)
                V.tensor_tensor(xl[:, k, C3:T], conv[:, k, :], xh[:, k, C3:T].bitcast(f32), ALU.subtract).then_inc(s_nl, 1)
            def mixed_lo(g):
                dve.wait_ge(s_mhi, g + 1)
                V.tensor_tensor(ml[:, g, :], nf[:, g % 2, 0:T3], mh[:, g, :].bitcast(f32), ALU.subtract).then_inc(s_ml, 1)

            for n in range(N_CO, N_CO + 4):
                lo(n + 1)
                for half in range(2):
                    gi = 2 * n + half
                    g = gi - 2 * N_CO
                    dve.wait_ge(s_mm, gi + 1)
                    t = nf[:, g % 2, 0:T3]
                    if g >= 2:
                        dve.wait_ge(s_ml, g - 1)
                    ins = V.tensor_tensor(t.rearrange("p (a b) -> p a b", a=2), ALLP[gi % 4][:, :, 0:H3],
                                          span(sgc, g, 0, H3), ALU.mult)
                    ins.then_inc(s_ed, 1)
                    dve.wait_ge(s_ed, evacuated(gi)[1])
                    V.tensor_tensor(t, t, yT[:, g, C3:T], ALU.add).then_inc(s_m, 1)
                    mixed_lo(g)
            clear_sums()
            for n in range(N_WO, N_WO + 4):
                lo(n + 1)
                for half in range(2):
                    gi = 2 * n + half
                    k = gi - 2 * N_WO
                    dve.wait_ge(s_mm, gi + 1)
                    V.tensor_tensor(span(hT, k, C3, H3), ALLP[gi % 4][:, :, 0:H3], span(hT, k, C3, H3), ALU.add).then_inc(s_ed, 1)
                    if k:
                        add_square(16 + k - 1, T3)
            add_square(16 + KT - 1, T3)
            norm(2, 2, hT, C3, C3, T3, V_FFN)

            def ffn(n0, b, use, per):
                f = FG * use
                with dve.Fori(0, FG // 2) as i:
                    own.enter(i, per)
                    for j in range(2):
                        lo(n0 + j + 1, i, 2)
                        for x in range(2):
                            e, c = evacuated(2 * (n0 + j) + x)
                            dve.wait_ge(s_ea, lin(c, 4, i))
                            w = [fdw[:, b, v, ds(i * 2 + (j + FG * x), 1)] for v in range(4)]
                            own(V.tensor_scalar(acc[:, x, :], upr[:, j, x, 4:4 + S], w[2], w[3], ALU.mult, ALU.add))
                            own(V.scalar_tensor_tensor(acc[:, x, :], upr[:, j, x, 3:3 + S], w[1], acc[:, x, :], ALU.mult, ALU.add))
                            V.scalar_tensor_tensor(acc[:, x, :], upr[:, j, x, 2:2 + S], w[0], acc[:, x, :], ALU.mult,
                                                   ALU.add).then_inc(s_cva, 1)
                        dve.wait_ge(s_cva, lin(2 * CREDIT + 2 * f + 2 * j + 2, 4, i))
                        dve.wait_ge(s_sil, lin(f + j + 1, 2, i))
                        dve.wait_ge(s_pl, lin(CREDIT + f + j - 1, 2, i))
                        V.tensor_tensor(prod[:, j, :], acc[:, 0, :], acc[:, 1, :], ALU.mult).then_inc(s_pr, 1)
                        dve.wait_ge(s_ph, lin(f + j + 1, 2, i))
                        V.tensor_tensor(actl[:, ds(i * 2 + j, 1), :], prod[:, j, :], acth[:, ds(i * 2 + j, 1), :].bitcast(f32),
                                        ALU.subtract).then_inc(s_pl, 1)
                    own.leave(FG // 2)

            ffn(N_UP, 0, 0, 8)
            dve.wait_ge(s_pl, CREDIT + FG)
            clear_sums()
            with dve.Fori(0, 4) as i:
                for g in range(2):
                    lo(N_DN + 2 * g + 1, i, 4)
                    lo(N_DN + 2 * g + 2, i, 4)
                    gi = 2 * N_DN + 4 * g + 3
                    dve.wait_ge(s_mm, lin(gi + 1, 8, i))
                    h_ = hT[:, ds(i * 2 + g, 1), NM:T]
                    V.tensor_tensor(h_, psP[g][:, 0, :], h_, ALU.add).then_inc(s_ed, 1)
                    for w in range(2):
                        add_square(24 + 2 * g + w, S, w, i, 4)

            lo(N_IN2 + 1)
            dve.wait_ge(s_sqf, 4)
            halves = (lambda t: t.rearrange("p (a b) -> p a b", a=2))
            own(V.tensor_scalar(halves(rstd[:, 0:S]), psS[0][:, :, 0:S // 2], 1e-6 / D, 1e-12, ALU.mult, ALU.add))
            V.scalar_tensor_tensor(halves(rstd[:, 0:S]), psS[1][:, :, 0:S // 2], 1.0 / D, halves(rstd[:, 0:S]), ALU.mult,
                                   ALU.add).then_inc(s_n2, 1)
            norm(3, 3, hT, NM, NM, S, V_FP)
            dve.wait_ge(s_rt, 5)
            own(V.reciprocal(sacc[:, 0, 0:S], sacc[:, 0, 0:S]))
            for k in range(KT):
                V.scalar_tensor_tensor(hT[:, k, NM:T], hT[:, k, NM:T], vec[:, V_FIN + k:V_FIN + k + 1], sacc[:, 0, 0:S],
                                       ALU.mult, ALU.mult).then_inc(s_x2, 1)
            ready2 = 16 * (12 + 1)

            def log1p(e, z, z2, p):
                own(V.tensor_scalar(z, e, 2.0, None, ALU.add))
                own(V.reciprocal(z, z))
                own(V.tensor_tensor(z, z, e, ALU.mult))
                own(V.tensor_tensor(z2, z, z, ALU.mult))
                own(V.tensor_scalar(p, z2, 1.0 / 13, None, ALU.mult))
                for c in (11, 9, 7, 5, 3):
                    own(V.scalar_tensor_tensor(p, p, 1.0 / c, z2, ALU.add, ALU.mult))
                own(V.scalar_tensor_tensor(p, p, 1.0, z, ALU.add, ALU.mult))

            def index(t):
                n_ = 128 * (t + 1)
                for h in range(4):
                    dve.wait_ge(s_rl, 4 * t + h + 1)
                    iw = gcol[:, 0, t, h:h + 1]
                    if h == 0:
                        V.tensor_scalar(sc[:, t, 0:n_], rl[:, 0, 0:n_], iw, None, ALU.mult).then_inc(s_ixa, 1)
                    else:
                        dve.wait_ge(s_ixa, 4 * t + h)
                        V.scalar_tensor_tensor(sc[:, t, 0:n_], rl[:, h % 2, 0:n_], iw, sc[:, t, 0:n_], ALU.mult,
                                               ALU.add).then_inc(s_ixa, 1)

            def select(t, r0=0, r1=TOPK // 8):
                n_ = 128 * (t + 1)
                dve.wait_ge(s_ixa, 4 * (t + 1))
                if t == 0:
                    own(V.memset(sc[:, 0, 0:128], 0.0))
                    own(V.memset(sc[0:64, 0, 64:128], -BIG))
                    return
                if r0 == 0:
                    own(V.memset(sc[0:64, t, n_ - 64:n_], -1.0e37))
                for r in range(r0, r1):
                    own(V.max(m8[:, r % 2, :], sc[:, t, 0:n_]))
                    own(V.match_replace(sc[:, t, 0:n_], m8[:, r % 2, :], sc[:, t, 0:n_], -3.0e38))
                if r1 == TOPK // 8:
                    own(V.tensor_scalar(sc[:, t, 0:n_], sc[:, t, 0:n_], -2.0e38, -BIG, ALU.is_gt, ALU.mult))

            def convolve(g):
                dve.wait_ge(s_ea, evacuated(2 * (n + 2 + g))[1])
                y = xc[:, g, :]
                own(V.tensor_scalar(y, lx[:, g, 0:S], vec[:, V_LCW + g:V_LCW + g + 1], vec[:, V_LCB + g:V_LCB + g + 1],
                                    ALU.mult, ALU.add))
                for k in range(1, 4):
                    w = vec[:, V_LCW + 3 * k + g:V_LCW + 3 * k + g + 1]
                    ins = V.scalar_tensor_tensor(y, lx[:, g, k:k + S], w, y, ALU.mult, ALU.add)
                    if k < 3:
                        own(ins)
                    else:
                        ins.then_inc(s_xc, 1)

            def attend(h):
                for t in range(TT):
                    u_, n_ = TT * h + t, 128 * (t + 1)
                    dve.wait_ge(s_lg, u_ + 1)
                    if u_ >= 2:
                        dve.wait_ge(s_pt, u_ - 1)
                    p = pr[:, u_ % 2, 0:n_]
                    own(V.scalar_tensor_tensor(p, psS[u_ % 4 // 2][:, u_ % 2, 0:n_], 0.125, sc[:, t, 0:n_], ALU.mult, ALU.add))
                    V.tensor_reduce(mx2[:, 0, u_ % 2:u_ % 2 + 1], p, AX, ALU.max, negate=True).then_inc(s_pm, 1)
                    dve.wait_ge(s_pe, u_ + 1)
                    c = mx2[:, 1, u_ % 2:u_ % 2 + 1]
                    own(V.reciprocal(c, c))
                    V.tensor_scalar(p, p, c, None, ALU.mult).then_inc(s_pn, 1)
                if h % 2:
                    dve.wait_ge(s_hc, h // 2 + 1)
                    V.tensor_tensor(cl[:, 6 + h // 2, :], psP[1][:, 1, :], ch[:, 6 + h // 2, :].bitcast(f32),
                                    ALU.subtract).then_inc(s_hcl, 1)

            def mlstm(h):
                dve.wait_ge(s_mb, h + 1)
                V.tensor_tensor(md[:], psS[0][:, 0, :].rearrange("p (t q) -> p t q", t=TT),
                                tri[:].rearrange("p (o q) -> p o q", o=1).to_broadcast([128, TT, 128]), ALU.add).then_inc(s_md, 1)
                dve.wait_ge(s_mw, h + 1)
                for j in range(TT):
                    dve.wait_ge(s_st, 4 * h + j + 1)
                    w = PT[:, j, 128 * j:S]
                    V.tensor_tensor(w, psS[1][:, j % 2, 0:S - 128 * j], w, ALU.mult).then_inc(s_pp, 1)
                dve.wait_ge(s_mo, h + 1)
                o = psP[1][:, 0, 0:97 * TT].rearrange("p (t c) -> p t c", c=97)
                den = st2[:, TT:2 * TT].rearrange("p (t o) -> p t o", o=1)
                neg = st2[:, 0:TT].rearrange("p (t o) -> p t o", o=1)
                own(V.tensor_copy(den, o[:, :, 96:97]))
                own(V.scalar_tensor_tensor(neg, den, -1.0, den, ALU.mult, ALU.max))
                own(V.tensor_tensor(den, neg, gcol[:, 2, :, h:h + 1], ALU.max))
                own(V.reciprocal(den, den))
                V.tensor_tensor(hA[:, :, ML_D * h:ML_D * (h + 1)], o[:, :, 0:96], den.to_broadcast([128, TT, ML_D]),
                                ALU.mult).then_inc(s_mn, 1)

            n = N_IN2
            dve.wait_ge(s_x2, KT)
            V.memset(lx[:, :, 0:3], 0.0)
            lam = vec[:, V_LAM:V_LAM + LG]
            V.scalar_tensor_tensor(lcol[:, 0, :], lam, -1.0, lam, ALU.mult, ALU.max).then_inc(s_lb, 1)
            lo(n + 2)
            dve.wait_ge(s_ea, evacuated(2 * n + 3)[1])
            f_, i_, e_, z_, iw_ = (rows[:, j, :] for j in range(5))
            own(V.tensor_scalar(i_, i_, bif[:, 0:1], None, ALU.add))
            V.scalar_tensor_tensor(e_, f_, -1.0, f_, ALU.mult, ALU.max).then_inc(s_az, 1)
            dve.wait_ge(s_gc, 1)
            index(0)
            index(1)
            dve.wait_ge(s_ez, 1)
            dve.wait_ge(s_gt, 1)
            p_ = iw_
            log1p(e_, z_, e_, p_)
            lo(n + 3)
            own(V.tensor_scalar(f_, f_, 0.0, None, ALU.min))
            own(V.scalar_tensor_tensor(f_, p_, -2.0, f_, ALU.mult, ALU.add))
            own(V.memset(z_, 1.0))
            own(V.tensor_tensor_scan(p_, z_, f_, 0.0, ALU.mult, ALU.add))
            own(V.tensor_tensor(i_, i_, p_, ALU.subtract))
            own(V.tensor_tensor_scan(e_, i_, i_, 0.0, ALU.max, ALU.max))
            V.tensor_tensor(z_, p_, e_, ALU.add).then_inc(s_mrow, 1)
            index(2)
            dve.wait_ge(s_ez, 2)
            log1p(lcol[:, 1, :], lcol[:, 2, :], lcol[:, 3, :], lcol[:, 4, :])
            own(V.tensor_scalar(lcol[:, 5, :], lam, -1.0, 0.0, ALU.mult, ALU.max))
            own(V.scalar_tensor_tensor(lcol[:, 5, :], lcol[:, 4, :], 2.0, lcol[:, 5, :], ALU.mult, ALU.add))
            V.tensor_scalar(lcol[:, 2, :], lcol[:, 5, :], -RG_C, None, ALU.mult).then_inc(s_lb, 1)
            convolve(0)
            lo(n + 4)
            index(3)
            select(0)
            convolve(1)
            select(3, 0, 4)
            lo(n + 5)
            convolve(2)
            select(3, 4, 8)
            lo(n + 6)
            select(3, 8, 10)
            dve.wait_ge(s_la, LG)
            own(V.tensor_tensor(li[:], li[:], xc[:], ALU.mult))
            own(V.tensor_scalar(xc[:], lt[:], -1.0, 1.0, ALU.mult, ALU.add))
            own(V.reciprocal(xc[:], xc[:]))
            V.scalar_tensor_tensor(lt[:], lt[:], -2.0, xc[:], ALU.mult, ALU.mult).then_inc(s_lv, 1)
            select(3, 10, 12)
            lo(n + 7)
            dve.wait_ge(s_lq, 1)
            own(V.tensor_tensor(li[:], li[:], lt[:], ALU.mult))
            for g in range(LG):
                own(V.tensor_tensor_scan(lt[:, g, :], lx[:, g, 3:], li[:, g, :], 0.0, ALU.mult, ALU.add))
                V.tensor_tensor(li[:, g, :], lt[:, g, :], lg[:, g, :], ALU.mult).then_inc(s_hb, 1)
            select(3, 12)
            lo(n + 8)
            select(2, 0, 6)
            for g in range(LG):
                dve.wait_ge(s_hbh, g + 1)
                V.tensor_tensor(cl[:, 3 + g, :], li[:, g, :], ch[:, 3 + g, :].bitcast(f32), ALU.subtract).then_inc(s_hbl, 1)
            dve.wait_ge(s_hbl, LG)
            V.memset(va[:].rearrange("p t (h c) -> p t h c", h=ML_H)[:, :, :, ML_D:], 1.0).then_inc(s_pz2, 1)
            lo(n + 9)
            select(2, 6)
            lo(n + 10)
            select(1)
            dve.wait_ge(s_p2, ready2)
            dve.wait_ge(s_pz, 5)
            lo(n + 11)
            attend(0)
            lo(n + 12)
            attend(1)
            lo(n + 13)
            attend(2)
            attend(3)
            lo(n + 14)
            mlstm(0)
            lo(n + 15)
            mlstm(1)
            mlstm(2)
            mlstm(3)
            dve.wait_ge(s_hs, 1)
            ss = mx2[:, 2:4, :].rearrange("p a b -> p (a b)")
            V.tensor_reduce(ss, PT[:, 0:3, :].rearrange("p a b -> p (a b)").rearrange("p (x d) -> p x d", d=ML_D), AX,
                            ALU.add).then_inc(s_h2, 1)
            dve.wait_ge(s_hrt, 1)
            own(V.reciprocal(ss, ss))
            hx = hA[:].rearrange("p t (h d) -> p (t h) d", d=ML_D)
            own(V.tensor_tensor(hx, hx, ss.rearrange("p (x o) -> p x o", o=1).to_broadcast([128, 16, ML_D]), ALU.mult))
            own(V.tensor_tensor(hA[:], hA[:], mnb[:].rearrange("p (o c) -> p o c", o=1).to_broadcast([128, TT, ML_W]), ALU.mult))
            V.tensor_tensor(hA[:], hA[:], mo[:], ALU.mult).then_inc(s_hg, 1)
            for g in range(LG):
                dve.wait_ge(s_hh, g + 1)
                ps = (psS[0][:, 0, :], psS[0][:, 1, :], psS[1][:, 0, :])[g]
                V.tensor_tensor(cl[:, g, :], ps, ch[:, g, :].bitcast(f32), ALU.subtract).then_inc(s_hl, 1)
            dve.wait_ge(s_hl, LG)
            clear_sums()
            for c in range(4):
                lo(N_WO2 + c + 1)
                for half in range(2):
                    add_square(40 + 2 * c + half, S)

            def add_normed(use, src, weight):
                inverse(use, S)
                for k in range(KT + 1):
                    if k < KT:
                        V.scalar_tensor_tensor(src[:, k, :], src[:, k, :], vec[:, weight + k:weight + k + 1], rstd[:, 0:S],
                                               ALU.mult, ALU.mult).then_inc(s_w, 1)
                    if k:
                        dve.wait_ge(s_w, (8 if use == 7 else 0) + k)
                        V.tensor_tensor(hT[:, k - 1, NM:T], hT[:, k - 1, NM:T], src[:, k - 1, :], ALU.add).then_inc(s_y, 1)

            add_normed(5, mT, V_POST)
            norm(6, 4, hT, NM, NM, S, V_FPRE)
            dve.wait_ge(s_nl, 8 * 5)
            V.memset(upr[:, :, :, 0:4], 0.0).then_inc(s_uz, 1)
            dve.wait_ge(s_uz, 1)
            ffn(N_UP2, 1, 1, 8)
            dve.wait_ge(s_pl, CREDIT + 2 * FG)
            clear_sums()
            with dve.Fori(0, 3) as i:
                for g in range(2):
                    lo(N_DN2 + 2 * g + 1, i, 4)
                    lo(N_DN2 + 2 * g + 2, i, 4)
                    add_square(56 + g, S, 0, i, 2)
            for g in range(2):
                lo(N_DN2 + 12 + 2 * g + 1)
                if g == 0:
                    lo(N_DN2 + 14)
                add_square(62 + g, S)
            add_normed(7, mT2, V_FPOST)
            dve.wait_ge(s_ot, KT)
            for t in range(2, TT):
                V.tensor_copy(xo[:, t, 512:D], ALLP[t][:, 1, :]).then_inc(s_od, 1)


_INS = ["x", "meta_tokens", "norm_mix_w", "w_in", "lambda_q1", "lambda_k1", "lambda_q2", "lambda_k2", "subln_w",
        "conv_dw_w", "conv_dw_b", "conv_ln_w", "conv_ln_b", "w_conv_out", "w_out", "norm_ffn_w", "w_up", "ffn_dw_w",
        "ffn_dw_b", "w_down", "norm_final_w", "norm_mix_pre_2", "norm_mix_post_2", "norm_ffn_pre_2",
        "norm_ffn_post_2", "w_in_2", "b_igate_2", "b_fgate_2", "mlstm_norm_2", "lru_conv_w_2", "lru_conv_b_2",
        "lru_w_a_2", "lru_b_a_2", "lru_w_x_2", "lru_b_x_2", "lru_lambda_2", "w_out_2", "ffn_up_2", "ffn_conv_w_2",
        "ffn_conv_b_2", "ffn_down_2"]


def kernel(**inputs):
    import numpy as _np
    import concourse.bacc as _bacc
    from concourse import mybir as _mybir
    from concourse.bass_utils import run_bass_kernel_spmd as _run

    nc = _bacc.Bacc("TRN2", target_bir_lowering=False, num_devices=1)
    arrays, args = {}, {}
    for name in _INS:
        a = _np.ascontiguousarray(inputs[name])
        arrays[f"in_{name}_dram"] = a
        args[name] = nc.dram_tensor(f"in_{name}_dram", a.shape, _mybir.dt.from_np(a.dtype), kind="ExternalInput").ap()
    out = nc.dram_tensor("out_0_dram", [1, S, D], _mybir.dt.float32, kind="ExternalOutput").ap()
    program(nc, args, out)
    r = _run(nc, [arrays], core_ids=[0])
    return r.results[0]["out_0_dram"]
```
